# Optimizing a Trainium2 kernel written in Bass

```python
import jax, jax.numpy as jnp
from jax import lax
import numpy as np
import math

D_MODEL = 1024
BATCH = 1
SEQ = 256
DEPTH = 2

HEAD_DIM = 64
MOBA_HEADS = 8
MOBA_BLOCK = 256
MOBA_TOPK = 3
SB_HEADS = 8
MLA_HEADS = 8
MLA_Q_LORA = 256
MLA_KV_LORA = 128
MLA_NOPE = 64
MLA_ROPE = 32
MLA_V = 64
MLA_QK = MLA_NOPE + MLA_ROPE
ROPE_THETA = 500000.0
PARTIAL_ROT = HEAD_DIM // 4
Q_BLOCK = 128
D_FF = 2816
N_BRANCH = 3
BRANCH_W = 512
N_SUB = 3
EPS = 1e-6

MOBA_W = MOBA_HEADS * HEAD_DIM
SB_W = SB_HEADS * HEAD_DIM
SPLIT_1 = 3 * MOBA_W
SPLIT_2 = SPLIT_1 + 3 * SB_W
SPLIT_3 = SPLIT_2 + MLA_Q_LORA
SPLIT_4 = SPLIT_3 + MLA_KV_LORA
SPLIT_5 = SPLIT_4 + MLA_ROPE
N_IN = SPLIT_5 + N_BRANCH * D_MODEL


def rms_norm(x, g):
    xf = x.astype(jnp.float32)
    y = xf * lax.rsqrt(jnp.mean(xf * xf, axis=-1, keepdims=True) + EPS)
    return (y * g.astype(jnp.float32)).astype(x.dtype)

def rope_tables(n_rot, seq):
    inv = jnp.power(jnp.float32(ROPE_THETA), -jnp.arange(0, n_rot, 2, dtype=jnp.float32) / n_rot)
    ang = jnp.arange(seq, dtype=jnp.float32)[:, None] * inv[None, :]
    return jnp.cos(ang), jnp.sin(ang)

def apply_rope(x, cos, sin):
    x1, x2 = jnp.split(x, 2, axis=-1)
    cos = cos.astype(x.dtype)
    sin = sin.astype(x.dtype)
    return jnp.concatenate([x1 * cos - x2 * sin, x1 * sin + x2 * cos], axis=-1)

def partial_rope(x, cos, sin):
    return jnp.concatenate([apply_rope(x[..., :PARTIAL_ROT], cos, sin), x[..., PARTIAL_ROT:]], axis=-1)

def to_heads(x, n_heads):
    b, s, _ = x.shape
    return x.reshape(b, s, n_heads, -1).transpose(0, 2, 1, 3)

def from_heads(x):
    b, h, s, d = x.shape
    return x.transpose(0, 2, 1, 3).reshape(b, s, h * d)

def query_blocks(q):
    b, h, s, d = q.shape
    nq = s // Q_BLOCK
    return q.reshape(b, h, nq, Q_BLOCK, d).transpose(2, 0, 1, 3, 4), nq

def merge_query_blocks(o):
    nq, b, h, qb, d = o.shape
    return o.transpose(1, 2, 0, 3, 4).reshape(b, h, nq * qb, d)

def causal_softmax_attention(q, k, v):
    s_len = k.shape[2]
    scale = q.shape[-1] ** -0.5
    qb, nq = query_blocks(q)
    kpos = jnp.arange(s_len)

    def one(args):
        qc, i = args
        sc = jnp.einsum('bhqd,bhkd->bhqk', qc, k).astype(jnp.float32) * scale
        qpos = i * Q_BLOCK + jnp.arange(Q_BLOCK)
        sc = jnp.where(kpos[None, :] <= qpos[:, None], sc, -jnp.inf)
        p = jax.nn.softmax(sc, axis=-1).astype(v.dtype)
        return jnp.einsum('bhqk,bhkd->bhqd', p, v)

    return merge_query_blocks(lax.map(one, (qb, jnp.arange(nq))))

def stick_breaking_attention(q, k, v):
    s_len = k.shape[2]
    scale = q.shape[-1] ** -0.5
    qb, nq = query_blocks(q)
    kpos = jnp.arange(s_len)

    def one(args):
        qc, i = args
        z = jnp.einsum('bhqd,bhkd->bhqk', qc, k).astype(jnp.float32) * scale
        qpos = i * Q_BLOCK + jnp.arange(Q_BLOCK)
        mask = kpos[None, :] < qpos[:, None]
        log_1m = jnp.where(mask, jax.nn.log_sigmoid(-z), 0.0)
        suffix = lax.cumsum(log_1m, axis=3, reverse=True) - log_1m
        w = jnp.where(mask, jnp.exp(jax.nn.log_sigmoid(z) + suffix), 0.0).astype(v.dtype)
        return jnp.einsum('bhqk,bhkd->bhqd', w, v)

    return merge_query_blocks(lax.map(one, (qb, jnp.arange(nq))))

def moba_attention(q, k, v):
    b, h, s_len, d = q.shape
    n = b * h
    scale = d ** -0.5
    s_pad = -(-s_len // MOBA_BLOCK) * MOBA_BLOCK
    nb = s_pad // MOBA_BLOCK
    top = min(MOBA_TOPK, nb)
    qf = q.reshape(n, s_len, d)
    pad = ((0, 0), (0, s_pad - s_len), (0, 0))
    kb = jnp.pad(k.reshape(n, s_len, d), pad).reshape(n, nb, MOBA_BLOCK, d)
    vb = jnp.pad(v.reshape(n, s_len, d), pad).reshape(n, nb, MOBA_BLOCK, d)
    k_mean = jnp.mean(kb.astype(jnp.float32), axis=2)
    gate = jnp.einsum('nsd,nbd->nsb', qf.astype(jnp.float32), k_mean)
    qblk = jnp.arange(s_len) // MOBA_BLOCK
    past = jnp.arange(nb)[None, :] < qblk[:, None]
    gate = jnp.where(past[None], gate, -jnp.inf)
    _, sel = lax.top_k(gate, top)
    valid = sel < qblk[None, :, None]
    nq = s_len // Q_BLOCK
    q_all = qf.reshape(n, nq, Q_BLOCK, d).transpose(1, 0, 2, 3)
    sel_all = sel.reshape(n, nq, Q_BLOCK, top).transpose(1, 0, 2, 3)
    val_all = valid.reshape(n, nq, Q_BLOCK, top).transpose(1, 0, 2, 3)
    rows = jnp.arange(n)[:, None, None]

    def one(args):
        qc, sc, vc, i = args
        ks = kb[rows, sc]
        vs = vb[rows, sc]
        own = (i * Q_BLOCK) // MOBA_BLOCK
        ko = lax.dynamic_index_in_dim(kb, own, axis=1, keepdims=False)
        vo = lax.dynamic_index_in_dim(vb, own, axis=1, keepdims=False)
        s_sel = jnp.einsum('nqd,nqkjd->nqkj', qc, ks).astype(jnp.float32) * scale
        s_sel = jnp.where(vc[..., None], s_sel, -jnp.inf).reshape(n, Q_BLOCK, top * MOBA_BLOCK)
        s_own = jnp.einsum('nqd,njd->nqj', qc, ko).astype(jnp.float32) * scale
        qpos = i * Q_BLOCK + jnp.arange(Q_BLOCK)
        kpos = own * MOBA_BLOCK + jnp.arange(MOBA_BLOCK)
        s_own = jnp.where(kpos[None, :] <= qpos[:, None], s_own, -jnp.inf)
        p = jax.nn.softmax(jnp.concatenate([s_sel, s_own], axis=-1), axis=-1).astype(v.dtype)
        p_sel = p[..., :top * MOBA_BLOCK].reshape(n, Q_BLOCK, top, MOBA_BLOCK)
        p_own = p[..., top * MOBA_BLOCK:]
        return jnp.einsum('nqkj,nqkjd->nqd', p_sel, vs) + jnp.einsum('nqj,njd->nqd', p_own, vo)

    out = lax.map(one, (q_all, sel_all, val_all, jnp.arange(nq)))
    return out.transpose(1, 0, 2, 3).reshape(b, h, s_len, d)

def token_mixer(hn, w_in, b_gate, q_norm, w_uq, kv_norm, w_ukv, w_branch, w_out, cos_p, sin_p, cos_m, sin_m):
    bsz, s_len, _ = hn.shape
    proj = hn @ w_in
    moba_qkv, sb_qkv, c_q, c_kv, k_rope, gates = jnp.split(
        proj, [SPLIT_1, SPLIT_2, SPLIT_3, SPLIT_4, SPLIT_5], axis=-1)
    qa, ka, va = [to_heads(t, MOBA_HEADS) for t in jnp.split(moba_qkv, 3, axis=-1)]
    y_a = from_heads(moba_attention(partial_rope(qa, cos_p, sin_p), partial_rope(ka, cos_p, sin_p), va))
    qb_, kb_, vb_ = [to_heads(t, SB_HEADS) for t in jnp.split(sb_qkv, 3, axis=-1)]
    y_b = from_heads(stick_breaking_attention(qb_, kb_, vb_))
    qc = to_heads(rms_norm(c_q, q_norm) @ w_uq, MLA_HEADS)
    qc = jnp.concatenate([qc[..., :MLA_NOPE], apply_rope(qc[..., MLA_NOPE:], cos_m, sin_m)], axis=-1)
    kv = to_heads(rms_norm(c_kv, kv_norm) @ w_ukv, MLA_HEADS)
    k_nope, vc = kv[..., :MLA_NOPE], kv[..., MLA_NOPE:]
    kr = jnp.broadcast_to(apply_rope(k_rope, cos_m, sin_m)[:, None], (bsz, MLA_HEADS, s_len, MLA_ROPE))
    y_c = from_heads(causal_softmax_attention(qc, jnp.concatenate([k_nope, kr], axis=-1), vc))
    g = jax.nn.sigmoid(gates.reshape(bsz, s_len, N_BRANCH, D_MODEL) + b_gate)
    ys = jnp.stack([y_a, y_b, y_c], axis=2)
    merged = jnp.einsum('bsnk,nkd,bsnd->bsd', ys, w_branch, g)
    return merged @ w_out

def swiglu(h, w_gate, w_up, w_down):
    return (jax.nn.silu(h @ w_gate) * (h @ w_up)) @ w_down

def modulate(x, g_pre, shift, scale):
    return rms_norm(x, g_pre) * (1 + scale) + shift

def residual_add(x, y, g_post, gate, res_w):
    return x + res_w * (1 + gate) * rms_norm(y, g_post)

def first_inputs(seed: int = 0) -> dict:
    key = jax.random.key(seed)
    ks = jax.random.split(key, 20)
    f32 = jnp.float32
    nrm = lambda k, shape, fan: jax.random.normal(k, shape, f32) * fan ** -0.5
    return {
        'x': jax.random.normal(ks[0], (BATCH, SEQ, D_MODEL), f32),
        'c': jax.random.normal(ks[1], (BATCH, D_MODEL), f32),
        'ada_w': 0.2 * nrm(ks[2], (DEPTH, D_MODEL, N_SUB * 3 * D_MODEL), D_MODEL),
        'ada_b': 0.01 * jax.random.normal(ks[3], (DEPTH, N_SUB * 3 * D_MODEL), f32),
        'norm_pre': 1.0 + 0.05 * jax.random.normal(ks[4], (DEPTH, N_SUB, D_MODEL), f32),
        'norm_post': 1.0 + 0.05 * jax.random.normal(ks[5], (DEPTH, N_SUB, D_MODEL), f32),
        'ffn_w_gate': nrm(ks[6], (DEPTH, 2, D_MODEL, D_FF), D_MODEL),
        'ffn_w_up': nrm(ks[7], (DEPTH, 2, D_MODEL, D_FF), D_MODEL),
        'ffn_w_down': nrm(ks[8], (DEPTH, 2, D_FF, D_MODEL), D_FF),
        'mix_w_in': nrm(ks[9], (DEPTH, D_MODEL, N_IN), D_MODEL),
        'mix_b_gate': 0.1 * jax.random.normal(ks[10], (DEPTH, N_BRANCH, D_MODEL), f32),
        'mla_q_norm': 1.0 + 0.05 * jax.random.normal(ks[11], (DEPTH, MLA_Q_LORA), f32),
        'mla_w_uq': nrm(ks[12], (DEPTH, MLA_Q_LORA, MLA_HEADS * MLA_QK), MLA_Q_LORA),
        'mla_kv_norm': 1.0 + 0.05 * jax.random.normal(ks[13], (DEPTH, MLA_KV_LORA), f32),
        'mla_w_ukv': nrm(ks[14], (DEPTH, MLA_KV_LORA, MLA_HEADS * (MLA_NOPE + MLA_V)), MLA_KV_LORA),
        'mix_w_branch': nrm(ks[15], (DEPTH, N_BRANCH, BRANCH_W, D_MODEL), BRANCH_W),
        'mix_w_out': nrm(ks[16], (DEPTH, D_MODEL, D_MODEL), D_MODEL),
    }

def first_block(x, c, ada_w, ada_b, norm_pre, norm_post, ffn_w_gate, ffn_w_up, ffn_w_down, mix_w_in, mix_b_gate,
              mla_q_norm, mla_w_uq, mla_kv_norm, mla_w_ukv, mix_w_branch, mix_w_out):
    bsz, s_len, _ = x.shape
    cos_p, sin_p = rope_tables(PARTIAL_ROT, s_len)
    cos_m, sin_m = rope_tables(MLA_ROPE, s_len)
    c_act = jax.nn.silu(c)
    for l in range(DEPTH):
        mod = (c_act @ ada_w[l] + ada_b[l]).reshape(bsz, N_SUB, 3, D_MODEL)[:, :, :, None, :]
        h = modulate(x, norm_pre[l, 0], mod[:, 0, 0], mod[:, 0, 1])
        x = residual_add(x, swiglu(h, ffn_w_gate[l, 0], ffn_w_up[l, 0], ffn_w_down[l, 0]), norm_post[l, 0], mod[:, 0, 2], 0.5)
        h = modulate(x, norm_pre[l, 1], mod[:, 1, 0], mod[:, 1, 1])
        y = token_mixer(h, mix_w_in[l], mix_b_gate[l], mla_q_norm[l], mla_w_uq[l], mla_kv_norm[l], mla_w_ukv[l],
                        mix_w_branch[l], mix_w_out[l], cos_p, sin_p, cos_m, sin_m)
        x = residual_add(x, y, norm_post[l, 1], mod[:, 1, 2], 1.0)
        h = modulate(x, norm_pre[l, 2], mod[:, 2, 0], mod[:, 2, 1])
        x = residual_add(x, swiglu(h, ffn_w_gate[l, 1], ffn_w_up[l, 1], ffn_w_down[l, 1]), norm_post[l, 2], mod[:, 2, 2], 0.5)
    return x


CHUNK = 64
N_MIXERS = 2
N_LAYERS_A = (DEPTH + 1) // 2
N_LAYERS_B = DEPTH // 2

A_HEADS = 8
A_HEAD_DIM = 64
A_V_DIM = 2 * A_HEAD_DIM
T5_BUCKETS = 32
T5_MAX_DIST = 1024

B_HEADS = 16
B_HEAD_DIM = D_MODEL // B_HEADS
LEFT_CHUNKS = 8
BAND = (LEFT_CHUNKS + 1) * CHUNK
MAX_REL = 256

N_EXPERTS = 16
N_GROUPS = 4
E_PER_GROUP = N_EXPERTS // N_GROUPS
TOPK_GROUPS = 1
TOP_K = 2
D_FF_EXPERT = 512

NORM_EPS = 1e-6
NEG_INF = -1e30


def rms_norm_2(x, g):
    xf = x.astype(jnp.float32)
    y = xf * lax.rsqrt(jnp.mean(xf * xf, axis=-1, keepdims=True) + NORM_EPS)
    return (y * g.astype(jnp.float32)).astype(x.dtype)

def t5_bucket(rel):
    nb = T5_BUCKETS // 2
    ret = jnp.where(rel > 0, nb, 0)
    n = jnp.abs(rel)
    max_exact = nb // 2
    nf = jnp.maximum(n, 1).astype(jnp.float32)
    large = max_exact + (jnp.log(nf / max_exact) / math.log(T5_MAX_DIST / max_exact)
                         * (nb - max_exact)).astype(jnp.int32)
    large = jnp.minimum(large, nb - 1)
    return ret + jnp.where(n < max_exact, n, large)

def diff_attention(h, w_qkv, q_gain, k_gain, lam, subln_g, w_o, t5_bias, lambda_init):
    B, S, D = h.shape
    qkv = h @ w_qkv
    q, k, v = jnp.split(qkv, 3, axis=-1)
    q = q.reshape(B, S, A_HEADS, 2, A_HEAD_DIM)
    k = k.reshape(B, S, A_HEADS, 2, A_HEAD_DIM)
    v = v.reshape(B, S, A_HEADS, A_V_DIM)
    q = rms_norm_2(q, q_gain) * (A_HEAD_DIM ** -0.5)
    k = rms_norm_2(k, k_gain)
    lamf = lam.astype(jnp.float32)
    lam_full = (jnp.exp(jnp.sum(lamf[0] * lamf[1])) - jnp.exp(jnp.sum(lamf[2] * lamf[3]))
                + lambda_init)
    n_blocks = S // Q_BLOCK
    q_blocks = q.reshape(B, n_blocks, Q_BLOCK, A_HEADS, 2, A_HEAD_DIM).transpose(1, 0, 2, 3, 4, 5)
    k_pos = jnp.arange(S, dtype=jnp.int32)

    def one_block(args):
        qb, blk = args
        q_pos = blk * Q_BLOCK + jnp.arange(Q_BLOCK, dtype=jnp.int32)
        rel = k_pos[None, :] - q_pos[:, None]
        bias = t5_bias.astype(jnp.float32)[t5_bucket(rel)].transpose(2, 0, 1)
        allowed = (k_pos[None, :] // CHUNK) <= (q_pos[:, None] // CHUNK)
        s = jnp.einsum('bqhmd,bkhmd->bmhqk', qb, k).astype(jnp.float32) + bias[None, None]
        s = jnp.where(allowed[None, None, None], s, NEG_INF)
        p = jax.nn.softmax(s, axis=-1)
        a = p[:, 0] - lam_full * p[:, 1]
        return jnp.einsum('bhqk,bkhe->bqhe', a.astype(v.dtype), v)

    o = lax.map(one_block, (q_blocks, jnp.arange(n_blocks, dtype=jnp.int32)))
    o = o.transpose(1, 0, 2, 3, 4).reshape(B, S, A_HEADS, A_V_DIM)
    o = rms_norm_2(o, subln_g) * (1.0 - lambda_init)
    return o.reshape(B, S, D) @ w_o

def chunked_attention(h, w_qkv, q_gain, k_gain, rel_bias, w_o):
    B, S, D = h.shape
    NC = S // CHUNK
    qkv = h @ w_qkv
    q, k, v = jnp.split(qkv, 3, axis=-1)
    q = rms_norm_2(q.reshape(B, S, B_HEADS, B_HEAD_DIM), q_gain) * (B_HEAD_DIM ** -0.5)
    k = rms_norm_2(k.reshape(B, S, B_HEADS, B_HEAD_DIM), k_gain)
    v = v.reshape(B, S, B_HEADS, B_HEAD_DIM)
    pad = ((0, 0), (LEFT_CHUNKS * CHUNK, 0), (0, 0), (0, 0))
    kp = jnp.pad(k, pad)
    vp = jnp.pad(v, pad)
    qi = jnp.arange(CHUNK, dtype=jnp.int32)
    kb = jnp.arange(BAND, dtype=jnp.int32)
    rel = kb[None, :] - LEFT_CHUNKS * CHUNK - qi[:, None]
    idx = jnp.clip(rel, -MAX_REL, MAX_REL) + MAX_REL
    bias = rel_bias.astype(jnp.float32)[:, idx]
    band_chunk = kb // CHUNK
    q_chunks = q.reshape(B, NC, CHUNK, B_HEADS, B_HEAD_DIM).transpose(1, 0, 2, 3, 4)

    def one_chunk(args):
        qc, ci = args
        kband = lax.dynamic_slice_in_dim(kp, ci * CHUNK, BAND, axis=1)
        vband = lax.dynamic_slice_in_dim(vp, ci * CHUNK, BAND, axis=1)
        valid = (ci - LEFT_CHUNKS + band_chunk) >= 0
        s = jnp.einsum('bqhd,bkhd->bhqk', qc, kband).astype(jnp.float32) + bias[None]
        s = jnp.where(valid[None, None, None, :], s, NEG_INF)
        p = jax.nn.softmax(s, axis=-1)
        return jnp.einsum('bhqk,bkhd->bqhd', p.astype(vband.dtype), vband)

    o = lax.map(one_chunk, (q_chunks, jnp.arange(NC, dtype=jnp.int32)))
    o = o.transpose(1, 0, 2, 3, 4).reshape(B, S, D)
    return o @ w_o

def grouped_moe(h, router_w, router_bias, w_gate, w_up, w_down):
    B, S, D = h.shape
    t = h.reshape(B * S, D)
    scores = jax.nn.sigmoid((t @ router_w).astype(jnp.float32))
    sel = scores + router_bias.astype(jnp.float32)
    grp = sel.reshape(-1, N_GROUPS, E_PER_GROUP)
    group_score = lax.top_k(grp, TOP_K)[0].sum(-1)
    _, g_idx = lax.top_k(group_score, TOPK_GROUPS)
    group_mask = jax.nn.one_hot(g_idx, N_GROUPS, dtype=jnp.float32).sum(1) > 0
    expert_mask = jnp.repeat(group_mask, E_PER_GROUP, axis=1)
    masked = jnp.where(expert_mask, sel, NEG_INF)
    _, e_idx = lax.top_k(masked, TOP_K)
    w = jnp.take_along_axis(scores, e_idx, axis=1)
    w = w / jnp.sum(w, axis=-1, keepdims=True)
    gates = jnp.sum(jax.nn.one_hot(e_idx, N_EXPERTS, dtype=jnp.float32) * w[..., None], axis=1)
    gates = gates.astype(t.dtype)
    out = jnp.zeros_like(t)
    for e in range(N_EXPERTS):
        he = jax.nn.silu(t @ w_gate[e]) * (t @ w_up[e])
        out = out + gates[:, e:e + 1] * (he @ w_down[e])
    return out.reshape(B, S, D)

def second_inputs(seed: int = 0) -> dict:
    key = jax.random.key(seed)
    ks = jax.random.split(key, 24)
    D, F, E = D_MODEL, D_FF_EXPERT, N_EXPERTS
    nrm = lambda k, shape, s: jax.random.normal(k, shape, jnp.float32) * s
    gain = lambda k, shape: 1.0 + 0.02 * jax.random.normal(k, shape, jnp.float32)
    return {
        "x": nrm(ks[0], (BATCH, SEQ, D), 1.0),
        "c": nrm(ks[1], (BATCH, D), 1.0),
        "ada_w": nrm(ks[2], (DEPTH, D, 6 * D), 0.5 * D ** -0.5),
        "ada_b": nrm(ks[3], (DEPTH, 6 * D), 0.01),
        "norm_mix_g": gain(ks[4], (DEPTH, D)),
        "norm_ffn_g": gain(ks[5], (DEPTH, D)),
        "t5_bias": nrm(ks[6], (T5_BUCKETS, A_HEADS), 0.2),
        "a_w_qkv": nrm(ks[7], (N_LAYERS_A, D, 3 * D), D ** -0.5),
        "a_q_gain": gain(ks[8], (N_LAYERS_A, A_HEAD_DIM)),
        "a_k_gain": gain(ks[9], (N_LAYERS_A, A_HEAD_DIM)),
        "a_lambda": nrm(ks[10], (N_LAYERS_A, 4, A_HEAD_DIM), 0.1),
        "a_subln_g": gain(ks[11], (N_LAYERS_A, A_V_DIM)),
        "a_w_o": nrm(ks[12], (N_LAYERS_A, D, D), D ** -0.5),
        "b_w_qkv": nrm(ks[13], (N_LAYERS_B, D, 3 * D), D ** -0.5),
        "b_q_gain": gain(ks[14], (N_LAYERS_B, B_HEAD_DIM)),
        "b_k_gain": gain(ks[15], (N_LAYERS_B, B_HEAD_DIM)),
        "b_rel_bias": nrm(ks[16], (N_LAYERS_B, B_HEADS, 2 * MAX_REL + 1), 0.2),
        "b_w_o": nrm(ks[17], (N_LAYERS_B, D, D), D ** -0.5),
        "router_w": nrm(ks[18], (D, E), D ** -0.5),
        "router_bias": nrm(ks[19], (E,), 0.01),
        "moe_w_gate": nrm(ks[20], (DEPTH, E, D, F), D ** -0.5),
        "moe_w_up": nrm(ks[21], (DEPTH, E, D, F), D ** -0.5),
        "moe_w_down": nrm(ks[22], (DEPTH, E, F, D), F ** -0.5),
    }

def second_block(x, c, ada_w, ada_b, norm_mix_g, norm_ffn_g, t5_bias,
              a_w_qkv, a_q_gain, a_k_gain, a_lambda, a_subln_g, a_w_o,
              b_w_qkv, b_q_gain, b_k_gain, b_rel_bias, b_w_o,
              router_w, router_bias, moe_w_gate, moe_w_up, moe_w_down):
    silu_c = jax.nn.silu(c)
    for i in range(DEPTH):
        mod = silu_c @ ada_w[i] + ada_b[i]
        sh1, sc1, g1, sh2, sc2, g2 = [m[:, None, :] for m in jnp.split(mod, 6, axis=-1)]
        h = rms_norm_2(x, norm_mix_g[i]) * (1.0 + sc1) + sh1
        if i % N_MIXERS == 0:
            j = i // N_MIXERS
            lambda_init = 0.8 - 0.6 * math.exp(-0.3 * i)
            y = diff_attention(h, a_w_qkv[j], a_q_gain[j], a_k_gain[j], a_lambda[j],
                               a_subln_g[j], a_w_o[j], t5_bias, lambda_init)
        else:
            j = i // N_MIXERS
            y = chunked_attention(h, b_w_qkv[j], b_q_gain[j], b_k_gain[j], b_rel_bias[j], b_w_o[j])
        x = x + g1 * y
        h = rms_norm_2(x, norm_ffn_g[i]) * (1.0 + sc2) + sh2
        x = x + g2 * grouped_moe(h, router_w, router_bias, moe_w_gate[i], moe_w_up[i], moe_w_down[i])
    return x


def setup_inputs(seed=0):
    out = dict(first_inputs(seed))
    for name, value in second_inputs(seed + 1).items():
        if name != "x":
            out[name + "_2"] = value
    return out


def reference(
    x, c, ada_w, ada_b, norm_pre, norm_post, ffn_w_gate, ffn_w_up, ffn_w_down, mix_w_in,
    mix_b_gate, mla_q_norm, mla_w_uq, mla_kv_norm, mla_w_ukv, mix_w_branch, mix_w_out, c_2,
    ada_w_2, ada_b_2, norm_mix_g_2, norm_ffn_g_2, t5_bias_2, a_w_qkv_2, a_q_gain_2, a_k_gain_2,
    a_lambda_2, a_subln_g_2, a_w_o_2, b_w_qkv_2, b_q_gain_2, b_k_gain_2, b_rel_bias_2, b_w_o_2,
    router_w_2, router_bias_2, moe_w_gate_2, moe_w_up_2, moe_w_down_2,
):
    x = first_block(
        x, c, ada_w, ada_b, norm_pre, norm_post, ffn_w_gate, ffn_w_up, ffn_w_down, mix_w_in,
        mix_b_gate, mla_q_norm, mla_w_uq, mla_kv_norm, mla_w_ukv, mix_w_branch, mix_w_out,
    )
    return second_block(
        x, c_2, ada_w_2, ada_b_2, norm_mix_g_2, norm_ffn_g_2, t5_bias_2, a_w_qkv_2, a_q_gain_2,
        a_k_gain_2, a_lambda_2, a_subln_g_2, a_w_o_2, b_w_qkv_2, b_q_gain_2, b_k_gain_2,
        b_rel_bias_2, b_w_o_2, router_w_2, router_bias_2, moe_w_gate_2, moe_w_up_2,
        moe_w_down_2,
    )


_drawn_inputs = setup_inputs


def setup_inputs(seed=0):
    import zlib

    import numpy as np

    out = dict(_drawn_inputs(seed))
    spreads = {}
    factors = {'mla_q_norm': 3.23,
     'ada_b_2': 4.241,
     'norm_mix_g_2': 8.0,
     'norm_ffn_g_2': 3.979,
     't5_bias_2': 3.646,
     'a_q_gain_2': 8.0,
     'a_k_gain_2': 8.0,
     'a_lambda_2': 3.836,
     'a_subln_g_2': 8.0,
     'b_q_gain_2': 8.0,
     'b_k_gain_2': 8.0,
     'b_rel_bias_2': 8.0}
    for name, (base, spread) in spreads.items():
        noise = np.random.default_rng([zlib.crc32(name.encode()), seed]).standard_normal(out[name].shape)
        drawn = base * np.exp(spread * noise) if base else spread * noise
        out[name] = __import__('jax').numpy.asarray(drawn.astype(out[name].dtype))
    for name, factor in factors.items():
        out[name] = (out[name] * factor).astype(out[name].dtype)
    return out
```

```python
from contextlib import ExitStack
import math

import numpy as np
import concourse.bass as bass
from concourse import mybir

F32 = mybir.dt.float32
F32R = mybir.dt.float32r
ACT = mybir.ActivationFunctionType
ALU = mybir.AluOpType
AX = mybir.AxisListType.X

P = 128
S = 256
NT = S // P
D = 1024
KT = D // P
DEPTH = 2
FF = 2816
HD = 64
NH = 8
W_BR = NH * HD
QL, KVL, ROPE, NOPE = 256, 128, 32, 64
QK_C = NOPE + ROPE
ROT = HD // 4
THETA = 500000.0
EXP, EF = 16, 512
GROUPS = 4
BAND_CHUNK = 64
EPS = 1e-6
BIG = 1e30
BLK = 256
CW = 2048

STAGES = 6
PARTS = 3
NVEC = DEPTH * 9 + DEPTH * 6
N_ADA = NVEC * 4
NSUB = DEPTH * 3 + DEPTH * 2
FFN_BLOCKS = FF // BLK
MOE_BLOCKS = EXP * EF // BLK
PROJ_W = 6 * 512 + QL + KVL + ROPE

Y_COL = (0, 1536, 512)
MQ, MK = 512, 2048


def mla_value_col(h):
    return (MQ if h < 4 else MK) + NH * QK_C + (h % 4) * HD



CONST = {}
_at = 0
for _name, _w in (("ident", P), ("flip", P), ("ones", P), ("tri", P), ("before", P), ("slots", P), ("causal", 384), ("strict", 384), ("chunked", 384),
                  ("cos_p", NT * 8), ("sin_p", NT * 8), ("cos_m", NT * 16), ("sin_m", NT * 16),
                  ("rank", NT * EXP), ("grank", NT * GROUPS)):
    CONST[_name] = (_at, _at + _w)
    _at += _w
N_CONST = _at
VEC = {}
_at = 0
for _name, _w in (("c", KT), ("c_2", KT), ("ada_b", NVEC * KT), ("pre", NSUB * KT), ("post", DEPTH * 3 * KT),
                  ("q_norm", DEPTH * 2), ("kv_norm", DEPTH), ("a_q", 1), ("a_k", 1), ("subln", 1), ("b_q", 1), ("b_k", 1)):
    VEC[_name] = (_at, _at + _w)
    _at += _w
N_VEC = _at


def make_plan():
    steps = []
    for l in range(DEPTH):
        steps += [("norm", 3 * l), ("ffn", 3 * l, FFN_BLOCKS, None), ("resid", 3 * l)]
        k = 3 * l + 1
        steps += [("norm", k), ("proj", 7), ("rope_p",),
                  ("qkT", "pairs", 0, 512, None), ("soft", "moba"),
                  ("qkT", "pairs", 1536, 2048, None), ("stick",),
                  ("mla_norm", l), ("mla_T", l), ("mla_up",), ("rope_m",), ("qkT", "mla", MQ, MK, None), ("soft", "mla"),
                  ("merge", l), ("backT", "merged"), ("out", k), ("resid", k)]
        steps += [("norm", 3 * l + 2), ("ffn", 3 * l + 2, FFN_BLOCKS, None), ("resid", 3 * l + 2)]
    for l in range(DEPTH):
        k = 3 * DEPTH + 2 * l
        which = "ab"[l]
        steps += [("norm", k), ("proj", 6), ("head_norm",),
                  ("qkT", "wide", 0, 1024, which), ("diff" if l == 0 else "soft", "band")]
        steps += [("out_norm",)] if l == 0 else []
        steps += [("backT", "subln" if l == 0 else "y"), ("out", k), ("resid", k)]
        steps += [("norm", k + 1), ("route", l), ("ffn", k + 1, MOE_BLOCKS, "moe"), ("resid", k + 1)]
    kinds = ("n", "u", "th", "tf", "hid", "req", "src", "x", "ev", "sc", "pr", "ov", "st", "mg", "sq", "mx", "hn")
    at = dict.fromkeys(kinds, 0)
    at["n"] = N_ADA
    plan = []
    for step in steps:
        plan.append((step, dict(at)))
        kind = step[0]
        uses = {
            "norm": dict(u=4, th=4, tf=4, req=1, src=1),
            "proj": dict(n=2 * step[1], ev=step[1]) if kind == "proj" else None,
            "rope_p": dict(src=1), "rope_m": dict(src=1), "mla_norm": dict(req=1, src=1),
            "mla_T": dict(u=2, th=2, tf=2), "mla_up": dict(n=2, ev=2),
            "qkT": dict(u=4 if "pairs" in step else 8),
            "stick": dict(sc=8, pr=8, ov=8, st=8),
            "merge": dict(n=18, u=6, th=6, mg=6), "out": dict(n=4, u=2, tf=2),
            "resid": dict(x=1, req=1 if step[1:] and isinstance(step[1], int) and step[1] < 6 else 0),
            "head_norm": dict(req=1, src=1, sq=2, hn=1), "out_norm": dict(req=1, src=1, sq=1),
            "diff": dict(sc=16, mx=16, pr=16, u=8, ov=8), "route": dict(u=2, th=1),
        }
        if kind == "ffn":
            nb = step[2]
            used = dict(n=3 * nb, u=nb + 2, th=nb, tf=2, hid=nb)
            if step[3]:
                used.update(u=MOE_TURNS, th=MOE_HIGHS)
        elif kind == "soft":
            h = 16 if step[1] == "band" else 8
            used = dict(sc=h, mx=h, pr=h, u=h, ov=h)
        elif kind == "backT":
            used = dict(u=4, th=4, tf=4) if step[1] == "subln" else dict(u=4, th=4)
        else:
            used = uses[kind]
        for name, c in used.items():
            at[name] += c
    plan.append((("end",), dict(at)))
    return plan


MOE_TURNS = 2 + 8 + 5 * EXP + MOE_BLOCKS
MOE_HIGHS = 4 * EXP + MOE_BLOCKS


def moe_gather_at(u0, e):
    return u0 if e == 0 else u0 + 6 + 7 * (e - 1)


def moe_scatter_at(u0, g):
    if g == 0:
        return u0 + 5
    if g >= MOE_BLOCKS - 3:
        return u0 + 11 + 7 * (EXP - 2) + g - (MOE_BLOCKS - 3)
    return u0 + 11 + 7 * ((g + 1) // 2 - 1) + (g + 1) % 2


def block_order(nb):
    peeled = 1 if nb % 2 == 0 else 2
    return peeled, (nb - 1 - peeled) // 2


def build(nc, wstream, xin, const_in, vec_in, bgate_in, lam_in, rbias_in, t5_in, t5hot_in, rel_in, rw_in, out):
    plan = make_plan()
    n_chunks = plan[-1][1]["n"]
    assert n_chunks % STAGES == 0 and N_ADA % STAGES == 0 and N_ADA % PARTS == 0
    loc = {step: base for step, base in plan}

    with ExitStack() as ctx:
        def sb(name, shape, dt=F32):
            return ctx.enter_context(nc.sbuf_tensor(name, shape, dt))

        def sem(name):
            return ctx.enter_context(nc.semaphore(name))

        stage = sb("stage", [P, STAGES, CW])
        w_hi = sb("w_hi", [P, PARTS, CW], F32R)
        w_lo = sb("w_lo", [P, PARTS, CW], F32R)
        x = sb("x_tok", [P, NT, D])
        tok = sb("tok", [P, NT, D])
        hT_hi = sb("hT_hi", [P, KT, S], F32R)
        hT_lo = sb("hT_lo", [P, KT, S], F32R)
        proj_at = nc.sbuf_base
        proj = sb("proj", [P, NT, PROJ_W])
        h_hi = nc.alloc_sbuf_tensor_at("h_hi", [P, NT, D], F32R, offset=proj_at)
        h_lo = nc.alloc_sbuf_tensor_at("h_lo", [P, NT, D], F32R, offset=proj_at + NT * D * 4)
        pick = nc.alloc_sbuf_tensor_at("pick", [P, 2, NT, P], F32R, offset=proj_at + 2 * NT * D * 4)
        yT_hi = sb("yT_hi", [P, 4, S], F32R)
        yT_lo = sb("yT_lo", [P, 4, S], F32R)
        qk = sb("qk", [P, 16, S])
        pair = sb("pair", [P, 2, NT, BLK])
        hid_hi = yT_hi[:, 0:2, :].rearrange("p a s -> p (a s)")
        hid_lo = yT_lo[:, 0:2, :].rearrange("p a s -> p (a s)")
        tf = sb("tf", [P, 2, 512])
        prob = tok[:, :, 512:896]
        probT = pair[:].rearrange("p a t c -> p a (t c)")[:, :, 0:384]
        mixp = tf[:, 0, 0:384]
        bias_in = proj[:, :, 3072:3456]
        rope_t = pair[:, 0].rearrange("p t c -> p (t c)").rearrange("p (i w) -> p i w", i=4)
        pickg = qk[:, 0:2, :].rearrange("p a (t s) -> p a t s", t=NT)
        pickT = qk[:, 2:4, :]
        const = sb("const", [P, N_CONST])
        vec = sb("vec", [P, N_VEC])
        mod = sb("mod", [P, NVEC, KT])
        c_act = sb("c_act", [P, 2 * KT])
        c_tmp = sb("c_tmp", [P, 2 * KT])
        ss = sb("ss", [P, 64])
        rs = sb("rs", [P, 64])
        mhalf = sb("mhalf", [P, 64])
        nmax = sb("nmax", [P, 2, 2])
        rsum = sb("rsum", [P, 2, 2])
        rinv = sb("rinv", [P, 2, 2])
        lam = sb("lam", [P, 4 * HD])
        lam_s = sb("lam_s", [P, 4])
        rw = sb("rw", [P, KT * EXP])
        rw_hi = sb("rw_hi", [P, KT * EXP], F32R)
        rw_lo = sb("rw_lo", [P, KT * EXP], F32R)
        rbias = sb("rbias", [P, EXP])
        gates = sb("gates", [P, NT, EXP])
        rank = sb("rank", [P, NT, EXP])
        fullest = sb("fullest", [P, 1])
        fullest_i = sb("fullest_i", [P, 1], mybir.dt.int32)
        rt = sb("rt", [P, 8, NT * EXP])
        t5 = sb("t5", [32, 8])
        t5hot = tf[0:32, 1, :]
        t5row = tf[0:8, 0, :]
        t5_dram = nc.dram_tensor("t5_rows", [8, 512], F32)

        acc = ctx.enter_context(nc.psum_tensor("acc", [P, 4, 512], F32))
        gu = ctx.enter_context(nc.psum_tensor("gu", [P, 2, 512], F32))
        tr = ctx.enter_context(nc.psum_tensor("tr", [P, 2, 512], F32))

        landed = [sem(f"landed{i}") for i in range(STAGES)]
        chunk_ready = sem("chunk_ready")
        hi_ready = sem("hi_ready")
        pe_used = sem("pe_used")
        tr_full = sem("tr_full")
        tr_free = sem("tr_free")
        th_ready = sem("th_ready")
        tf_ready = sem("tf_ready")
        sg_ready = sem("sg_ready")
        hid_ready = sem("hid_ready")
        rs_req = sem("rs_req")
        rs_done = sem("rs_done")
        src_ready = sem("src_ready")
        x_ready = sem("x_ready")
        ev_ready = sem("ev_ready")
        s_full = sem("s_full")
        s_free = sem("s_free")
        m_ready = sem("m_ready")
        p_ready = sem("p_ready")
        a_ready = sem("a_ready")
        o_full = sem("o_full")
        o_free = sem("o_free")
        soft_ready = sem("soft_ready")
        sp_ready = sem("sp_ready")
        c_full = sem("c_full")
        arg_ready = sem("arg_ready")
        z_ready = sem("z_ready")
        e_ready = sem("e_ready")
        mg_ready = sem("mg_ready")
        bg_in = [sem("bg_in0"), sem("bg_in1")]
        bias_ld = [sem("bias_ld0"), sem("bias_ld1")]
        ld = sem("ld")
        act_up = sem("act_up")
        dve_up = sem("dve_up")
        pool_up = sem("pool_up")
        c_exp = sem("c_exp")
        c_ready = sem("c_ready")
        ada_out = sem("ada_out")
        sq_ready = sem("sq_ready")
        sq_used = sem("sq_used")
        ada_sum = sem("ada_sum")
        mod_ready = sem("mod_ready")
        sent_ready = sem("sent_ready")
        count_ready = sem("count_ready")
        pick_ready = sem("pick_ready")
        rwhi_ready = sem("rwhi_ready")
        rw_ready = sem("rw_ready")
        t5_mm = sem("t5_mm")
        t5_sb = sem("t5_sb")
        t5_st = sem("t5_st")
        lam_dot = sem("lam_dot")
        lam_exp = sem("lam_exp")
        mh_ready = sem("mh_ready")
        st_out = sem("st_out")
        N_LD = 10

        def cst(name):
            return const[:, CONST[name][0]:CONST[name][1]]

        def col(name, i):
            return vec[:, VEC[name][0] + i:VEC[name][0] + i + 1]

        ident, flip, ones, tri = cst("ident"), cst("flip"), cst("ones"), cst("tri")
        block = ctx.enter_context(nc.Block())

        @block.sync
        def _(sp):
            def chunk(dst, n):
                return sp.dma_start(stage[:, dst, :], wstream[bass.ds(n, 1)].rearrange("a p c -> (a p) c"))

            for n in range(STAGES):
                chunk(n, n).then_inc(landed[n], 16)
            with sp.Fori(1, n_chunks // STAGES) as i:
                for s in range(STAGES):
                    sp.wait_ge(chunk_ready, i * STAGES + (s + 1 - STAGES))
                    chunk(s, i * STAGES + s).then_inc(landed[s], 16)
            sp.wait_ge(x_ready, NSUB)
            sp.dma_start(out.rearrange("(t p) d -> p t d", p=P), x[:]).then_inc(st_out, 16)
            sp.wait_ge(st_out, 16)

        @block.gpsimd
        def _(pool):
            pool.dma_start(vec[:], vec_in).then_inc(ld, 16)
            pool.dma_start(const[:], const_in).then_inc(ld, 16)
            pool.dma_start(x[:], xin.rearrange("(t p) d -> p t d", p=P)).then_inc(ld, 16)
            pool.dma_start(rw[:], rw_in).then_inc(ld, 16)
            pool.dma_start(rbias[:], rbias_in.partition_broadcast(P)).then_inc(ld, 16)
            pool.dma_start(lam[:], lam_in.partition_broadcast(P)).then_inc(ld, 16)
            pool.dma_start(t5[:], t5_in).then_inc(ld, 16)
            pool.dma_start(t5hot, t5hot_in).then_inc(ld, 16)
            pool.memset(mhalf[:], -0.5).then_inc(mh_ready, 1)
            pool.wait_ge(mh_ready, 1)
            pool.wait_ge(t5_sb, 1)
            pool.dma_start(t5_dram.ap(), t5row).then_inc(t5_st, 16)
            pool.wait_ge(t5_st, 16)
            ups = 0

            def root(b, w):
                nonlocal ups
                pool.wait_ge(rs_req, b["req"] + 1)
                pool.tensor_scalar(ss[:, 0:w], ss[:, 0:w], EPS, None, ALU.add).then_inc(pool_up, 1)
                ups += 1
                pool.wait_ge(pool_up, ups)
                pool.tensor_tensor(rs[:, 0:w], ss[:, 0:w], mhalf[:, 0:w], ALU.pow).then_inc(rs_done, 1)

            loads = 0
            for step, b in plan:
                kind = step[0]
                if kind == "norm" or (kind == "resid" and step[1] < 6):
                    root(b, 2)
                elif kind == "mla_norm":
                    root(b, 4)
                elif kind == "head_norm":
                    root(b, 64)
                elif kind == "out_norm":
                    root(b, 16)
                elif (kind == "soft" and step[1] == "band") or kind == "diff":
                    table, pitch, heads = (t5_dram, 512, 8) if kind == "diff" else (rel_in.tensor, 513, 16)
                    per = 2 if kind == "diff" else 1
                    for h in range(heads):
                        if h >= 2:
                            pool.wait_ge(s_full, b["sc"] + per * (h - 1))
                        for q, (a, w) in enumerate(((0, 128), (128, 256))):
                            win = bass.AP(table, h * pitch + 129 - 128 * q, [[1, P], [1, w]])
                            pool.dma_start(bias_in[:, h % 2, a:a + w], win).then_inc(bias_ld[h % 2], 16)
                        loads += 1

        @block.scalar
        def _(act):
            ups = 0

            def hi(n, i=0, rounds=1):
                act.wait_ge(landed[n % STAGES], 16 * (n // STAGES + 1) + 16 * rounds * i)
                act.wait_ge(pe_used, n - N_ADA + 1 + STAGES * rounds * i)
                act.activation(w_hi[:, n % PARTS, :], stage[:, n % STAGES, :], ACT.Copy).then_inc(hi_ready, 1)

            def ahead(n):
                if n < n_chunks:
                    hi(n)
                    hi(n + 1)

            def own(ins):
                nonlocal ups
                ups += 1
                ins.then_inc(act_up, 1)
                act.wait_ge(act_up, ups)

            act.wait_ge(ld, 16 * 8)
            act.activation(c_tmp[:], vec[:, 0:2 * KT], ACT.Exp, scale=-1.0).then_inc(c_exp, 1)
            act.activation(rw_hi[:], rw[:], ACT.Copy).then_inc(rwhi_ready, 1)
            act.wait_ge(t5_mm, 1)
            act.activation(t5row, tr[0:8, 0, :], ACT.Copy).then_inc(t5_sb, 1)
            act.wait_ge(lam_dot, 1)
            act.activation(lam_s[:, 2:4], lam_s[:, 0:2], ACT.Exp).then_inc(lam_exp, 1)

            def squares(b, srcs):
                for i, (src, width) in enumerate(srcs):
                    ins = act.activation(tok[:, i % 2, 0:width], src, ACT.Square, scale=width ** -0.5,
                                         accum_out=ss[:, i:i + 1])
                    if i < len(srcs) - 1:
                        own(ins)
                ins.then_inc(rs_req, 1)

            def take_hi(b, rounds, dst, plain, width=512):
                for r in range(rounds):
                    if plain:
                        act.wait_ge(tr_full, b["u"] + r + 1)
                        src = tr[:, (b["u"] + r) % 2, :]
                    else:
                        act.wait_ge(tf_ready, b["tf"] + r + 1)
                        src = tf[:, (b["tf"] + r) % 2, :]
                    w = width[r] if isinstance(width, tuple) else width
                    d = dst[:, 2 * r:2 * r + w // S, :].rearrange("p a s -> p (a s)")
                    act.activation(d, src[:, 0:w], ACT.Copy).then_inc(th_ready, 1)

            def ffn(b, nb):
                peeled, turns = block_order(nb)
                n0, u0, g0 = b["n"], b["u"] + 0, b["hid"]

                def silu(g, i=0):
                    act.wait_ge(pe_used, n_b(g) - N_ADA + 1 + PARTS + STAGES * i)
                    if not isinstance(i, int) or g >= 1:
                        act.wait_ge(hid_ready, g0 + g + 2 * i)
                    act.activation(pair[:, 0], gu[:, :, 0:BLK], ACT.Silu).then_inc(sg_ready, 1)

                def n_b(g):
                    return n0 + 1 if g == 0 else n0 + 3 * g

                def turn_hi(g, u, i=0):
                    act.wait_ge(tr_full, u + 1 + 2 * i)
                    if not isinstance(i, int) or g >= 1:
                        act.wait_ge(pe_used, n0 + 3 * g + 1 - N_ADA + 1 + PARTS + STAGES * i)
                    act.activation(hid_hi, tr[:, u % 2, :], ACT.Copy).then_inc(th_ready, 1)

                def block_(g, i=0):
                    hi(n0 + 3 * g - 1, i)
                    silu(g - 1, i)
                    hi(n0 + 3 * g, i)
                    hi(n0 + 3 * g + 1, i)
                    turn_hi(g - 1, u_of(g - 1), i)

                def u_of(g):
                    return u0 + 2 + g

                for g in range(1, 1 + peeled):
                    block_(g)
                with act.Fori(0, turns) as i:
                    block_(1 + peeled, i)
                    block_(2 + peeled, i)
                silu(nb - 1)
                hi(n0 + 3 * nb - 1)
                turn_hi(nb - 1, u_of(nb - 1))
                ahead(n0 + 3 * nb)

            def moe(b, l):
                n0, g0 = b["n"], b["hid"]
                u0, th_u = b["u"] + 2 + 8, None

                def chunk_of(g):
                    return n0 if g == 0 else n0 + 3 * g - 1

                def silu(g, i=0):
                    act.wait_ge(pe_used, chunk_of(g) + 1 - N_ADA + 1 + PARTS + 12 * i)
                    if not isinstance(i, int) or g >= 2:
                        act.wait_ge(hid_ready, g0 + g - 1 + 4 * i)
                    act.activation(pair[:, 0, g % 2, :], gu[:, g % 2, 0:BLK], ACT.Silu).then_inc(sg_ready, 1)

                def turn_hi(g, u, i=0):
                    act.wait_ge(tr_full, u + 1 + 14 * i)
                    if not isinstance(i, int) or g >= 1:
                        act.wait_ge(pe_used, n0 + 3 * g + 1 - N_ADA + 1 + PARTS + 12 * i)
                    act.activation(hid_hi, tr[:, u % 2, :], ACT.Copy).then_inc(th_ready, 1)

                def gather_hi(e, u, i=0):
                    for r in range(4):
                        act.wait_ge(tr_full, u + r + 1 + 14 * i)
                        dst = hT_hi[:, 2 * r:2 * r + 2, (e % 2) * P:(e % 2 + 1) * P]
                        act.activation(dst, tr[:, (u + r) % 2, 0:2 * P].rearrange("p (k s) -> p k s", k=2),
                                       ACT.Copy).then_inc(th_ready, 1)

                def expert(e, i=0):
                    for g in (2 * e, 2 * e + 1):
                        if g:
                            hi(chunk_of(g), i, 2)
                            silu(g - 1, i)
                            hi(chunk_of(g) + 1, i, 2)
                            hi(chunk_of(g) + 2, i, 2)
                            turn_hi(g - 1, moe_scatter_at(u0, g - 1), i)
                    if not (isinstance(i, int) and e == EXP - 1):
                        gather_hi(e + 1, moe_gather_at(u0, e + 1), i)

                gather_hi(0, u0)
                expert(0)
                with act.Fori(0, (EXP - 2) // 2) as i:
                    expert(1, i)
                    expert(2, i)
                expert(EXP - 1)
                silu(MOE_BLOCKS - 1)
                hi(n0 + 3 * MOE_BLOCKS - 1)
                turn_hi(MOE_BLOCKS - 1, moe_scatter_at(u0, MOE_BLOCKS - 1))
                ahead(n0 + 3 * MOE_BLOCKS)

            def soft(b, heads):
                for a in range(heads):
                    act.wait_ge(m_ready, b["mx"] + a + 1)
                    s = (b["sc"] + a) % 2
                    for q, (lo, w) in enumerate(((0, 128), (128, 256))):
                        ins = act.activation(prob[:, s, lo:lo + w], prob[:, s, lo:lo + w], ACT.Exp,
                                             bias=nmax[:, s, q:q + 1], accum_out=rsum[:, s, q:q + 1])
                    ins.then_inc(p_ready, 1)

            ahead(N_ADA)
            for step, b in plan:
                kind = step[0]
                if kind == "norm":
                    k = step[1]
                    act.wait_ge(x_ready, k) if k else act.wait_ge(mod_ready, 1)
                    squares(b, [(x[:, t, :], D) for t in range(NT)])
                    take_hi(b, 4, hT_hi, False)
                elif kind == "ffn" and not step[3]:
                    ffn(b, step[2])
                elif kind == "ffn":
                    l = (step[1] - 3 * DEPTH) // 2
                    act.wait_ge(count_ready, l + 1)
                    most = act.value_load(fullest_i[0:1, 0:1], min_val=0, max_val=S)
                    with act.If(most <= P):
                        moe(b, l)
                    with act.Else():
                        ffn(b, step[2])
                        act.nop().then_inc(th_ready, MOE_HIGHS - MOE_BLOCKS)
                elif kind == "resid" and step[1] < 6:
                    act.wait_ge(pe_used, b["n"] - N_ADA + PARTS)
                    for t in range(NT):
                        ins = act.activation(tok[:, 1, :], acc[:, 2 * t:2 * t + 2, :].rearrange("p a c -> p (a c)"),
                                             ACT.Square, scale=D ** -0.5, accum_out=ss[:, t:t + 1])
                        if t < NT - 1:
                            own(ins)
                    ins.then_inc(rs_req, 1)
                elif kind == "proj":
                    blocks = step[1]

                    def evac(j):
                        act.wait_ge(pe_used, b["n"] + 2 * j + 2 - N_ADA + PARTS)
                        w = 512 if j < 6 else PROJ_W - 6 * 512
                        act.activation(proj[:, :, 512 * j:512 * j + w], acc[:, 2 * (j % 2):2 * (j % 2) + 2, 0:w],
                                       ACT.Copy).then_inc(ev_ready, 1)

                    for j in range(blocks):
                        if j:
                            hi(b["n"] + 2 * j)
                            hi(b["n"] + 2 * j + 1)
                            evac(j - 1)
                    evac(blocks - 1)
                    ahead(b["n"] + 2 * blocks)
                elif kind == "soft":
                    soft(b, 16 if step[1] == "band" else 8)
                elif kind == "diff":
                    soft(b, 16)
                elif kind == "stick":
                    def soften(a):
                        act.wait_ge(s_free, b["sc"] + a + 1)
                        s = a % 2
                        own(act.activation(mixp_of(a), prob[:, s, :], ACT.Abs))
                        own(act.activation(mixp_of(a), mixp_of(a), ACT.Exp, scale=-1.0))
                        act.activation(mixp_of(a), mixp_of(a), ACT.Ln, bias=1.0).then_inc(soft_ready, 1)

                    def mixp_of(a):
                        return tok[:, a % 2, 0:384]

                    def weigh(a):
                        act.wait_ge(arg_ready, b["st"] + a + 1)
                        if a >= 2:
                            act.wait_ge(o_full, b["ov"] + a - 1)
                        act.activation(probT[:, a % 2, :], prob[:, a % 2, :], ACT.Exp).then_inc(p_ready, 1)

                    soften(0)
                    for a in range(NH):
                        if a + 1 < NH:
                            soften(a + 1)
                        weigh(a)
                elif kind == "mla_norm":
                    act.wait_ge(ev_ready, b["ev"])
                    c0 = 6 * 512
                    act.wait_ge(o_full, b["ov"])
                    squares(b, [(proj[:, t, c0 + o:c0 + o + w], w) for o, w in ((0, QL), (QL, KVL)) for t in range(NT)])
                elif kind == "mla_T":
                    take_hi(b, 2, yT_hi, False, (512, 256))
                elif kind == "mla_up":
                    n = b["n"]
                    q_out = acc[:].rearrange("p (t a) c -> p t (a c)", t=NT)
                    act.wait_ge(pe_used, n + 1 - N_ADA + PARTS)
                    act.activation(proj[:, :, MQ:MQ + NH * QK_C], q_out[:, :, 0:NH * QK_C], ACT.Copy).then_inc(ev_ready, 1)
                    act.wait_ge(pe_used, n + 2 - N_ADA + PARTS)
                    for t in range(NT):
                        kv = q_out[:, t, :].rearrange("p (h e) -> p h e", h=NH)
                        act.activation(proj[:, t, MK:MK + 768].rearrange("p (h e) -> p h e", h=NH)[:, :, 0:NOPE],
                                       kv[:, :, 0:NOPE], ACT.Copy)
                        for h in (0, 4):
                            v = proj[:, t, mla_value_col(h):mla_value_col(h) + 4 * HD]
                            ins = act.activation(v.rearrange("p (h e) -> p h e", h=4), kv[:, h:h + 4, NOPE:128], ACT.Copy)
                    ins.then_inc(ev_ready, 1)
                    ahead(n + 2)
                elif kind == "merge":
                    l = step[1]

                    def load_bias(j):
                        if j >= 2:
                            act.wait_ge(z_ready, b["mg"] + j - 1)
                        c = 512 * j
                        act.dma_start(tf[:, j % 2, :], bgate_in[l, c:c + 512].partition_broadcast(P)).then_inc(
                            bg_in[j % 2], 16)

                    act.wait_ge(tr_free, b["u"] + 2)
                    load_bias(0)
                    load_bias(1)
                    def sigmoid(j):
                        act.wait_ge(z_ready, b["mg"] + j + 1)
                        flat = pair[:].rearrange("p a t c -> p (a t c)")
                        act.activation(flat, flat, ACT.Sigmoid).then_inc(e_ready, 1)
                        if j + 2 < 6:
                            load_bias(j + 2)

                    for j in range(6):
                        n = b["n"] + 3 * j
                        if j:
                            hi(n)
                            sigmoid(j - 1)
                            hi(n + 1)
                        hi(n + 2)
                        if j % 2 == 0:
                            for r in range(2):
                                u = b["u"] + j + r
                                act.wait_ge(tr_full, u + 1)
                                d = yT_hi[:, 2 * r:2 * r + 2, :].rearrange("p a s -> p (a s)")
                                act.activation(d, tr[:, u % 2, :], ACT.Copy).then_inc(th_ready, 1)
                    ahead(b["n"] + 18)
                    sigmoid(5)
                elif kind == "backT":
                    take_hi(b, 4, hT_hi, step[1] != "subln")
                elif kind == "out":
                    for c in range(2, 4):
                        hi(b["n"] + c)
                    ahead(b["n"] + 4)
                elif kind == "head_norm":
                    act.wait_ge(ev_ready, b["ev"])
                    for t in range(NT):
                        if t:
                            act.wait_ge(sq_used, b["hn"] + t)
                        act.activation(tok[:].rearrange("p a c -> p (a c)"), proj[:, t, 0:2048], ACT.Square,
                                       scale=HD ** -0.5).then_inc(sq_ready, 1)
                elif kind == "out_norm":
                    act.wait_ge(o_free, b["ov"])
                    act.activation(tok[:], proj[:, :, 0:D], ACT.Square, scale=128 ** -0.5).then_inc(sq_ready, 1)
                elif kind == "route":
                    act.wait_ge(tr_full, b["u"] + 1)
                    act.activation(rt[:, 0, :], tr[:, b["u"] % 2, 0:NT * EXP], ACT.Exp, scale=-1.0).then_inc(th_ready, 1)

        @block.vector
        def _(dve):
            ups = 0
            turn, per_turn = 0, 0

            def own(ins):
                nonlocal ups
                ups += 1
                ins.then_inc(dve_up, 1)
                dve.wait_ge(dve_up, ups + per_turn * turn)

            def lo(n, i=0, rounds=1):
                dve.wait_ge(hi_ready, n - N_ADA + 1 + STAGES * rounds * i)
                dve.tensor_tensor(w_lo[:, n % PARTS, :], stage[:, n % STAGES, :], w_hi[:, n % PARTS, :].bitcast(F32),
                                  ALU.subtract).then_inc(chunk_ready, 1)

            def ahead(n):
                if n < n_chunks:
                    lo(n)
                    lo(n + 1)

            def flat(ap):
                return ap.rearrange("p a b -> p (a b)")

            def take_lo(b, rounds, dst_hi, dst_lo, cols=None, width=(512, 512, 512, 512)):
                def rest(r):
                    dve.wait_ge(th_ready, b["th"] + r + 1)
                    w = width[r]
                    src = tf[:, (b["tf"] + r) % 2, 0:w] if cols else tr[:, (b["u"] + r) % 2, 0:w]
                    dve.tensor_tensor(flat(dst_lo[:, 2 * r:2 * r + w // S, :]), src,
                                      flat(dst_hi[:, 2 * r:2 * r + w // S, :]).bitcast(F32),
                                      ALU.subtract).then_inc(tr_free, 1)

                for r in range(rounds):
                    if cols:
                        dve.wait_ge(tr_full, b["u"] + r + 1)
                        for a in range(width[r] // S):
                            c0, c1, op1 = cols(2 * r + a)
                            ins = dve.tensor_scalar(tf[:, (b["tf"] + r) % 2, a * S:(a + 1) * S],
                                                    tr[:, (b["u"] + r) % 2, a * S:(a + 1) * S], c0, c1, ALU.mult, op1)
                        ins.then_inc(tf_ready, 1)
                        if r:
                            rest(r - 1)
                    else:
                        rest(r)
                if cols:
                    rest(rounds - 1)

            def gate_row(b, k, u, between=None):
                dve.wait_ge(tr_free, u + 2)
                for r in range(2):
                    for j in range(4):
                        ins = dve.tensor_scalar(tf[:, (b["tf"] + r) % 2, j * P:(j + 1) * P], ident,
                                                mod[:, 3 * k + 2, 4 * r + j:4 * r + j + 1], None, ALU.mult)
                    ins.then_inc(tf_ready, 1)
                for r in range(2):
                    dve.wait_ge(tr_full, u + r + 1)
                    dve.tensor_copy(tok[:, 0, r * 512:(r + 1) * 512], tr[:, (u + r) % 2, :]).then_inc(tr_free, 1)

            dve.nop().then_inc(tr_free, 2)
            dve.nop().then_inc(ada_out, 1)
            dve.wait_ge(ld, 16 * 8)
            dve.wait_ge(c_exp, 1)
            own(dve.tensor_scalar(c_tmp[:], c_tmp[:], 1.0, None, ALU.add))
            own(dve.reciprocal(c_tmp[:], c_tmp[:]))
            own(dve.tensor_tensor(c_act[:], c_tmp[:], vec[:, 0:2 * KT], ALU.mult))
            dve.wait_ge(rwhi_ready, 1)
            dve.tensor_tensor(rw_lo[:], rw[:], rw_hi[:].bitcast(F32), ALU.subtract).then_inc(rw_ready, 1)
            lam4 = lam[:].rearrange("p (a b e) -> p a b e", a=2, b=2)
            dots = rope_t[:, 0, :].rearrange("p (a e) -> p a e", a=2)
            own(dve.tensor_tensor(dots, lam4[:, :, 0, :], lam4[:, :, 1, :], ALU.mult))
            dve.tensor_reduce(lam_s[:, 0:2], dots, AX, ALU.add).then_inc(lam_dot, 1)
            dve.wait_ge(lam_exp, 1)
            own(dve.tensor_tensor(lam_s[:, 0:1], lam_s[:, 3:4], lam_s[:, 2:3], ALU.subtract))
            own(dve.tensor_scalar(lam_s[:, 0:1], lam_s[:, 0:1], -0.2, None, ALU.add))

            first_turns = DEPTH * 9 // 6
            for lo_turn, hi_turn, c0 in ((0, first_turns, 0), (first_turns, NVEC // 6, KT)):
                with dve.Fori(lo_turn, hi_turn) as i:
                    base = ups
                    turn, per_turn = i - lo_turn, 24
                    for q in range(6):
                        dve.wait_ge(ada_sum, 6 * i + q + 1)
                        for kp in range(4):
                            n = 4 * q + kp
                            s = n % STAGES
                            dve.wait_ge(landed[s], 16 * (n // STAGES + 1) + 64 * i)
                            for j in range(2):
                                w = stage[:, s, j * D:(j + 1) * D]
                                c = c_act[:, c0 + 2 * kp + j:c0 + 2 * kp + j + 1]
                                if kp == 0 and j == 0:
                                    ins = dve.tensor_scalar(tok[:, q % 2, :], w, c, None, ALU.mult)
                                else:
                                    ins = dve.scalar_tensor_tensor(tok[:, q % 2, :], w, c, tok[:, q % 2, :],
                                                                   ALU.mult, ALU.add)
                                if j == 0:
                                    own(ins)
                                else:
                                    ins.then_inc(chunk_ready, 1)
                                    dve.wait_ge(chunk_ready, 24 * i + n + 1)
                    dve.wait_ge(ada_sum, 6 * i + 8)
                    vecs = flat(mod[:, bass.ds(6 * i, 6), :])
                    bias = vec[:, bass.ds(VEC["ada_b"][0] + 48 * i, 48)]
                    dve.tensor_tensor(vecs, acc[:, 0, 0:48], bias, ALU.add).then_inc(ada_out, 1)
                    assert ups == base + 24
                ups += 24 * (hi_turn - lo_turn - 1)
                turn, per_turn = 0, 0
            dve.wait_ge(ada_out, 1 + NVEC // 6)
            mods = mod[:].rearrange("p (k v) c -> p k v c", v=3)
            pre = vec[:, VEC["pre"][0]:VEC["pre"][1]].rearrange("p (k c) -> p k c", c=KT)
            post = vec[:, VEC["post"][0]:VEC["post"][1]].rearrange("p (k c) -> p k c", c=KT)
            dve.scalar_tensor_tensor(mods[:, :, 1, :], mods[:, :, 1, :], 1.0, pre, ALU.add, ALU.mult)
            own(dve.scalar_tensor_tensor(mods[:, 0:6, 2, :], mods[:, 0:6, 2, :], 1.0, post, ALU.add, ALU.mult))
            for k in (0, 2, 3, 5):
                ins = dve.tensor_scalar(mods[:, k, 2, :], mods[:, k, 2, :], 0.5, None, ALU.mult)
            ins.then_inc(mod_ready, 1)
            dve.wait_ge(mod_ready, 1)
            ahead(N_ADA)

            def ffn(b, k, nb, moe):
                peeled, turns = block_order(nb)
                n0, g0, th0, u0 = b["n"], b["hid"], b["th"], b["u"] + 2
                sg, hid = pair[:, 0], pair[:, 1]

                def silu(g, i=0, expert=None):
                    dve.wait_ge(sg_ready, g0 + g + 1 + 2 * i)
                    if moe:
                        e = g // 2 if isinstance(i, int) else i + g // 2
                        for t in range(NT):
                            w = gates[:, t, e:e + 1] if isinstance(i, int) else gates[:, t, bass.ds(e, 1)]
                            ins = dve.scalar_tensor_tensor(hid[:, t, :], sg[:, t, :], w, gu[:, t, BLK:2 * BLK],
                                                           ALU.mult, ALU.mult)
                    else:
                        ins = dve.tensor_tensor(hid, sg, gu[:, :, BLK:2 * BLK], ALU.mult)
                    ins.then_inc(hid_ready, 1)

                def turn_lo(g, i=0):
                    dve.wait_ge(th_ready, th0 + g + 1 + 2 * i)
                    dve.tensor_tensor(hid_lo, tr[:, (u0 + g) % 2, :], hid_hi.bitcast(F32),
                                      ALU.subtract).then_inc(tr_free, 1)

                def block_(g, i=0):
                    lo(n0 + 3 * g - 1, i)
                    silu(g - 1, i)
                    lo(n0 + 3 * g, i)
                    lo(n0 + 3 * g + 1, i)
                    turn_lo(g - 1, i)

                gate_row(b, k, b["u"])
                for g in range(1, 1 + peeled):
                    block_(g)
                with dve.Fori(0, turns) as i:
                    block_(1 + peeled, i)
                    block_(2 + peeled, i)
                silu(nb - 1)
                lo(n0 + 3 * nb - 1)
                turn_lo(nb - 1)
                ahead(n0 + 3 * nb)

            def moe(b, k, l):
                n0, g0, th0 = b["n"], b["hid"], b["th"]
                u0 = b["u"] + 2 + 8

                def select(e, i=0):
                    at = slice(e, e + 1) if isinstance(i, int) else bass.ds(2 * i + e, 1)
                    for t in range(NT):
                        dve.tensor_scalar(pick[:, e % 2, t, :], cst("slots"), rank[:, t, at], None, ALU.is_equal)
                        ins = dve.tensor_scalar(pickg[:, e % 2, t, :], cst("slots"), rank[:, t, at], gates[:, t, at],
                                                ALU.is_equal, ALU.mult)
                    ins.then_inc(pick_ready, 1)

                def th_at(g=None, e=None):
                    if e is not None:
                        return th0 if e == 0 else th0 + 4 + 1 + 6 * (e - 1)
                    if g == 0:
                        return th0 + 4
                    if g >= MOE_BLOCKS - 3:
                        return th0 + 9 + 6 * (EXP - 2) + g - (MOE_BLOCKS - 3)
                    return th0 + 9 + 6 * ((g + 1) // 2 - 1) + (g + 1) % 2

                def gather_lo(e, i=0):
                    u = moe_gather_at(u0, e)
                    for r in range(4):
                        dve.wait_ge(th_ready, th_at(e=e) + r + 1 + 12 * i)
                        dst = hT_lo[:, 2 * r:2 * r + 2, (e % 2) * P:(e % 2 + 1) * P]
                        dve.tensor_copy(dst, tr[:, (u + r) % 2, 2 * P:4 * P].rearrange("p (k s) -> p k s", k=2)
                                        ).then_inc(tr_free, 1)
                    dve.wait_ge(tr_full, u + 5 + 14 * i)
                    dve.tensor_copy(pickT[:, e % 2, :], tr[:, (u + 4) % 2, 0:S]).then_inc(tr_free, 1)

                def hidden(g, i=0):
                    dve.wait_ge(sg_ready, g0 + g + 1 + 4 * i)
                    dve.tensor_tensor(pair[:, 1, g % 2, :], pair[:, 0, g % 2, :], gu[:, g % 2, BLK:2 * BLK],
                                      ALU.mult).then_inc(hid_ready, 1)

                def turn_lo(g, i=0):
                    dve.wait_ge(th_ready, th_at(g=g) + 1 + 12 * i)
                    dve.tensor_tensor(hid_lo, tr[:, moe_scatter_at(u0, g) % 2, :], hid_hi.bitcast(F32),
                                      ALU.subtract).then_inc(tr_free, 1)

                def expert(e, i=0):
                    for g in (2 * e, 2 * e + 1):
                        if g:
                            lo(n0 + 3 * g - 1, i, 2)
                            hidden(g - 1, i)
                            lo(n0 + 3 * g, i, 2)
                            if g % 2 and not (isinstance(i, int) and e == EXP - 1):
                                select(e + 1, i)
                            lo(n0 + 3 * g + 1, i, 2)
                            turn_lo(g - 1, i)
                    if not (isinstance(i, int) and e == EXP - 1):
                        gather_lo(e + 1, i)

                gate_row(b, k, b["u"])
                for r in range(8):
                    part, t, half = r // 4, r // 2 % 2, r % 2
                    u = b["u"] + 2 + r
                    dve.wait_ge(tr_full, u + 1)
                    dve.tensor_copy((h_hi, h_lo)[part][:, t, half * 512:(half + 1) * 512],
                                    tr[:, u % 2, :]).then_inc(tr_free, 1)
                select(0)
                gather_lo(0)
                expert(0)
                with dve.Fori(0, (EXP - 2) // 2) as i:
                    expert(1, i)
                    expert(2, i)
                expert(EXP - 1)
                hidden(MOE_BLOCKS - 1)
                lo(n0 + 3 * MOE_BLOCKS - 1)
                turn_lo(MOE_BLOCKS - 1)
                ahead(n0 + 3 * MOE_BLOCKS)

            def soft_max_in(b, a, mask, scale):
                s = a % 2
                dve.wait_ge(s_full, b["sc"] + a + 1)
                dve.scalar_tensor_tensor(prob[:, s, :], gu[:, s, 0:384], scale, cst(mask),
                                         ALU.mult, ALU.add).then_inc(s_free, 1)
                dve.wait_ge(s_free, b["sc"] + a + 1)
                dve.tensor_reduce(nmax[:, s, 0:1], prob[:, s, 0:128], AX, ALU.max, negate=True)
                dve.tensor_reduce(nmax[:, s, 1:2], prob[:, s, 128:384], AX, ALU.max, negate=True).then_inc(m_ready, 1)

            def turn_prob(b, h):
                dve.wait_ge(tr_full, b["u"] + h + 1)
                if h >= 2:
                    dve.wait_ge(o_full, b["ov"] + h - 1)
                dve.tensor_copy(probT[:, h % 2, :], tr[:, (b["u"] + h) % 2, 0:384]).then_inc(tr_free, 1)

            def rotate(x1, x2, cos, sin, w, o1=None, o2=None):
                shape = x1.shape[1:]
                def tmp(i):
                    v = rope_t[:, i, 0:w]
                    return v.rearrange("p (h f) -> p h f", h=shape[0]) if len(shape) == 2 else v
                dve.tensor_tensor(tmp(0), x1, cos, ALU.mult)
                dve.tensor_tensor(tmp(1), x2, sin, ALU.mult)
                dve.tensor_tensor(tmp(2), x1, sin, ALU.mult)
                own(dve.tensor_tensor(tmp(3), x2, cos, ALU.mult))
                dve.tensor_tensor(x1 if o1 is None else o1, tmp(0), tmp(1), ALU.subtract)
                own(dve.tensor_tensor(x2 if o2 is None else o2, tmp(2), tmp(3), ALU.add))

            for step, b in plan:
                kind = step[0]
                if kind == "norm":
                    k = step[1]
                    dve.wait_ge(rs_done, b["req"] + 1)
                    for t in range(NT):
                        ins = dve.tensor_scalar(tok[:, t, :], x[:, t, :], rs[:, t:t + 1], None, ALU.mult)
                    ins.then_inc(src_ready, 1)
                    take_lo(b, 4, hT_hi, hT_lo,
                            lambda c: (mod[:, 3 * k + 1, c:c + 1], mod[:, 3 * k, c:c + 1], ALU.add))
                elif kind == "ffn" and not step[3]:
                    ffn(b, step[1], step[2], False)
                elif kind == "ffn":
                    l = (step[1] - 3 * DEPTH) // 2
                    dve.wait_ge(count_ready, l + 1)
                    most = dve.value_load(fullest_i[0:1, 0:1], min_val=0, max_val=S)
                    with dve.If(most <= P):
                        moe(b, step[1], l)
                    with dve.Else():
                        ffn(b, step[1], step[2], True)
                        dve.nop().then_inc(tr_free, MOE_TURNS - MOE_BLOCKS - 2)
                        dve.nop().then_inc(pick_ready, EXP)
                elif kind == "resid":
                    k = step[1]
                    dve.wait_ge(tr_free, b["u"] + 2)
                    if k < 6:
                        dve.wait_ge(rs_done, b["req"] + 1)
                    else:
                        dve.wait_ge(pe_used, b["n"] - N_ADA + PARTS)
                    for t in range(NT):
                        a = flat(acc[:, 2 * t:2 * t + 2, :])
                        if k < 6:
                            own(dve.scalar_tensor_tensor(tok[:, 1, :], a, rs[:, t:t + 1], tok[:, 0, :],
                                                         ALU.mult, ALU.mult))
                        else:
                            own(dve.tensor_tensor(tok[:, 1, :], a, tok[:, 0, :], ALU.mult))
                        ins = dve.tensor_tensor(x[:, t, :], x[:, t, :], tok[:, 1, :], ALU.add)
                        if t < NT - 1:
                            own(ins)
                    ins.then_inc(x_ready, 1)
                elif kind == "proj":
                    for j in range(2, 2 * step[1]):
                        lo(b["n"] + j)
                elif kind == "rope_p":
                    dve.wait_ge(ev_ready, b["ev"])
                    half = ROT // 2
                    for t in range(NT):
                        heads = proj[:, t, 0:1024].rearrange("p (h e) -> p h e", e=HD)
                        c = CONST["cos_p"][0] + t * half
                        cos = const[:, c:c + half].unsqueeze(1).to_broadcast([P, 16, half])
                        c = CONST["sin_p"][0] + t * half
                        sin = const[:, c:c + half].unsqueeze(1).to_broadcast([P, 16, half])
                        rotate(heads[:, :, 0:half], heads[:, :, half:ROT], cos, sin, 16 * half)
                    dve.nop().then_inc(src_ready, 1)
                elif kind == "rope_m":
                    dve.wait_ge(ev_ready, b["ev"])
                    half = ROPE // 2
                    for t in range(NT):
                        c, s_ = CONST["cos_m"][0] + t * half, CONST["sin_m"][0] + t * half
                        kr = proj[:, t, PROJ_W - ROPE:PROJ_W]
                        rotate(kr[:, 0:half], kr[:, half:ROPE], const[:, c:c + half], const[:, s_:s_ + half], half)
                        cos = const[:, c:c + half].unsqueeze(1).to_broadcast([P, NH, half])
                        sin = const[:, s_:s_ + half].unsqueeze(1).to_broadcast([P, NH, half])
                        q = proj[:, t, MQ:MQ + 768].rearrange("p (h e) -> p h e", h=NH)
                        rotate(q[:, :, NOPE:NOPE + half], q[:, :, NOPE + half:QK_C], cos, sin, NH * half)
                        km = proj[:, t, MK:MK + 768].rearrange("p (h e) -> p h e", h=NH)
                        own(dve.tensor_copy(km[:, :, NOPE:QK_C], kr.unsqueeze(1).to_broadcast([P, NH, ROPE])))
                    dve.nop().then_inc(src_ready, 1)
                elif kind == "qkT":
                    rounds = 4 if step[1] == "pairs" else 8
                    rows = QK_C if step[1] == "mla" else P
                    for r in range(rounds):
                        u = b["u"] + r
                        dve.wait_ge(tr_full, u + 1)
                        dst, src = flat(qk[0:rows, 2 * r:2 * r + 2, :]), tr[0:rows, u % 2, :]
                        if step[1] != "wide":
                            dve.tensor_copy(dst, src).then_inc(tr_free, 1)
                        elif r < 4:
                            dve.tensor_scalar(dst, src, col(step[4] + "_q", 0), HD ** -0.5,
                                              ALU.mult, ALU.mult).then_inc(tr_free, 1)
                        else:
                            dve.tensor_scalar(dst, src, col(step[4] + "_k", 0), None, ALU.mult).then_inc(tr_free, 1)
                    if step[2] != 1536:
                        ahead(b["n"])
                elif kind == "soft":
                    which = step[1]
                    heads, mask, scale, out_col = {
                        "moba": (NH, "causal", HD ** -0.5, Y_COL[0]), "mla": (NH, "causal", QK_C ** -0.5, Y_COL[2]),
                        "band": (16, "chunked", 1.0, 0)}[which]
                    inv_at = {}

                    def emit_out(h):
                        s = h % 2
                        dve.wait_ge(o_full, b["ov"] + h + 1)
                        dve.wait_ge(dve_up, inv_at[h])
                        for q in range(NT):
                            ins = dve.tensor_scalar(proj[:, q, out_col + h * HD:out_col + (h + 1) * HD],
                                                    acc[:, s, q * P:q * P + HD], rinv[:, s, q:q + 1], None, ALU.mult)
                        ins.then_inc(o_free, 1)

                    soft_max_in(b, 0, mask, scale)
                    for h in range(heads):
                        if h + 1 < heads:
                            soft_max_in(b, h + 1, mask, scale)
                        turn_prob(b, h)
                        ups += 1
                        inv_at[h] = ups
                        if h >= 2:
                            dve.wait_ge(o_free, b["ov"] + h - 1)
                        dve.reciprocal(rinv[:, h % 2, :], rsum[:, h % 2, :]).then_inc(dve_up, 1)
                        if h:
                            emit_out(h - 1)
                    emit_out(heads - 1)
                elif kind == "diff":
                    def combine(h):
                        dve.wait_ge(p_ready, b["pr"] + 2 * h + 2)
                        own(dve.reciprocal(rinv[:], rsum[:]))
                        own(dve.tensor_scalar(rinv[:, 1, :], rinv[:, 1, :], lam_s[:, 0:1], None, ALU.mult))
                        segs = ((0, 128), (128, 384))
                        for q, (lo_, hi_) in enumerate(segs):
                            ins = dve.tensor_scalar(mixp[:, lo_:hi_], prob[:, 1, lo_:hi_], rinv[:, 1, q:q + 1], None,
                                                    ALU.mult)
                        own(ins)
                        for q, (lo_, hi_) in enumerate(segs):
                            ins = dve.scalar_tensor_tensor(mixp[:, lo_:hi_], prob[:, 0, lo_:hi_], rinv[:, 0, q:q + 1],
                                                           mixp[:, lo_:hi_], ALU.mult, ALU.add)
                        ins.then_inc(a_ready, 1)

                    def emit_diff(h):
                        dve.wait_ge(o_full, b["ov"] + h + 1)
                        o = acc[:, h % 2, 0:256].rearrange("p (q e) -> p q e", q=NT)
                        dve.tensor_copy(proj[:, :, h * 128:(h + 1) * 128], o).then_inc(o_free, 1)

                    soft_max_in(b, 0, "chunked", 1.0)
                    soft_max_in(b, 1, "chunked", 1.0)
                    for h in range(8):
                        combine(h)
                        if h < 7:
                            dve.wait_ge(a_ready, h + 1)
                            soft_max_in(b, 2 * h + 2, "chunked", 1.0)
                            soft_max_in(b, 2 * h + 3, "chunked", 1.0)
                        turn_prob(b, h)
                        if h:
                            emit_diff(h - 1)
                    emit_diff(7)
                elif kind == "stick":
                    def take_z(a):
                        s = a % 2
                        dve.wait_ge(s_full, b["sc"] + a + 1)
                        if a >= 2:
                            dve.wait_ge(p_ready, b["pr"] + a - 1)
                        dve.scalar_tensor_tensor(prob[:, s, :], gu[:, s, 0:384], HD ** -0.5, cst("strict"),
                                                 ALU.mult, ALU.add).then_inc(s_free, 1)

                    def emit_stick(a):
                        dve.wait_ge(o_full, b["ov"] + a + 1)
                        o = acc[:, a % 2, 0:256].rearrange("p (q e) -> p q e", q=NT)[:, :, 0:HD]
                        dve.tensor_copy(proj[:, :, Y_COL[1] + a * HD:Y_COL[1] + (a + 1) * HD], o).then_inc(o_free, 1)

                    take_z(0)
                    for a in range(NH):
                        if a + 1 < NH:
                            take_z(a + 1)
                        s = a % 2
                        dve.wait_ge(soft_ready, b["st"] + a + 1)
                        dve.scalar_tensor_tensor(tok[:, s, 0:384], prob[:, s, :], 0.0, tok[:, s, 0:384],
                                                 ALU.max, ALU.add).then_inc(sp_ready, 1)
                        dve.wait_ge(c_full, b["st"] + a + 1)
                        dve.tensor_tensor(prob[:, s, :], prob[:, s, :], acc[:, 2 + s, 0:384],
                                          ALU.subtract).then_inc(arg_ready, 1)
                        if a:
                            emit_stick(a - 1)
                    emit_stick(NH - 1)
                elif kind == "mla_norm":
                    dve.wait_ge(rs_done, b["req"] + 1)
                    c0 = 6 * 512
                    for i, (o, w) in enumerate(((0, QL), (QL, KVL))):
                        for t in range(NT):
                            v = proj[:, t, c0 + o:c0 + o + w]
                            ins = dve.tensor_scalar(v, v, rs[:, 2 * i + t:2 * i + t + 1], None, ALU.mult)
                    ins.then_inc(src_ready, 1)
                elif kind == "mla_T":
                    l = step[1]
                    take_lo(b, 2, yT_hi, yT_lo,
                            lambda c: (col("q_norm", 2 * l + c) if c < 2 else col("kv_norm", l), None, ALU.bypass),
                            (512, 256))
                elif kind == "merge":
                    l = step[1]
                    flat4 = pair[:].rearrange("p a t c -> p a (t c)")

                    def finish(j):
                        n = b["n"] + 3 * j
                        dve.wait_ge(e_ready, b["mg"] + j + 1)
                        dve.wait_ge(pe_used, n + 3 - N_ADA + PARTS)
                        half = tok[:, :, 512 * (j % 2):512 * (j % 2) + 512]
                        br = acc[:, 2 * (j % 2):2 * (j % 2) + 2, :]
                        if j < 2:
                            dve.tensor_tensor(half, flat4, br, ALU.mult).then_inc(mg_ready, 1)
                        else:
                            own(dve.tensor_tensor(flat4, flat4, br, ALU.mult))
                            dve.tensor_tensor(half, half, flat4, ALU.add).then_inc(mg_ready, 1)

                    for j in range(6):
                        n = b["n"] + 3 * j
                        if j:
                            lo(n)
                            finish(j - 1)
                            lo(n + 1)
                        lo(n + 2)
                        if j % 2 == 0:
                            for r in range(2):
                                dve.wait_ge(th_ready, b["th"] + j + r + 1)
                                dve.tensor_tensor(flat(yT_lo[:, 2 * r:2 * r + 2, :]), tr[:, (b["u"] + j + r) % 2, :],
                                                  flat(yT_hi[:, 2 * r:2 * r + 2, :]).bitcast(F32),
                                                  ALU.subtract).then_inc(tr_free, 1)
                        dve.wait_ge(pe_used, n + 2 - N_ADA + PARTS)
                        dve.wait_ge(bg_in[j % 2], 16 * (3 * l + j // 2 + 1))
                        bias = tf[:, j % 2, :].unsqueeze(1).to_broadcast([P, 2, 512])
                        if j:
                            dve.wait_ge(mg_ready, b["mg"] + j)
                        dve.tensor_tensor(flat4, gu[:], bias, ALU.add).then_inc(z_ready, 1)
                    ahead(b["n"] + 18)
                    finish(5)
                elif kind == "backT":
                    if step[1] == "subln":
                        take_lo(b, 4, hT_hi, hT_lo, lambda c: (col("subln", 0), 0.8, ALU.mult))
                    else:
                        take_lo(b, 4, hT_hi, hT_lo)
                elif kind == "out":
                    gate_row(b, step[1], b["u"])
                    lo(b["n"] + 2)
                    lo(b["n"] + 3)
                    ahead(b["n"] + 4)
                elif kind == "head_norm":
                    for t in range(NT):
                        dve.wait_ge(sq_ready, b["sq"] + t + 1)
                        sq = flat(tok[:]).rearrange("p (h e) -> p h e", e=HD)
                        ins = dve.tensor_reduce(ss[:, 32 * t:32 * t + 32], sq, AX, ALU.add)
                        ins.then_inc(sq_used if t < NT - 1 else rs_req, 1)
                    dve.wait_ge(rs_done, b["req"] + 1)
                    for t in range(NT):
                        v = proj[:, t, 0:2048].rearrange("p (h e) -> p h e", e=HD)
                        f = rs[:, 32 * t:32 * t + 32].unsqueeze(2).to_broadcast([P, 32, HD])
                        ins = dve.tensor_tensor(v, v, f, ALU.mult)
                    ins.then_inc(src_ready, 1)
                elif kind == "out_norm":
                    dve.wait_ge(sq_ready, b["sq"] + 1)
                    dve.tensor_reduce(ss[:, 0:16], flat(tok[:]).rearrange("p (h e) -> p h e", e=128), AX,
                                      ALU.add).then_inc(rs_req, 1)
                    dve.wait_ge(rs_done, b["req"] + 1)
                    for t in range(NT):
                        v = proj[:, t, 0:D].rearrange("p (h e) -> p h e", e=128)
                        f = rs[:, 8 * t:8 * t + 8].unsqueeze(2).to_broadcast([P, 8, 128])
                        ins = dve.tensor_tensor(v, v, f, ALU.mult)
                    ins.then_inc(src_ready, 1)
                elif kind == "route":
                    R = NT * EXP
                    sc, sel, key, oh1, oh2, cmp_ = (rt[:, i, 0:R] for i in (0, 1, 2, 3, 4, 5))
                    small = rt[:, 6, :]
                    pairs = rt[:, 7, :]

                    def by_t(v, w=EXP):
                        return v.rearrange("p (t e) -> p t e", t=NT)

                    def over(v, w):
                        return v.unsqueeze(2).to_broadcast([P, v.shape[1], w])

                    dve.wait_ge(th_ready, b["th"] + 1)
                    dve.tensor_scalar(sc, sc, 1.0, None, ALU.add).then_inc(tr_free, 1)
                    dve.wait_ge(tr_free, b["u"] + 1 + 2)
                    own(dve.reciprocal(sc, sc))
                    own(dve.tensor_tensor(by_t(sel), by_t(sc), rbias[:].unsqueeze(1).to_broadcast([P, NT, EXP]), ALU.add))
                    s4 = sel.rearrange("p (g e) -> p g e", e=4)
                    best, tmp3 = small[:, 0:8], pairs[:, 0:24].rearrange("p (g e) -> p g e", e=3)
                    tmp2 = key[:, 0:16].rearrange("p (g e) -> p g e", e=2)
                    dve.tensor_tensor(tmp3, s4[:, :, 0:3], s4[:, :, 1:4], ALU.add)
                    own(dve.tensor_tensor(tmp2, s4[:, :, 0:2], s4[:, :, 2:4], ALU.add))
                    dve.tensor_reduce(best, tmp3, AX, ALU.max)
                    own(dve.tensor_reduce(small[:, 8:16], tmp2, AX, ALU.max))
                    own(dve.tensor_tensor(best, best, small[:, 8:16], ALU.max))
                    last = small[:, 8:16].unsqueeze(2)
                    own(dve.tensor_tensor(last, s4[:, :, 0:1], s4[:, :, 3:4], ALU.add))
                    own(dve.tensor_tensor(best, best, small[:, 8:16], ALU.max))

                    def first_of_max(v, ranks, w, onehot, m):
                        v3 = v.rearrange("p (t e) -> p t e", t=NT)
                        k3 = key[:, 0:NT * w].rearrange("p (t e) -> p t e", t=NT)
                        o3 = onehot.rearrange("p (t e) -> p t e", t=NT)
                        own(dve.tensor_reduce(m, v3, AX, ALU.max))
                        own(dve.tensor_tensor(k3, v3, over(m, w), ALU.is_equal))
                        own(dve.tensor_tensor(key[:, 0:NT * w], key[:, 0:NT * w], ranks, ALU.mult))
                        own(dve.tensor_reduce(m, k3, AX, ALU.max))
                        own(dve.tensor_tensor(o3, k3, over(m, w), ALU.is_equal))

                    gm = small[:, 8:16]
                    first_of_max(best, cst("grank"), GROUPS, gm, small[:, 16:18])
                    s4m = cmp_.rearrange("p (g e) -> p g e", e=4)
                    own(dve.tensor_tensor(s4m, s4, over(gm, 4), ALU.mult))
                    own(dve.tensor_scalar(gm, gm, BIG, -BIG, ALU.mult, ALU.add))
                    own(dve.tensor_tensor(s4m, s4m, over(gm, 4), ALU.add))
                    first_of_max(cmp_, cst("rank"), EXP, oh1, small[:, 16:18])
                    own(dve.scalar_tensor_tensor(cmp_, oh1, -3 * BIG, cmp_, ALU.mult, ALU.add))
                    first_of_max(cmp_, cst("rank"), EXP, oh2, small[:, 16:18])
                    own(dve.tensor_tensor(oh1, oh1, oh2, ALU.add))
                    dve.nop().then_inc(sent_ready, 1)
                    own(dve.tensor_tensor(sc, sc, oh1, ALU.mult))
                    own(dve.tensor_reduce(small[:, 16:18], by_t(sc), AX, ALU.add))
                    own(dve.reciprocal(small[:, 16:18], small[:, 16:18]))
                    own(dve.tensor_tensor(gates[:], by_t(sc), over(small[:, 16:18], EXP), ALU.mult))
                    u = b["u"] + 1
                    dve.wait_ge(tr_full, u + 1)
                    rank_f = rank[:].rearrange("p t e -> p (t e)")
                    dve.tensor_reduce(fullest[:], tr[:, u % 2, R:R + EXP], AX, ALU.max)
                    own(dve.scalar_tensor_tensor(rank_f, tr[:, u % 2, 0:R], 1.0, oh1, ALU.add, ALU.mult))
                    dve.tensor_scalar(rank_f, rank_f, -1.0, None, ALU.add).then_inc(tr_free, 1)
                    dve.tensor_copy(fullest_i[:], fullest[:]).then_inc(count_ready, 1)

        @block.tensor
        def _(pe):
            def mm3(dst, l_hi, l_lo, r_hi, r_lo, start, stop):
                pe.matmul(dst, l_hi, r_hi, start=start, stop=False, skip_group_check=True)
                pe.matmul(dst, l_hi, r_lo, start=False, stop=False, skip_group_check=True)
                return pe.matmul(dst, l_lo, r_hi, start=False, stop=stop, skip_group_check=True)

            def chunk_wait(n, i=0, rounds=1):
                pe.wait_ge(chunk_ready, n + 1 + STAGES * rounds * i)

            def columns(n, dst, k0, kts, first, last, width=512, src=(hT_hi, hT_lo), i=0, pitch=512):
                chunk_wait(n, i)
                s = n % PARTS
                for t in range(NT):
                    for k in range(kts):
                        c = slice(k * pitch, k * pitch + width)
                        lhs = [v[:, k0 + k, t * P:(t + 1) * P] for v in src]
                        ins = mm3(dst(t), lhs[0], lhs[1], w_hi[:, s, c], w_lo[:, s, c], first and k == 0, last and k == kts - 1)
                ins.then_inc(pe_used, 1)

            def rows(n, lhs, first, last, i=0, rounds=1):
                chunk_wait(n, i, rounds)
                s = n % PARTS
                for k in range(2):
                    for t in range(NT):
                        l_hi, l_lo = lhs(k, t)
                        for h in range(2):
                            c = slice(k * D + h * 512, k * D + (h + 1) * 512)
                            ins = mm3(acc[:, 2 * t + h, :], l_hi, l_lo, w_hi[:, s, c], w_lo[:, s, c],
                                      first and k == 0, last and k == 1)
                ins.then_inc(pe_used, 1)

            def turn(u, srcs, i=0, per=0):
                pe.wait_ge(tr_free, u + 1 + per * i)
                for j, src in enumerate(srcs):
                    rows_ = src.shape[-1]
                    ins = pe.transpose(tr[0:rows_, u % 2, j * P:(j + 1) * P], src, ident)
                ins.then_inc(tr_full, 1)

            def gate_row(b, u):
                for r in range(2):
                    pe.wait_ge(tf_ready, b["tf"] + r + 1)
                    pe.wait_ge(tr_free, u + r + 1)
                    pe.matmul(tr[:, (u + r) % 2, :], ones, tf[:, (b["tf"] + r) % 2, :], start=True,
                              stop=True).then_inc(tr_full, 1)

            def ffn(b, nb):
                peeled, turns = block_order(nb)
                n0, u0, g0 = b["n"], b["u"] + 2, b["hid"]

                def up(n, half, g, i=0):
                    if half == 0:
                        pe.wait_ge(hid_ready, g0 + g + 2 * i)
                    columns(n, lambda t: gu[:, t, :], 4 * half, 4, half == 0, half == 1, i=i)

                def turn_hidden(g, i=0):
                    hid = pair[:, 1]
                    pe.wait_ge(hid_ready, g0 + g + 1 + 2 * i)
                    turn(u0 + g, [hid[:, t, k * P:(k + 1) * P] for k in range(2) for t in range(NT)], i, 2)

                def down(n, g, first=False, last=False, i=0):
                    pe.wait_ge(tr_free, u0 + g + 1 + 2 + 2 * i)
                    rows(n, lambda k, t: tuple(v[:, (2 * k + t) * P:(2 * k + t + 1) * P] for v in (hid_hi, hid_lo)),
                         first, last, i)

                def block_(g, i=0):
                    up(n0 + 3 * g - 1, 0, g, i)
                    turn_hidden(g - 1, i)
                    up(n0 + 3 * g, 1, g, i)
                    down(n0 + 3 * g + 1, g - 1, isinstance(i, int) and g == 1, False, i)

                pe.wait_ge(tr_free, b["u"] + 2)
                up(n0, 0, 0)
                up(n0 + 1, 1, 0)
                gate_row(b, b["u"])
                for g in range(1, 1 + peeled):
                    block_(g)
                with pe.Fori(0, turns) as i:
                    block_(1 + peeled, i)
                    block_(2 + peeled, i)
                turn_hidden(nb - 1)
                down(n0 + 3 * nb - 1, nb - 1, False, True)

            def moe(b, l):
                n0, g0 = b["n"], b["hid"]
                u0 = b["u"] + 2 + 8

                def gather(e, i=0):
                    u = moe_gather_at(u0, e)
                    pe.wait_ge(pick_ready, l * EXP + e + 1 + 2 * i)
                    for r in range(4):
                        pe.wait_ge(tr_free, u + r + 1 + 14 * i)
                        for part, h in enumerate((h_hi, h_lo)):
                            for k in range(2):
                                dst = tr[:, (u + r) % 2, (2 * part + k) * P:(2 * part + k + 1) * P]
                                for t in range(NT):
                                    ins = pe.matmul(dst, h[:, t, (2 * r + k) * P:(2 * r + k + 1) * P], pick[:, e % 2, t, :],
                                                    start=(t == 0), stop=(t == NT - 1), skip_group_check=True)
                        ins.then_inc(tr_full, 1)
                    turn(u + 4, [pickg[:, e % 2, t, :] for t in range(NT)], i, 14)

                def up(g, half, i=0):
                    e, n = g // 2, (n0 if g == 0 else n0 + 3 * g - 1) + half
                    if half == 0:
                        pe.wait_ge(tr_free, moe_gather_at(u0, e) + 4 + 1 + 2 + 14 * i)
                        if not isinstance(i, int) or g >= 2:
                            pe.wait_ge(hid_ready, g0 + g - 1 + 4 * i)
                    pe.wait_ge(chunk_ready, n + 1 + 12 * i)
                    slots = slice((e % 2) * P, (e % 2 + 1) * P)
                    for k in range(4):
                        c = slice(k * 512, (k + 1) * 512)
                        ins = mm3(gu[:, g % 2, :], hT_hi[:, 4 * half + k, slots], hT_lo[:, 4 * half + k, slots],
                                  w_hi[:, n % PARTS, c], w_lo[:, n % PARTS, c], half == 0 and k == 0, half == 1 and k == 3)
                    ins.then_inc(pe_used, 1)

                def scatter(g, i=0):
                    u = moe_scatter_at(u0, g)
                    pe.wait_ge(hid_ready, g0 + g + 1 + 4 * i)
                    pe.wait_ge(tr_free, u + 1 + 14 * i)
                    for k in range(2):
                        ins = pe.matmul(tr[:, u % 2, k * S:(k + 1) * S], pair[:, 1, g % 2, k * P:(k + 1) * P],
                                        pickT[:, (g // 2) % 2, :], start=True, stop=True)
                    ins.then_inc(tr_full, 1)

                def expert(e, i=0):
                    for g in (2 * e, 2 * e + 1):
                        up(g, 0, i)
                        if g:
                            scatter(g - 1, i)
                        up(g, 1, i)
                        if g % 2 and not (isinstance(i, int) and e == EXP - 1):
                            gather(e + 1, i)
                        if g:
                            down_after(g - 1, i)

                def down_after(g, i):
                    pe.wait_ge(tr_free, moe_scatter_at(u0, g) + 1 + 2 + 14 * i)
                    rows(n0 + 3 * g + 4, lambda k, t: tuple(v[:, (2 * k + t) * P:(2 * k + t + 1) * P] for v in (hid_hi, hid_lo)),
                         isinstance(i, int) and g == 0, False, i, 2)

                gate_row(b, b["u"])
                for r in range(8):
                    part, t, half = r // 4, r // 2 % 2, r % 2
                    src = (hT_hi, hT_lo)[part]
                    turn(b["u"] + 2 + r, [src[:, 4 * half + k, t * P:(t + 1) * P].bitcast(F32) for k in range(4)])
                gather(0)
                expert(0)
                with pe.Fori(0, (EXP - 2) // 2) as i:
                    expert(1, i)
                    expert(2, i)
                expert(EXP - 1)
                scatter(MOE_BLOCKS - 1)
                pe.wait_ge(tr_free, moe_scatter_at(u0, MOE_BLOCKS - 1) + 1 + 2)
                rows(n0 + 3 * MOE_BLOCKS - 1,
                     lambda k, t: tuple(v[:, (2 * k + t) * P:(2 * k + t + 1) * P] for v in (hid_hi, hid_lo)), False, True)

            def small_mm(dst, lhs, rhs, start=True, stop=True):
                return pe.matmul(dst, lhs, rhs, start=start, stop=stop, skip_group_check=True)

            def value_mm(b, h, pT, v, width):
                if h >= 2:
                    pe.wait_ge(o_free, b["ov"] + h - 1)
                o = acc[:, h % 2, :]
                small_mm(o[:, 0:width], pT[:, 0:128], v(0))
                small_mm(o[:, P:P + width], pT[:, 128:256], v(0), True, False)
                small_mm(o[:, P:P + width], pT[:, 256:384], v(1), False, True).then_inc(o_full, 1)

            pe.nop().then_inc(pe_used, PARTS)
            pe.nop().then_inc(ada_sum, 2)
            pe.wait_ge(ld, 16 * 8)
            pe.matmul(tr[0:8, 0, :], t5[:], t5hot, start=True, stop=True).then_inc(t5_mm, 1)
            with pe.Fori(0, NVEC // 6) as i:
                for q in range(6):
                    pe.wait_ge(chunk_ready, 24 * i + 4 * q + 4)
                    if q == 0:
                        pe.wait_ge(ada_out, i + 1)
                    for j in range(KT):
                        ins = pe.matmul(acc[:, 0, q * KT + j:q * KT + j + 1], tok[:, q % 2, j * P:(j + 1) * P],
                                        ones[:, 0:1], start=True, stop=True)
                    ins.then_inc(ada_sum, 1)
            pe.wait_ge(t5_sb, 1)

            for step, b in plan:
                kind = step[0]
                if kind == "norm":
                    pe.wait_ge(src_ready, b["src"] + 1)
                    for r in range(4):
                        turn(b["u"] + r, [tok[:, t, (2 * r + k) * P:(2 * r + k + 1) * P] for k in range(2) for t in range(NT)])
                elif kind == "ffn" and not step[3]:
                    ffn(b, step[2])
                elif kind == "ffn":
                    l = (step[1] - 3 * DEPTH) // 2
                    pe.wait_ge(count_ready, l + 1)
                    most = pe.value_load(fullest_i[0:1, 0:1], min_val=0, max_val=S)
                    with pe.If(most <= P):
                        moe(b, l)
                    with pe.Else():
                        ffn(b, step[2])
                        pe.nop().then_inc(tr_full, MOE_TURNS - MOE_BLOCKS - 2)
                elif kind == "proj":
                    pe.wait_ge(tr_free, b["u"] + 2)
                    for j in range(step[1]):
                        if j >= 2:
                            pe.wait_ge(ev_ready, b["ev"] + j - 1)
                        w = 512 if j < 6 else PROJ_W - 6 * 512
                        for half in range(2):
                            columns(b["n"] + 2 * j + half, lambda t: acc[:, 2 * (j % 2) + t, 0:w], 4 * half, 4,
                                    half == 0, half == 1, w)
                elif kind == "qkT":
                    pe.wait_ge(src_ready, b["src"])
                    pe.wait_ge(ev_ready, b["ev"])
                    _, how, q0, k0, _ = step
                    w = QK_C if how == "mla" else P
                    nq = 4 if how == "pairs" else 8
                    cols = [q0 + w * j for j in range(nq)] + [k0 + w * j for j in range(nq)]
                    for r in range(nq):
                        turn(b["u"] + r, [proj[:, t, c:c + w] for c in cols[2 * r:2 * r + 2] for t in range(NT)])
                elif kind in ("soft", "diff", "stick"):
                    which = step[1] if kind == "soft" else kind
                    heads = {"band": 16, "diff": 16}.get(which, NH)
                    nq = 4 if which in ("moba", "stick") else 8

                    def head(a):
                        if which == "mla":
                            return qk[0:QK_C, a, :], qk[0:QK_C, nq + a, :]
                        p = slice(HD * (a % 2), HD * (a % 2) + HD)
                        return qk[p, a // 2, :], qk[p, nq + a // 2, :]

                    def scores(a):
                        q, k = head(a)
                        s = gu[:, a % 2, :]
                        biased = which in ("band", "diff")
                        if a == 0:
                            pe.wait_ge(tr_free, b["u"] + 2)
                        if a >= 2:
                            pe.wait_ge(s_free, b["sc"] + a - 1)
                        if which == "band" or (which == "diff" and a % 2 == 0):
                            h = a if which == "band" else a // 2
                            before = (4 if which == "band" else 0) + h // 2 + 1
                            pe.wait_ge(bias_ld[h % 2], 32 * before)
                        for qt, (o, w) in enumerate(((0, 128), (128, 256))):
                            ins = small_mm(s[:, o:o + w], q[:, qt * P:(qt + 1) * P], k[:, 0:w], True, not biased)
                            if biased:
                                h = a if which == "band" else a // 2
                                ins = small_mm(s[:, o:o + w], flip, bias_in[:, h % 2, o:o + w], False, True)
                        ins.then_inc(s_full, 1)

                    def scores_T(a):
                        q, k = head(a)
                        s = gu[:, a % 2, :]
                        if a == 0:
                            pe.wait_ge(tr_free, b["u"] + 2)
                        if a >= 2:
                            pe.wait_ge(s_free, b["sc"] + a - 1)
                        small_mm(s[:, 0:256], k[:, 0:P], q[:, 0:S])
                        small_mm(s[:, 256:384], k[:, P:S], q[:, P:S]).then_inc(s_full, 1)

                    def values(c0, width):
                        return lambda h: (lambda kt: proj[:, kt, c0 + h * width:c0 + (h + 1) * width])

                    if which == "stick":
                        v = values(2560, HD)

                        def suffix(a):
                            sp = tok[:, a % 2, 0:384]
                            c = acc[:, 2 + a % 2, :]
                            pe.wait_ge(sp_ready, b["st"] + a + 1)
                            if a >= 2:
                                pe.wait_ge(arg_ready, b["st"] + a - 1)
                            small_mm(c[:, 256:384], tri, sp[:, 256:384])
                            small_mm(c[:, 0:256], tri, sp[:, 0:256], True, False)
                            small_mm(c[:, 128:256], ones, sp[:, 256:384], False, True).then_inc(c_full, 1)

                        def stick_out(a):
                            pe.wait_ge(p_ready, b["pr"] + a + 1)
                            value_mm(b, a, probT[:, a % 2, :], v(a), HD)

                        scores_T(0)
                        for a in range(NH):
                            if a + 1 < NH:
                                scores_T(a + 1)
                            suffix(a)
                            if a:
                                stick_out(a - 1)
                        stick_out(NH - 1)
                    else:
                        v = {"moba": values(1024, HD), "mla": lambda h: (lambda kt: proj[:, kt, mla_value_col(h):mla_value_col(h) + HD]), "band": values(2048, HD),
                             "diff": values(2048, 128)}[which]
                        width = 128 if which == "diff" else HD

                        def finish(h):
                            if which == "diff":
                                pe.wait_ge(a_ready, h + 1)
                                p = mixp
                                src = [p[:, j * P:(j + 1) * P] for j in range(3)]
                            else:
                                pe.wait_ge(p_ready, b["pr"] + h + 1)
                                src = [prob[:, h % 2, j * P:(j + 1) * P] for j in range(3)]
                            turn(b["u"] + h, src)
                            pe.wait_ge(tr_free, b["u"] + h + 1 + 2)
                            value_mm(b, h, probT[:, h % 2, :], v(h), width)

                        if which == "diff":
                            scores(0)
                            scores(1)
                            for h in range(8):
                                if h < 7:
                                    scores(2 * h + 2)
                                    scores(2 * h + 3)
                                finish(h)
                        else:
                            scores(0)
                            for h in range(heads):
                                if h + 1 < heads:
                                    scores(h + 1)
                                finish(h)
                elif kind == "mla_T":
                    pe.wait_ge(src_ready, b["src"])
                    c0 = 6 * 512
                    turn(b["u"], [proj[:, t, c0 + k * P:c0 + (k + 1) * P] for k in range(2) for t in range(NT)])
                    turn(b["u"] + 1, [proj[:, t, c0 + QL:c0 + QL + P] for t in range(NT)])
                elif kind == "mla_up":
                    n = b["n"]
                    pe.wait_ge(tr_free, b["u"] + 2)
                    pe.wait_ge(o_free, b["ov"])
                    wide = acc[:].rearrange("p (t a) c -> p t a c", t=NT)
                    chunk_wait(n)
                    s = n % PARTS
                    for t in range(NT):
                        for h, w in ((0, 512), (1, 256)):
                            for k in range(2):
                                c = slice(k * 768 + h * 512, k * 768 + h * 512 + w)
                                ins = mm3(wide[:, t, h, 0:w], yT_hi[:, k, t * P:(t + 1) * P], yT_lo[:, k, t * P:(t + 1) * P],
                                          w_hi[:, s, c], w_lo[:, s, c], k == 0, k == 1)
                    ins.then_inc(pe_used, 1)
                    chunk_wait(n + 1)
                    s = (n + 1) % PARTS
                    pe.wait_ge(ev_ready, b["ev"] + 1)
                    for t in range(NT):
                        for h in range(2):
                            c = slice(h * 512, h * 512 + 512)
                            ins = mm3(wide[:, t, h, :], yT_hi[:, 2, t * P:(t + 1) * P], yT_lo[:, 2, t * P:(t + 1) * P],
                                      w_hi[:, s, c], w_lo[:, s, c], True, True)
                    ins.then_inc(pe_used, 1)
                elif kind == "merge":
                    pe.wait_ge(o_free, b["ov"])
                    for j in range(6):
                        n = b["n"] + 3 * j
                        if j % 2 == 0:
                            for r in range(2):
                                c0 = Y_COL[j // 2] + 2 * r * P
                                turn(b["u"] + j + r, [proj[:, t, c0 + k * P:c0 + (k + 1) * P] for k in range(2) for t in range(NT)])
                        if j:
                            pe.wait_ge(z_ready, b["mg"] + j)
                        columns(n, lambda t: gu[:, t, :], 0, 4, True, False)
                        columns(n + 1, lambda t: gu[:, t, :], 4, 4, False, True)
                        if j >= 2:
                            pe.wait_ge(mg_ready, b["mg"] + j - 1)
                        pe.wait_ge(tr_free, b["u"] + 2 * (j // 2 + 1) + 2)
                        columns(n + 2, lambda t: acc[:, 2 * (j % 2) + t, :], 0, 4, True, True, src=(yT_hi, yT_lo))
                elif kind == "backT":
                    src = tok if step[1] == "merged" else proj
                    pe.wait_ge(mg_ready, b["mg"]) if step[1] == "merged" else pe.wait_ge(o_free, b["ov"])
                    if step[1] == "subln":
                        pe.wait_ge(src_ready, b["src"])
                    for r in range(4):
                        turn(b["u"] + r, [src[:, t, (2 * r + k) * P:(2 * r + k + 1) * P] for k in range(2) for t in range(NT)])
                elif kind == "out":
                    pe.wait_ge(tr_free, b["u"] + 2)
                    for c in range(4):
                        rows(b["n"] + c, lambda k, t: tuple(v[:, 2 * c + k, t * P:(t + 1) * P] for v in (hT_hi, hT_lo)),
                             c == 0, c == 3)
                        if c == 1:
                            gate_row(b, b["u"])
                elif kind == "route":
                    pe.wait_ge(rw_ready, 1)
                    pe.wait_ge(tr_free, b["u"] + 2)
                    for t in range(NT):
                        for k in range(KT):
                            ins = mm3(tr[:, b["u"] % 2, t * EXP:(t + 1) * EXP], hT_hi[:, k, t * P:(t + 1) * P],
                                      hT_lo[:, k, t * P:(t + 1) * P], rw_hi[:, k * EXP:(k + 1) * EXP],
                                      rw_lo[:, k * EXP:(k + 1) * EXP], k == 0, k == KT - 1)
                    ins.then_inc(tr_full, 1)
                    l = step[1]
                    pe.wait_ge(sent_ready, l + 1)
                    pe.wait_ge(tr_free, b["u"] + 2)
                    bank, sent, before = tr[:, (b["u"] + 1) % 2, :], rt[:, 3, :], cst("before")
                    s0, s1 = sent[:, 0:EXP], sent[:, EXP:2 * EXP]
                    for dst, terms in ((0, ((before, s0),)), (EXP, ((before, s1), (ones, s0))),
                                       (2 * EXP, ((ones, s0), (ones, s1)))):
                        for j, (lhs, rhs) in enumerate(terms):
                            ins = small_mm(bank[:, dst:dst + EXP], lhs, rhs, j == 0, j == len(terms) - 1)
                    ins.then_inc(tr_full, 1)


def constants():
    c = np.zeros((P, N_CONST), np.float32)

    def put(name, v):
        c[:, CONST[name][0]:CONST[name][1]] = np.asarray(v, np.float32).reshape(P, -1)

    r = np.arange(P)
    put("ident", np.eye(P))
    put("flip", np.eye(P)[::-1])
    put("ones", np.ones((P, P)))
    put("tri", (r[:, None] >= r[None, :]))
    put("before", (r[:, None] < r[None, :]))
    put("slots", np.tile(r, (P, 1)))
    keep = r[None, :] <= r[:, None]
    put("causal", np.where(np.concatenate([keep, np.ones((P, P), bool), keep], 1), 0.0, -BIG))
    keep = r[:, None] < r[None, :]
    put("strict", np.where(np.concatenate([keep, np.ones((P, P), bool), keep], 1), 0.0, -BIG))
    keep = (r[None, :] // BAND_CHUNK) <= (r[:, None] // BAND_CHUNK)
    put("chunked", np.where(np.concatenate([keep, np.ones((P, P), bool), keep], 1), 0.0, -BIG))
    for name, rot in (("p", ROT), ("m", ROPE)):
        inv = np.power(np.float32(THETA), -np.arange(0, rot, 2, dtype=np.float32) / np.float32(rot)).astype(np.float32)
        ang = np.arange(S, dtype=np.float32)[:, None] * inv[None, :]
        for f, fn in (("cos", np.cos), ("sin", np.sin)):
            put(f"{f}_{name}", fn(ang).astype(np.float32).reshape(NT, P, rot // 2).transpose(1, 0, 2))
    put("rank", np.tile(np.arange(EXP, 0, -1), (P, NT)))
    put("grank", np.tile(np.arange(GROUPS, 0, -1), (P, NT)))
    rel = np.arange(512) - 256
    n = np.abs(rel)
    large = 8 + (np.log(np.maximum(n, 1).astype(np.float32) / np.float32(8)) / math.log(1024 / 8) * 8).astype(np.int32)
    bucket = np.where(rel > 0, 16, 0) + np.where(n < 8, n, np.minimum(large, 15))
    return c, (np.arange(32)[:, None] == bucket[None, :]).astype(np.float32)


def weight_stream(a):
    n_chunks = make_plan()[-1][1]["n"]
    w = np.zeros((n_chunks, P, CW), np.float32)
    at = 0

    def tiles(m, kt, width):
        return m.reshape(kt, P, width).transpose(1, 0, 2)

    def add(block, pitch=None):
        nonlocal at
        kt, width = block.shape[1], block.shape[2]
        pitch = pitch or width
        w[at].reshape(P, CW)[:, :kt * pitch].reshape(P, kt, pitch)[:, :, :width] = block
        at += 1

    for name, vecs in (("ada_w", 9), ("ada_w_2", 6)):
        for l in range(DEPTH):
            for v in range(vecs):
                for kp in range(4):
                    add(tiles(a[name][l, kp * 256:(kp + 1) * 256, v * D:(v + 1) * D], 2, D))

    def ffn(blocks):
        held = None
        for g, u, d in blocks:
            for half in range(2):
                r = slice(512 * half, 512 * half + 512)
                add(np.concatenate([tiles(g[r], 4, BLK), tiles(u[r], 4, BLK)], 2))
            if held is not None:
                add(held)
            held = tiles(d, 2, D)
        add(held)

    def dense_ffn(l, s):
        ffn((a["ffn_w_gate"][l, s][:, c:c + BLK], a["ffn_w_up"][l, s][:, c:c + BLK], a["ffn_w_down"][l, s][c:c + BLK])
            for c in range(0, FF, BLK))

    def col_blocks(m, width=512):
        for half in range(2):
            add(tiles(m[512 * half:512 * half + 512], 4, width), 512)

    for l in range(DEPTH):
        dense_ffn(l, 0)
        w_in = a["mix_w_in"][l]
        for j in range(6):
            col_blocks(w_in[:, 512 * j:512 * j + 512])
        col_blocks(w_in[:, 3072:PROJ_W], PROJ_W - 3072)
        add(tiles(a["mla_w_uq"][l], 2, 768))
        add(tiles(a["mla_w_ukv"][l], 1, 1024))
        for n in range(3):
            for half in range(2):
                c = PROJ_W + n * D + half * 512
                col_blocks(w_in[:, c:c + 512])
                add(tiles(a["mix_w_branch"][l, n][:, half * 512:half * 512 + 512], 4, 512))
        for c in range(4):
            add(tiles(a["mix_w_out"][l][256 * c:256 * c + 256], 2, D))
        dense_ffn(l, 1)
    for l, which in enumerate("ab"):
        for j in range(6):
            col_blocks(a[f"{which}_w_qkv_2"][0][:, 512 * j:512 * j + 512])
        for c in range(4):
            add(tiles(a[f"{which}_w_o_2"][0][256 * c:256 * c + 256], 2, D))
        ffn((a["moe_w_gate_2"][l, e][:, c:c + BLK], a["moe_w_up_2"][l, e][:, c:c + BLK], a["moe_w_down_2"][l, e][c:c + BLK])
            for e in range(EXP) for c in range(0, EF, BLK))
    assert at == n_chunks, (at, n_chunks)
    return w


def column_vectors(a):
    v = np.zeros((P, N_VEC), np.float32)

    def put(name, *parts):
        cols = np.concatenate([np.asarray(p).reshape(-1, P).T for p in parts], 1)
        v[:, VEC[name][0]:VEC[name][1]] = cols

    put("c", a["c"])
    put("c_2", a["c_2"])
    put("ada_b", a["ada_b"], a["ada_b_2"])
    second = [p for l in range(DEPTH) for p in (a["norm_mix_g_2"][l], a["norm_ffn_g_2"][l])]
    put("pre", a["norm_pre"], *second)
    put("post", a["norm_post"])
    put("q_norm", a["mla_q_norm"])
    put("kv_norm", a["mla_kv_norm"])
    for name, src in (("a_q", "a_q_gain_2"), ("a_k", "a_k_gain_2"), ("b_q", "b_q_gain_2"), ("b_k", "b_k_gain_2")):
        put(name, np.tile(a[src][0], 2))
    put("subln", a["a_subln_g_2"])
    return v


def kernel(**inputs):
    import concourse.bacc as _bacc
    from concourse.bass_utils import run_bass_kernel_spmd as _run

    a = {k: np.asarray(v) for k, v in inputs.items()}
    const, t5hot = constants()
    rw = a["router_w_2"].reshape(KT, P, EXP).transpose(1, 0, 2).reshape(P, KT * EXP)
    arrays = {
        "wstream": weight_stream(a), "x_in": a["x"][0], "const_in": const, "vec_in": column_vectors(a),
        "bgate_in": a["mix_b_gate"].reshape(DEPTH, 3 * D), "lam_in": a["a_lambda_2"].reshape(4 * HD),
        "rbias_in": a["router_bias_2"], "t5_in": a["t5_bias_2"], "t5hot_in": t5hot, "rel_in": a["b_rel_bias_2"][0],
        "rw_in": rw,
    }
    arrays = {k: np.ascontiguousarray(v) for k, v in arrays.items()}
    nc = _bacc.Bacc("TRN2", target_bir_lowering=False, num_devices=1)
    aps = [nc.dram_tensor(k, v.shape, mybir.dt.from_np(v.dtype), kind="ExternalInput").ap() for k, v in arrays.items()]
    out = nc.dram_tensor("x_out", (S, D), F32, kind="ExternalOutput").ap()
    build(nc, *aps, out)
    r = _run(nc, [arrays], core_ids=[0])
    return r.results[0]["x_out"].reshape(1, S, D)
```

```python
from contextlib import ExitStack
import math

import numpy as np
import concourse.bass as bass
from concourse import mybir

F32 = mybir.dt.float32
F32R = mybir.dt.float32r
ACT = mybir.ActivationFunctionType
ALU = mybir.AluOpType
AX = mybir.AxisListType.X

P = 128
S = 256
NT = S // P
D = 1024
KT = D // P
DEPTH = 2
FF = 2816
HD = 64
NH = 8
W_BR = NH * HD
QL, KVL, ROPE, NOPE = 256, 128, 32, 64
QK_C = NOPE + ROPE
ROT = HD // 4
THETA = 500000.0
EXP, EF = 16, 512
GROUPS = 4
BAND_CHUNK = 64
EPS = 1e-6
BIG = 1e30
BLK = 256
CW = 2048

STAGES = 6
PARTS = 3
NVEC = DEPTH * 9 + DEPTH * 6
UW = 768
UC = UW // P
UNITS = NVEC * D // UW
FIRST_UNITS = 3 * D // UW
SLICES = 4
FFN_UNITS = 9
NSUB = DEPTH * 3 + DEPTH * 2
FFN_BLOCKS = FF // BLK
MOE_BLOCKS = EXP * EF // BLK
PROJ_W = 6 * 512 + QL + KVL + ROPE

Y_COL = (0, 1536, 512)
MQ, MK = 512, 2048


def mla_value_col(h):
    return (MQ if h < 4 else MK) + NH * QK_C + (h % 4) * HD



CONST = {}
_at = 0
for _name, _w in (("ident", P), ("flip", P), ("ones", P), ("tri", P), ("before", P), ("slots", P), ("causal", 384), ("strict", 384), ("chunked", 384),
                  ("cos_p", NT * 8), ("sin_p", NT * 8), ("cos_m", NT * 16), ("sin_m", NT * 16),
                  ("rank", NT * EXP), ("grank", NT * GROUPS)):
    CONST[_name] = (_at, _at + _w)
    _at += _w
N_CONST = _at
VEC = {}
_at = 0
for _name, _w in (("c", KT), ("c_2", KT), ("ada_b", NVEC * KT), ("pre", NSUB * KT), ("post", DEPTH * 3 * KT),
                  ("q_norm", DEPTH * 2), ("kv_norm", DEPTH), ("a_q", 1), ("a_k", 1), ("subln", 1), ("b_q", 1), ("b_k", 1)):
    VEC[_name] = (_at, _at + _w)
    _at += _w
N_VEC = _at


def make_plan():
    steps = []
    for l in range(DEPTH):
        steps += [("norm", 3 * l), ("ffn", 3 * l, FFN_BLOCKS, None), ("resid", 3 * l)]
        k = 3 * l + 1
        steps += [("norm", k), ("proj", 7), ("rope_p",),
                  ("qkT", "pairs", 0, 512, None), ("soft", "moba"),
                  ("qkT", "pairs", 1536, 2048, None), ("stick",),
                  ("mla_norm", l), ("mla_T", l), ("mla_up",), ("rope_m",), ("qkT", "mla", MQ, MK, None), ("soft", "mla"),
                  ("merge", l), ("backT", "merged"), ("out", k), ("resid", k)]
        steps += [("norm", 3 * l + 2), ("ffn", 3 * l + 2, FFN_BLOCKS, None), ("resid", 3 * l + 2)]
    for l in range(DEPTH):
        k = 3 * DEPTH + 2 * l
        which = "ab"[l]
        steps += [("norm", k), ("proj", 6), ("head_norm",),
                  ("qkT", "wide", 0, 1024, which), ("diff" if l == 0 else "soft", "band")]
        steps += [("out_norm",)] if l == 0 else []
        steps += [("backT", "subln" if l == 0 else "y"), ("out", k), ("resid", k)]
        steps += [("norm", k + 1), ("route", l), ("ffn", k + 1, MOE_BLOCKS, "moe"), ("resid", k + 1)]
    kinds = ("n", "u", "th", "tf", "hid", "req", "src", "x", "ev", "sc", "pr", "ov", "st", "mg", "sq", "mx", "hn")
    at = dict.fromkeys(kinds, 0)
    plan = []
    for step in steps:
        plan.append((step, dict(at)))
        kind = step[0]
        uses = {
            "norm": dict(u=4, th=4, tf=4, req=NT, src=1),
            "rope_p": dict(src=1), "rope_m": dict(src=1), "mla_norm": dict(req=1, src=1),
            "mla_T": dict(u=2, th=2, tf=2), "mla_up": dict(n=2, ev=2),
            "qkT": dict(u=4 if "pairs" in step else 8),
            "stick": dict(sc=8, pr=8, ov=8, st=8),
            "merge": dict(n=18, u=6, th=6, mg=6), "out": dict(n=4, u=2, tf=2),
            "head_norm": dict(req=1, src=1), "out_norm": dict(req=1, src=1, sq=1),
            "diff": dict(sc=16, mx=16, pr=16, u=8, ov=8), "route": dict(u=2, th=1),
        }
        if kind == "ffn":
            nb = step[2]
            used = dict(n=3 * nb, u=nb + 2 + (0 if step[3] else FFN_UNITS), th=nb, tf=2, hid=nb)
            if step[3]:
                used.update(u=MOE_TURNS, th=MOE_HIGHS)
        elif kind == "proj":
            used = dict(n=2 * step[1], ev=step[1])
            if step[1] == 6:
                used.update(sq=2, hn=1)
        elif kind == "resid":
            used = dict(req=NT if step[1] < 6 else 0)
        elif kind == "soft":
            h = 16 if step[1] == "band" else 8
            used = dict(sc=h, mx=h, pr=h, u=h, ov=h)
        elif kind == "backT":
            used = dict(u=4, th=4, tf=4) if step[1] == "subln" else dict(u=4, th=4)
        else:
            used = uses[kind]
        for name, c in used.items():
            at[name] += c
    plan.append((("end",), dict(at)))
    return plan


PAIRS = EXP // 2
MOE_TURNS = 2 + 8 + 9 * PAIRS + MOE_BLOCKS
MOE_HIGHS = 8 * PAIRS + MOE_BLOCKS


def moe_order(start, per_pair):
    first = start + per_pair - 4

    def gather(p, r):
        if p == 0:
            return start + r
        return first - 1 + per_pair * (p - 1) + (12 if r == KT else 1 + 3 * (r // 2) + r % 2)

    def scatter(g):
        p, j = (g + 1) // 4, (g + 1) % 4
        if g >= MOE_BLOCKS - 5:
            p, j, step = PAIRS - 1, g + 5 - MOE_BLOCKS, 1
        else:
            step = 3
        return first - 1 + per_pair * p + step * j

    return gather, scatter


def ffn_order(start, units):
    if not units:
        return (lambda g: start + 2 + g), None, 2
    return (lambda g: start + 2 + (g if g < 2 else 2 * g - 2)), (lambda g: start + 2 + 2 * g - 1), 4


def block_order(nb):
    peeled = 1 if nb % 2 == 0 else 2
    return peeled, (nb - 1 - peeled) // 2


def build(nc, wstream, ada_stream, xin, const_in, vec_in, bgate_in, lam_in, rbias_in, t5_in, t5hot_in, rel_in, rw_in, out):
    plan = make_plan()
    n_chunks = plan[-1][1]["n"]
    dense_steps = [(step[1], b["n"]) for step, b in plan if step[0] == "ffn" and not step[3]]
    unit_base = {k: FIRST_UNITS + FFN_UNITS * i for i, (k, _) in enumerate(dense_steps)}
    assert FIRST_UNITS + FFN_UNITS * len(dense_steps) == UNITS and FFN_BLOCKS == FFN_UNITS + 2
    assert block_order(FFN_BLOCKS)[0] == 2

    with ExitStack() as ctx:
        def sb(name, shape, dt=F32):
            return ctx.enter_context(nc.sbuf_tensor(name, shape, dt))

        def sem(name):
            return ctx.enter_context(nc.semaphore(name))

        stage = sb("stage", [P, STAGES, CW])
        w_hi = sb("w_hi", [P, PARTS, CW], F32R)
        w_lo = sb("w_lo", [P, PARTS, CW], F32R)
        x = sb("x_tok", [P, NT, D])
        tok = sb("tok", [P, NT, D])
        hT_hi = sb("hT_hi", [P, KT, S], F32R)
        hT_lo = sb("hT_lo", [P, KT, S], F32R)
        proj_at = nc.sbuf_base
        proj = sb("proj", [P, NT, PROJ_W])
        h_hi = nc.alloc_sbuf_tensor_at("h_hi", [P, NT, D], F32R, offset=proj_at)
        h_lo = nc.alloc_sbuf_tensor_at("h_lo", [P, NT, D], F32R, offset=proj_at + NT * D * 4)
        pick = nc.alloc_sbuf_tensor_at("pick", [P, NT, 2 * P], F32R, offset=proj_at + 2 * NT * D * 4)
        g_lo = nc.alloc_sbuf_tensor_at("g_lo", [P, KT, S], F32R, offset=proj_at + 2 * NT * (D + P) * 4)
        yT_hi = sb("yT_hi", [P, 4, S], F32R)
        yT_lo = sb("yT_lo", [P, 4, S], F32R)
        qk_at = nc.sbuf_base
        qk = sb("qk", [P, 16, S])
        g_hi = nc.alloc_sbuf_tensor_at("g_hi", [P, KT, S], F32R, offset=qk_at)
        pair = sb("pair", [P, 2, NT, BLK])
        hid_hi = yT_hi[:, 0:2, :].rearrange("p a s -> p (a s)")
        hid_lo = yT_lo[:, 0:2, :].rearrange("p a s -> p (a s)")
        tf = sb("tf", [P, 2, 512])
        prob = tok[:, :, 512:896]
        probT = pair[:].rearrange("p a t c -> p a (t c)")[:, :, 0:384]
        mixp = tf[:, 0, 0:384]
        bias_in = proj[:, :, 3072:3456]
        rope_t = pair[:, 0].rearrange("p t c -> p (t c)").rearrange("p (i w) -> p i w", i=4)
        pickT = qk[:, 8:12, :].rearrange("p (b e) s -> p b (e s)", b=2)
        pickg = qk[:, 12:14, :]
        gathered = ((hT_hi, hT_lo), (g_hi, g_lo))
        ada_stage = proj[:].rearrange("p t c -> p (t c)")[:, 0:SLICES * 2 * UW].rearrange("p (q c) -> p q c", q=SLICES)
        ada_acc = qk[:, 0:6, :].rearrange("p a s -> p (a s)").rearrange("p (b c) -> p b c", b=2)
        const = sb("const", [P, N_CONST])
        vec = sb("vec", [P, N_VEC])
        mod = sb("mod", [P, NVEC, KT])
        c_act = sb("c_act", [P, 2 * KT])
        c_unit = sb("c_unit", [P, UNITS, KT])
        c_tmp = sb("c_tmp", [P, 2 * KT])
        ss = sb("ss", [P, 64])
        rs = sb("rs", [P, 64])
        mhalf = sb("mhalf", [P, 64])
        nmax = sb("nmax", [P, 2, 2])
        rsum = sb("rsum", [P, 2, 2])
        rinv = sb("rinv", [P, 2, 2])
        lam = sb("lam", [P, 4 * HD])
        lam_s = sb("lam_s", [P, 4])
        rw = sb("rw", [P, KT * EXP])
        rw_hi = sb("rw_hi", [P, KT * EXP], F32R)
        rw_lo = sb("rw_lo", [P, KT * EXP], F32R)
        rbias = sb("rbias", [P, EXP])
        gates = sb("gates", [P, NT, EXP])
        rank = sb("rank", [P, NT, EXP])
        fullest = sb("fullest", [P, 1])
        fullest_i = sb("fullest_i", [P, 1], mybir.dt.int32)
        rt = sb("rt", [P, 8, NT * EXP])
        t5 = sb("t5", [32, 8])
        t5hot = tf[0:32, 1, :]
        t5row = tf[0:8, 0, :]
        t5_dram = nc.dram_tensor("t5_rows", [8, 512], F32)

        acc = ctx.enter_context(nc.psum_tensor("acc", [P, 4, 512], F32))
        gu = ctx.enter_context(nc.psum_tensor("gu", [P, 2, 512], F32))
        tr = ctx.enter_context(nc.psum_tensor("tr", [P, 2, 512], F32))

        landed = [sem(f"landed{i}") for i in range(STAGES)]
        chunk_ready = sem("chunk_ready")
        hi_ready = sem("hi_ready")
        pe_used = sem("pe_used")
        tr_full = sem("tr_full")
        tr_free = sem("tr_free")
        th_ready = sem("th_ready")
        tf_ready = sem("tf_ready")
        sg_ready = sem("sg_ready")
        hid_ready = sem("hid_ready")
        rs_req = sem("rs_req")
        rs_done = sem("rs_done")
        src_ready = sem("src_ready")
        x_ready = sem("x_ready")
        half_done = sem("half_done")
        ev_ready = sem("ev_ready")
        s_full = sem("s_full")
        s_free = sem("s_free")
        m_ready = sem("m_ready")
        p_ready = sem("p_ready")
        a_ready = sem("a_ready")
        o_full = sem("o_full")
        o_free = sem("o_free")
        soft_ready = sem("soft_ready")
        sp_ready = sem("sp_ready")
        c_full = sem("c_full")
        arg_ready = sem("arg_ready")
        z_ready = sem("z_ready")
        e_ready = sem("e_ready")
        mg_ready = sem("mg_ready")
        bg_in = [sem("bg_in0"), sem("bg_in1")]
        bias_ld = [sem("bias_ld0"), sem("bias_ld1")]
        ld = sem("ld")
        act_up = sem("act_up")
        dve_up = sem("dve_up")
        pool_up = sem("pool_up")
        c_exp = sem("c_exp")
        ada_landed = [sem(f"ada_landed{q}") for q in range(SLICES)]
        half_sum = sem("half_sum")
        slice_sum = sem("slice_sum")
        sq_ready = sem("sq_ready")
        sq_used = sem("sq_used")
        ada_sum = sem("ada_sum")
        sent_ready = sem("sent_ready")
        count_ready = sem("count_ready")
        pick_ready = sem("pick_ready")
        rwhi_ready = sem("rwhi_ready")
        rw_ready = sem("rw_ready")
        t5_mm = sem("t5_mm")
        t5_sb = sem("t5_sb")
        t5_st = sem("t5_st")
        lam_dot = sem("lam_dot")
        lam_exp = sem("lam_exp")
        mh_ready = sem("mh_ready")
        st_out = sem("st_out")
        N_LD = 10

        def cst(name):
            return const[:, CONST[name][0]:CONST[name][1]]

        def col(name, i):
            return vec[:, VEC[name][0] + i:VEC[name][0] + i + 1]

        ident, flip, ones, tri = cst("ident"), cst("flip"), cst("ones"), cst("tri")
        block = ctx.enter_context(nc.Block())

        @block.sync
        def _(sp):
            def chunk(n, i=0, rounds=1):
                if not isinstance(i, int) or n >= STAGES:
                    sp.wait_ge(chunk_ready, n + 1 - STAGES + STAGES * rounds * i)
                at = bass.ds(n + STAGES * rounds * i, 1)
                sp.dma_start(stage[:, n % STAGES, :], wstream[at].rearrange("a p c -> (a p) c")).then_inc(
                    landed[n % STAGES], 16)

            def ada_slice(unit, q, i=0):
                m = SLICES * unit + q
                if not isinstance(i, int) or m >= SLICES:
                    sp.wait_ge(slice_sum, m + 1 - SLICES + 2 * SLICES * i)
                at = bass.ds(m + 2 * SLICES * i, 1)
                sp.dma_start(ada_stage[:, q, :], ada_stream[at].rearrange("a p c -> (a p) c")).then_inc(
                    ada_landed[q], 16)

            def stream(n, end):
                turns = (end - n) // STAGES
                if turns > 1:
                    with sp.Fori(0, turns) as i:
                        for s in range(STAGES):
                            chunk(n + s, i)
                    n += turns * STAGES
                for m in range(n, end):
                    chunk(m)

            for unit in range(FIRST_UNITS + 1):
                for q in range(SLICES):
                    ada_slice(unit, q)
                    if unit >= FIRST_UNITS - 1 and q % 4 < 3:
                        chunk(3 * (unit - FIRST_UNITS + 1) + q)
            n = STAGES
            for k, n0 in dense_steps:
                stream(n, n0 + 8)
                if k:
                    sp.wait_ge(x_ready, NT * k)
                    for q in range(SLICES):
                        ada_slice(unit_base[k], q)
                stream(n0 + 8, n0 + 12)
                with sp.Fori(0, (FFN_UNITS - 1) // 2) as i:
                    for a in range(2):
                        for q in range(SLICES):
                            if q < 3:
                                chunk(n0 + 12 + 3 * a + q, i)
                            ada_slice(unit_base[k] + 1 + a, q, i)
                n = n0 + 12 + 3 * (FFN_UNITS - 1)
            stream(n, n_chunks)
            sp.wait_ge(x_ready, NT * NSUB)
            sp.dma_start(out.rearrange("(t p) d -> p t d", p=P), x[:]).then_inc(st_out, 16)
            sp.wait_ge(st_out, 16)

        @block.gpsimd
        def _(pool):
            pool.dma_start(vec[:], vec_in).then_inc(ld, 16)
            pool.dma_start(const[:], const_in).then_inc(ld, 16)
            pool.dma_start(x[:], xin.rearrange("(t p) d -> p t d", p=P)).then_inc(ld, 16)
            pool.dma_start(rw[:], rw_in).then_inc(ld, 16)
            pool.dma_start(rbias[:], rbias_in.partition_broadcast(P)).then_inc(ld, 16)
            pool.dma_start(lam[:], lam_in.partition_broadcast(P)).then_inc(ld, 16)
            pool.dma_start(t5[:], t5_in).then_inc(ld, 16)
            pool.dma_start(t5hot, t5hot_in).then_inc(ld, 16)
            pool.memset(mhalf[:], -0.5).then_inc(mh_ready, 1)
            pool.wait_ge(mh_ready, 1)
            pool.wait_ge(t5_sb, 1)
            pool.dma_start(t5_dram.ap(), t5row).then_inc(t5_st, 16)
            pool.wait_ge(t5_st, 16)
            ups = 0

            def root(b, w, at=0, nth=0):
                nonlocal ups
                c = slice(at, at + w)
                pool.wait_ge(rs_req, b["req"] + nth + 1)
                pool.tensor_scalar(ss[:, c], ss[:, c], EPS, None, ALU.add).then_inc(pool_up, 1)
                ups += 1
                pool.wait_ge(pool_up, ups)
                pool.tensor_tensor(rs[:, c], ss[:, c], mhalf[:, c], ALU.pow).then_inc(rs_done, 1)

            loads = 0
            for step, b in plan:
                kind = step[0]
                if kind == "norm" or (kind == "resid" and step[1] < 6):
                    for t in range(NT):
                        root(b, 1, t + (NT if kind == "resid" else 0), t)
                elif kind == "mla_norm":
                    root(b, 4)
                elif kind == "head_norm":
                    root(b, 64)
                elif kind == "out_norm":
                    root(b, 16)
                elif (kind == "soft" and step[1] == "band") or kind == "diff":
                    table, pitch, heads = (t5_dram, 512, 8) if kind == "diff" else (rel_in.tensor, 513, 16)
                    per = 2 if kind == "diff" else 1
                    for h in range(heads):
                        if h >= 2:
                            pool.wait_ge(s_full, b["sc"] + per * (h - 1))
                        for q, (a, w) in enumerate(((0, 128), (128, 256))):
                            win = bass.AP(table, h * pitch + 129 - 128 * q, [[1, P], [1, w]])
                            pool.dma_start(bias_in[:, h % 2, a:a + w], win).then_inc(bias_ld[h % 2], 16)
                        loads += 1

        @block.scalar
        def _(act):
            ups = 0

            def hi(n, i=0, rounds=1):
                act.wait_ge(landed[n % STAGES], 16 * (n // STAGES + 1) + 16 * rounds * i)
                act.wait_ge(pe_used, n + 1 + STAGES * rounds * i)
                act.activation(w_hi[:, n % PARTS, :], stage[:, n % STAGES, :], ACT.Copy).then_inc(hi_ready, 1)

            def ahead(n):
                if n < n_chunks:
                    hi(n)
                    hi(n + 1)

            def own(ins):
                nonlocal ups
                ups += 1
                ins.then_inc(act_up, 1)
                act.wait_ge(act_up, ups)

            act.wait_ge(ld, 16 * 8)
            act.activation(c_tmp[:], vec[:, 0:2 * KT], ACT.Exp, scale=-1.0).then_inc(c_exp, 1)
            act.activation(rw_hi[:], rw[:], ACT.Copy).then_inc(rwhi_ready, 1)
            act.wait_ge(t5_mm, 1)
            act.activation(t5row, tr[0:8, 0, :], ACT.Copy).then_inc(t5_sb, 1)
            act.wait_ge(lam_dot, 1)
            act.activation(lam_s[:, 2:4], lam_s[:, 0:2], ACT.Exp).then_inc(lam_exp, 1)

            def squares(b, srcs):
                for i, (src, width) in enumerate(srcs):
                    ins = act.activation(tok[:, i % 2, 0:width], src, ACT.Square, scale=width ** -0.5,
                                         accum_out=ss[:, i:i + 1])
                    if i < len(srcs) - 1:
                        own(ins)
                ins.then_inc(rs_req, 1)

            def mean_square(b, t, src, at):
                if b["req"] + t:
                    act.wait_ge(rs_req, b["req"] + t)
                act.activation(pair[:].rearrange("p a t c -> p (a t c)"), src, ACT.Square, scale=D ** -0.5,
                               accum_out=ss[:, at:at + 1]).then_inc(rs_req, 1)

            def take_hi(b, rounds, dst, plain, width=512):
                for r in range(rounds):
                    if plain:
                        act.wait_ge(tr_full, b["u"] + r + 1)
                        src = tr[:, (b["u"] + r) % 2, :]
                    else:
                        act.wait_ge(tf_ready, b["tf"] + r + 1)
                        src = tf[:, (b["tf"] + r) % 2, :]
                    w = width[r] if isinstance(width, tuple) else width
                    d = dst[:, 2 * r:2 * r + w // S, :].rearrange("p a s -> p (a s)")
                    act.activation(d, src[:, 0:w], ACT.Copy).then_inc(th_ready, 1)

            def ffn(b, nb, units):
                peeled, turns = block_order(nb)
                n0, g0 = b["n"], b["hid"]
                u_of, _, per_turn = ffn_order(b["u"], units)

                def silu(g, i=0):
                    act.wait_ge(pe_used, n_b(g) + 1 + PARTS + STAGES * i)
                    if not isinstance(i, int) or g >= 1:
                        act.wait_ge(hid_ready, g0 + g + 2 * i)
                    act.activation(pair[:, 0], gu[:, :, 0:BLK], ACT.Silu).then_inc(sg_ready, 1)

                def n_b(g):
                    return n0 + 1 if g == 0 else n0 + 3 * g

                def turn_hi(g, u, i=0):
                    act.wait_ge(tr_full, u + 1 + per_turn * i)
                    if not isinstance(i, int) or g >= 1:
                        act.wait_ge(pe_used, n0 + 3 * g + 1 + 1 + PARTS + STAGES * i)
                    act.activation(hid_hi, tr[:, u % 2, :], ACT.Copy).then_inc(th_ready, 1)

                def block_(g, i=0):
                    hi(n0 + 3 * g - 1, i)
                    silu(g - 1, i)
                    hi(n0 + 3 * g, i)
                    hi(n0 + 3 * g + 1, i)
                    turn_hi(g - 1, u_of(g - 1), i)

                for g in range(1, 1 + peeled):
                    block_(g)
                with act.Fori(0, turns) as i:
                    block_(1 + peeled, i)
                    block_(2 + peeled, i)
                silu(nb - 1)
                hi(n0 + 3 * nb - 1)
                turn_hi(nb - 1, u_of(nb - 1))
                ahead(n0 + 3 * nb)

            def moe(b, l):
                n0, g0 = b["n"], b["hid"]
                gather_u, scatter_u = moe_order(b["u"] + 2 + 8, 13)

                def chunk_of(g):
                    return n0 if g == 0 else n0 + 3 * g - 1

                def silu(g, i=0):
                    act.wait_ge(pe_used, chunk_of(g) + 1 + 1 + PARTS + 24 * i)
                    if not isinstance(i, int) or g >= 2:
                        act.wait_ge(hid_ready, g0 + g - 1 + 8 * i)
                    act.activation(pair[:, 0, g % 2, :], gu[:, g % 2, 0:BLK], ACT.Silu).then_inc(sg_ready, 1)

                def turn_hi(g, i=0):
                    u = scatter_u(g)
                    act.wait_ge(tr_full, u + 1 + 26 * i)
                    if not isinstance(i, int) or g >= 1:
                        act.wait_ge(pe_used, n0 + 3 * g + 1 + 1 + PARTS + 24 * i)
                    act.activation(hid_hi, tr[:, u % 2, :], ACT.Copy).then_inc(th_ready, 1)

                def gather_hi(p, r, i=0):
                    u = gather_u(p, r)
                    act.wait_ge(tr_full, u + 1 + 26 * i)
                    act.activation(gathered[p % 2][0][:, r, :], tr[:, u % 2, 0:S], ACT.Copy).then_inc(th_ready, 1)

                def pair_of(p, i=0):
                    for j in range(4):
                        g = 4 * p + j
                        if g:
                            hi(chunk_of(g), i, 4)
                            silu(g - 1, i)
                            hi(chunk_of(g) + 1, i, 4)
                            hi(chunk_of(g) + 2, i, 4)
                            turn_hi(g - 1, i)
                        if p < PAIRS - 1:
                            for r in (2 * j, 2 * j + 1):
                                gather_hi(p + 1, r, i)

                for r in range(KT):
                    gather_hi(0, r)
                pair_of(0)
                with act.Fori(0, (PAIRS - 2) // 2) as i:
                    pair_of(1, i)
                    pair_of(2, i)
                pair_of(PAIRS - 1)
                silu(MOE_BLOCKS - 1)
                hi(n0 + 3 * MOE_BLOCKS - 1)
                turn_hi(MOE_BLOCKS - 1)
                ahead(n0 + 3 * MOE_BLOCKS)

            def soft(b, heads):
                for a in range(heads):
                    act.wait_ge(m_ready, b["mx"] + a + 1)
                    s = (b["sc"] + a) % 2
                    for q, (lo, w) in enumerate(((0, 128), (128, 256))):
                        ins = act.activation(prob[:, s, lo:lo + w], prob[:, s, lo:lo + w], ACT.Exp,
                                             bias=nmax[:, s, q:q + 1], accum_out=rsum[:, s, q:q + 1])
                    ins.then_inc(p_ready, 1)

            ahead(0)
            for step, b in plan:
                kind = step[0]
                if kind == "norm":
                    k = step[1]
                    for t in range(NT):
                        act.wait_ge(x_ready, NT * (k - 1) + t + 1) if k else act.wait_ge(ld, 16 * 8)
                        mean_square(b, t, x[:, t, :], t)
                    take_hi(b, 4, hT_hi, False)
                elif kind == "ffn" and not step[3]:
                    ffn(b, step[2], True)
                elif kind == "ffn":
                    l = (step[1] - 3 * DEPTH) // 2
                    act.wait_ge(count_ready, l + 1)
                    most = act.value_load(fullest_i[0:1, 0:1], min_val=0, max_val=S)
                    with act.If(most <= P):
                        moe(b, l)
                    with act.Else():
                        ffn(b, step[2], False)
                        act.wait_ge(th_ready, b["th"] + MOE_BLOCKS)
                        act.nop().then_inc(th_ready, MOE_HIGHS - MOE_BLOCKS)
                elif kind == "resid" and step[1] < 6:
                    for t in range(NT):
                        act.wait_ge(pe_used, b["n"] + PARTS) if t else act.wait_ge(half_done, step[1] + 1)
                        mean_square(b, t, acc[:, 2 * t:2 * t + 2, :].rearrange("p a c -> p (a c)"), NT + t)
                elif kind == "proj":
                    blocks = step[1]

                    def evac(j):
                        act.wait_ge(pe_used, b["n"] + 2 * j + 2 + PARTS)
                        w = 512 if j < 6 else PROJ_W - 6 * 512
                        act.activation(proj[:, :, 512 * j:512 * j + w], acc[:, 2 * (j % 2):2 * (j % 2) + 2, 0:w],
                                       ACT.Copy).then_inc(ev_ready, 1)

                    for j in range(blocks):
                        if j:
                            hi(b["n"] + 2 * j)
                            hi(b["n"] + 2 * j + 1)
                            evac(j - 1)
                        if blocks == 6 and j >= 4:
                            if j == 4:
                                act.wait_ge(ev_ready, b["ev"] + 4)
                            else:
                                act.wait_ge(sq_used, b["hn"] + 1)
                            act.activation(tok[:].rearrange("p a c -> p (a c)"), proj[:, j - 4, 0:2048], ACT.Square,
                                           scale=HD ** -0.5).then_inc(sq_ready, 1)
                    evac(blocks - 1)
                    ahead(b["n"] + 2 * blocks)
                elif kind == "soft":
                    soft(b, 16 if step[1] == "band" else 8)
                elif kind == "diff":
                    soft(b, 16)
                elif kind == "stick":
                    def soften(a):
                        act.wait_ge(s_free, b["sc"] + a + 1)
                        s = a % 2
                        own(act.activation(mixp_of(a), prob[:, s, :], ACT.Abs))
                        own(act.activation(mixp_of(a), mixp_of(a), ACT.Exp, scale=-1.0))
                        act.activation(mixp_of(a), mixp_of(a), ACT.Ln, bias=1.0).then_inc(soft_ready, 1)

                    def mixp_of(a):
                        return tok[:, a % 2, 0:384]

                    def weigh(a):
                        act.wait_ge(arg_ready, b["st"] + a + 1)
                        if a >= 2:
                            act.wait_ge(o_full, b["ov"] + a - 1)
                        act.activation(probT[:, a % 2, :], prob[:, a % 2, :], ACT.Exp).then_inc(p_ready, 1)

                    soften(0)
                    for a in range(NH):
                        if a + 1 < NH:
                            soften(a + 1)
                        weigh(a)
                elif kind == "mla_norm":
                    act.wait_ge(ev_ready, b["ev"])
                    c0 = 6 * 512
                    act.wait_ge(o_full, b["ov"])
                    squares(b, [(proj[:, t, c0 + o:c0 + o + w], w) for o, w in ((0, QL), (QL, KVL)) for t in range(NT)])
                elif kind == "mla_T":
                    take_hi(b, 2, yT_hi, False, (512, 256))
                elif kind == "mla_up":
                    n = b["n"]
                    q_out = acc[:].rearrange("p (t a) c -> p t (a c)", t=NT)
                    act.wait_ge(pe_used, n + 1 + PARTS)
                    act.activation(proj[:, :, MQ:MQ + NH * QK_C], q_out[:, :, 0:NH * QK_C], ACT.Copy).then_inc(ev_ready, 1)
                    act.wait_ge(pe_used, n + 2 + PARTS)
                    for t in range(NT):
                        kv = q_out[:, t, :].rearrange("p (h e) -> p h e", h=NH)
                        act.activation(proj[:, t, MK:MK + 768].rearrange("p (h e) -> p h e", h=NH)[:, :, 0:NOPE],
                                       kv[:, :, 0:NOPE], ACT.Copy)
                        for h in (0, 4):
                            v = proj[:, t, mla_value_col(h):mla_value_col(h) + 4 * HD]
                            ins = act.activation(v.rearrange("p (h e) -> p h e", h=4), kv[:, h:h + 4, NOPE:128], ACT.Copy)
                    ins.then_inc(ev_ready, 1)
                    ahead(n + 2)
                elif kind == "merge":
                    l = step[1]

                    def load_bias(j):
                        if j >= 2:
                            act.wait_ge(z_ready, b["mg"] + j - 1)
                        c = 512 * j
                        act.dma_start(tf[:, j % 2, :], bgate_in[l, c:c + 512].partition_broadcast(P)).then_inc(
                            bg_in[j % 2], 16)

                    act.wait_ge(tr_free, b["u"] + 2)
                    load_bias(0)
                    load_bias(1)
                    def sigmoid(j):
                        act.wait_ge(z_ready, b["mg"] + j + 1)
                        flat = pair[:].rearrange("p a t c -> p (a t c)")
                        act.activation(flat, flat, ACT.Sigmoid).then_inc(e_ready, 1)
                        if j + 2 < 6:
                            load_bias(j + 2)

                    for j in range(6):
                        n = b["n"] + 3 * j
                        if j:
                            hi(n)
                            sigmoid(j - 1)
                            hi(n + 1)
                        hi(n + 2)
                        if j % 2 == 0:
                            for r in range(2):
                                u = b["u"] + j + r
                                act.wait_ge(tr_full, u + 1)
                                d = yT_hi[:, 2 * r:2 * r + 2, :].rearrange("p a s -> p (a s)")
                                act.activation(d, tr[:, u % 2, :], ACT.Copy).then_inc(th_ready, 1)
                    ahead(b["n"] + 18)
                    sigmoid(5)
                elif kind == "backT":
                    take_hi(b, 4, hT_hi, step[1] != "subln")
                elif kind == "out":
                    for c in range(2, 4):
                        hi(b["n"] + c)
                    ahead(b["n"] + 4)
                elif kind == "out_norm":
                    act.wait_ge(o_free, b["ov"])
                    act.activation(tok[:], proj[:, :, 0:D], ACT.Square, scale=128 ** -0.5).then_inc(sq_ready, 1)
                elif kind == "route":
                    act.wait_ge(tr_full, b["u"] + 1)
                    act.activation(rt[:, 0, :], tr[:, b["u"] % 2, 0:NT * EXP], ACT.Exp, scale=-1.0).then_inc(th_ready, 1)

        @block.vector
        def _(dve):
            ups = 0
            turn, per_turn = 0, 0

            def own(ins):
                nonlocal ups
                ups += 1
                ins.then_inc(dve_up, 1)
                dve.wait_ge(dve_up, ups + per_turn * turn)

            def lo(n, i=0, rounds=1):
                dve.wait_ge(hi_ready, n + 1 + STAGES * rounds * i)
                dve.tensor_tensor(w_lo[:, n % PARTS, :], stage[:, n % STAGES, :], w_hi[:, n % PARTS, :].bitcast(F32),
                                  ALU.subtract).then_inc(chunk_ready, 1)

            def ahead(n):
                if n < n_chunks:
                    lo(n)
                    lo(n + 1)

            def flat(ap):
                return ap.rearrange("p a b -> p (a b)")

            def take_lo(b, rounds, dst_hi, dst_lo, cols=None, width=(512, 512, 512, 512)):
                def rest(r):
                    dve.wait_ge(th_ready, b["th"] + r + 1)
                    w = width[r]
                    src = tf[:, (b["tf"] + r) % 2, 0:w] if cols else tr[:, (b["u"] + r) % 2, 0:w]
                    dve.tensor_tensor(flat(dst_lo[:, 2 * r:2 * r + w // S, :]), src,
                                      flat(dst_hi[:, 2 * r:2 * r + w // S, :]).bitcast(F32),
                                      ALU.subtract).then_inc(tr_free, 1)

                for r in range(rounds):
                    if cols:
                        dve.wait_ge(tr_full, b["u"] + r + 1)
                        for a in range(width[r] // S):
                            c0, c1, op1 = cols(2 * r + a)
                            ins = dve.tensor_scalar(tf[:, (b["tf"] + r) % 2, a * S:(a + 1) * S],
                                                    tr[:, (b["u"] + r) % 2, a * S:(a + 1) * S], c0, c1, ALU.mult, op1)
                        ins.then_inc(tf_ready, 1)
                        if r:
                            rest(r - 1)
                    else:
                        rest(r)
                if cols:
                    rest(rounds - 1)

            def gate_row(b, k, u, between=None):
                dve.wait_ge(tr_free, u + 2)
                for r in range(2):
                    for j in range(4):
                        ins = dve.tensor_scalar(tf[:, (b["tf"] + r) % 2, j * P:(j + 1) * P], ident,
                                                mod[:, 3 * k + 2, 4 * r + j:4 * r + j + 1], None, ALU.mult)
                    ins.then_inc(tf_ready, 1)
                for r in range(2):
                    dve.wait_ge(tr_full, u + r + 1)
                    dve.tensor_copy(tok[:, 0, r * 512:(r + 1) * 512], tr[:, (u + r) % 2, :]).then_inc(tr_free, 1)

            dve.nop().then_inc(tr_free, 2)
            dve.wait_ge(ld, 16 * 8)
            dve.wait_ge(c_exp, 1)
            own(dve.tensor_scalar(c_tmp[:], c_tmp[:], 1.0, None, ALU.add))
            own(dve.reciprocal(c_tmp[:], c_tmp[:]))
            own(dve.tensor_tensor(c_act[:], c_tmp[:], vec[:, 0:2 * KT], ALU.mult))
            dve.wait_ge(rwhi_ready, 1)
            dve.tensor_tensor(rw_lo[:], rw[:], rw_hi[:].bitcast(F32), ALU.subtract).then_inc(rw_ready, 1)
            lam4 = lam[:].rearrange("p (a b e) -> p a b e", a=2, b=2)
            dots = rope_t[:, 0, :].rearrange("p (a e) -> p a e", a=2)
            own(dve.tensor_tensor(dots, lam4[:, :, 0, :], lam4[:, :, 1, :], ALU.mult))
            dve.tensor_reduce(lam_s[:, 0:2], dots, AX, ALU.add).then_inc(lam_dot, 1)
            dve.wait_ge(lam_exp, 1)
            own(dve.tensor_tensor(lam_s[:, 0:1], lam_s[:, 3:4], lam_s[:, 2:3], ALU.subtract))
            own(dve.tensor_scalar(lam_s[:, 0:1], lam_s[:, 0:1], -0.2, None, ALU.add))

            split_at = DEPTH * 9 * D // UW
            for u_from, u_to, c0 in ((0, split_at, 0), (split_at, UNITS, KT)):
                ins = dve.tensor_copy(c_unit[:, u_from:u_to, :],
                                      c_act[:, c0:c0 + KT].unsqueeze(1).to_broadcast([P, u_to - u_from, KT]))
            own(ins)
            mod_flat, c_flat = flat(mod[:]), flat(c_unit[:])
            mods = mod[:].rearrange("p (k v) c -> p k v c", v=3)

            def ada_add(unit, q, i=0):
                m, total = SLICES * unit + q, ada_acc[:, unit % 2, :]
                dve.wait_ge(ada_landed[q], 16 * (unit + 1) + 32 * i)
                for j in range(2):
                    w = ada_stage[:, q, j * UW:(j + 1) * UW]
                    k = KT * unit + 2 * q + j
                    c = c_flat[:, k:k + 1] if isinstance(i, int) else c_flat[:, bass.ds(k + 2 * KT * i, 1)]
                    if j:
                        dve.wait_ge(half_sum, m + 1 + 2 * SLICES * i)
                    elif not isinstance(i, int) or m:
                        dve.wait_ge(slice_sum, m + 2 * SLICES * i)
                    if q == 0 and j == 0:
                        ins = dve.tensor_scalar(total, w, c, None, ALU.mult)
                    else:
                        ins = dve.scalar_tensor_tensor(total, w, c, total, ALU.mult, ALU.add)
                    ins.then_inc(slice_sum if j else half_sum, 1)

            for unit in range(FIRST_UNITS):
                dve.wait_ge(ada_sum, unit + 1)
                for q in range(SLICES):
                    ada_add(unit, q)
            dve.wait_ge(ada_sum, FIRST_UNITS + 2)
            n_first = FIRST_UNITS * UC
            own(dve.tensor_tensor(mod_flat[:, 0:n_first], acc[:, 0, 0:n_first],
                                  vec[:, VEC["ada_b"][0]:VEC["ada_b"][0] + n_first], ALU.add))
            ahead(0)

            def factors(k):
                scale, gate = mods[:, k, 1, :], mods[:, k, 2, :]
                def gain(name):
                    return vec[:, VEC[name][0] + k * KT:VEC[name][0] + (k + 1) * KT]

                ins = dve.scalar_tensor_tensor(scale, scale, 1.0, gain("pre"), ALU.add, ALU.mult)
                if k < 6:
                    own(dve.scalar_tensor_tensor(gate, gate, 1.0, gain("post"), ALU.add, ALU.mult))
                    if k % 3 != 1:
                        own(dve.tensor_scalar(gate, gate, 0.5, None, ALU.mult))
                else:
                    own(ins)

            def ffn(b, k, nb, moe):
                peeled, turns = block_order(nb)
                n0, g0, th0 = b["n"], b["hid"], b["th"]
                sg, hid = pair[:, 0], pair[:, 1]
                u_of, u_unit, per_turn_u = ffn_order(b["u"], not moe)

                def silu(g, i=0, expert=None):
                    dve.wait_ge(sg_ready, g0 + g + 1 + 2 * i)
                    if moe:
                        e = g // 2 if isinstance(i, int) else i + g // 2
                        for t in range(NT):
                            w = gates[:, t, e:e + 1] if isinstance(i, int) else gates[:, t, bass.ds(e, 1)]
                            ins = dve.scalar_tensor_tensor(hid[:, t, :], sg[:, t, :], w, gu[:, t, BLK:2 * BLK],
                                                           ALU.mult, ALU.mult)
                    else:
                        ins = dve.tensor_tensor(hid, sg, gu[:, :, BLK:2 * BLK], ALU.mult)
                    ins.then_inc(hid_ready, 1)

                def turn_lo(g, i=0):
                    dve.wait_ge(th_ready, th0 + g + 1 + 2 * i)
                    dve.tensor_tensor(hid_lo, tr[:, u_of(g) % 2, :], hid_hi.bitcast(F32),
                                      ALU.subtract).then_inc(tr_free, 1)

                def take_unit(g, i=0):
                    at = UC * (unit_base[k] + g - 2)
                    dve.wait_ge(tr_full, u_unit(g) + 1 + per_turn_u * i)
                    if isinstance(i, int):
                        dst, bias = mod_flat[:, at:at + UC], vec[:, VEC["ada_b"][0] + at:VEC["ada_b"][0] + at + UC]
                    else:
                        dst = mod_flat[:, bass.ds(at + 2 * UC * i, UC)]
                        bias = vec[:, bass.ds(VEC["ada_b"][0] + at + 2 * UC * i, UC)]
                    dve.tensor_tensor(dst, tr[:, u_unit(g) % 2, 0:UC], bias, ALU.add).then_inc(tr_free, 1)

                def block_(g, i=0):
                    add = (lambda q: ada_add(unit_base[k] + g - 2, q, i)) if not moe and g >= 2 else (lambda q: None)
                    lo(n0 + 3 * g - 1, i)
                    silu(g - 1, i)
                    add(0)
                    lo(n0 + 3 * g, i)
                    add(1)
                    lo(n0 + 3 * g + 1, i)
                    turn_lo(g - 1, i)
                    if not moe and g >= 3:
                        take_unit(g - 1, i)
                    add(2)
                    add(3)

                gate_row(b, k, b["u"])
                for g in range(1, 1 + peeled):
                    block_(g)
                with dve.Fori(0, turns) as i:
                    block_(1 + peeled, i)
                    block_(2 + peeled, i)
                silu(nb - 1)
                lo(n0 + 3 * nb - 1)
                turn_lo(nb - 1)
                if not moe:
                    take_unit(nb - 1)
                ahead(n0 + 3 * nb)

            def moe(b, k, l):
                n0, g0 = b["n"], b["hid"]
                gather_u, scatter_u = moe_order(b["u"] + 2 + 8, 13)
                gather_th, scatter_th = moe_order(b["th"], 12)

                def select(p, i=0):
                    for e in range(2):
                        at = slice(2 * p + e, 2 * p + e + 1) if isinstance(i, int) else bass.ds(4 * i + 2 * p + e, 1)
                        for t in range(NT):
                            dst = slice(e * P, (e + 1) * P)
                            dve.tensor_scalar(pick[:, t, dst], cst("slots"), rank[:, t, at], None, ALU.is_equal)
                            ins = dve.tensor_scalar(pickg[:, t, dst], cst("slots"), rank[:, t, at], gates[:, t, at],
                                                    ALU.is_equal, ALU.mult)
                    ins.then_inc(pick_ready, 1)

                def gather_lo(p, r, i=0):
                    u = gather_u(p, r)
                    if r < KT:
                        dve.wait_ge(th_ready, gather_th(p, r) + 1 + 24 * i)
                        dve.tensor_copy(gathered[p % 2][1][:, r, :], tr[:, u % 2, S:2 * S]).then_inc(tr_free, 1)
                    else:
                        dve.wait_ge(tr_full, u + 1 + 26 * i)
                        dve.tensor_copy(pickT[:, p % 2, :], tr[:, u % 2, :]).then_inc(tr_free, 1)

                def hidden(g, i=0):
                    dve.wait_ge(sg_ready, g0 + g + 1 + 8 * i)
                    dve.tensor_tensor(pair[:, 1, g % 2, :], pair[:, 0, g % 2, :], gu[:, g % 2, BLK:2 * BLK],
                                      ALU.mult).then_inc(hid_ready, 1)

                def turn_lo(g, i=0):
                    dve.wait_ge(th_ready, scatter_th(g) + 1 + 24 * i)
                    dve.tensor_tensor(hid_lo, tr[:, scatter_u(g) % 2, :], hid_hi.bitcast(F32),
                                      ALU.subtract).then_inc(tr_free, 1)

                def pair_of(p, i=0):
                    for j in range(4):
                        g = 4 * p + j
                        if g:
                            lo(n0 + 3 * g - 1, i, 4)
                            hidden(g - 1, i)
                            lo(n0 + 3 * g, i, 4)
                        if j == 0 and p < PAIRS - 1:
                            select(p + 1, i)
                        if g:
                            lo(n0 + 3 * g + 1, i, 4)
                            turn_lo(g - 1, i)
                        if p < PAIRS - 1:
                            for r in (2 * j, 2 * j + 1) + ((8,) if j == 3 else ()):
                                gather_lo(p + 1, r, i)

                gate_row(b, k, b["u"])
                for r in range(8):
                    part, t, half = r // 4, r // 2 % 2, r % 2
                    u = b["u"] + 2 + r
                    dve.wait_ge(tr_full, u + 1)
                    dve.tensor_copy((h_hi, h_lo)[part][:, t, half * 512:(half + 1) * 512],
                                    tr[:, u % 2, :]).then_inc(tr_free, 1)
                select(0)
                for r in range(KT + 1):
                    gather_lo(0, r)
                pair_of(0)
                with dve.Fori(0, (PAIRS - 2) // 2) as i:
                    pair_of(1, i)
                    pair_of(2, i)
                pair_of(PAIRS - 1)
                hidden(MOE_BLOCKS - 1)
                lo(n0 + 3 * MOE_BLOCKS - 1)
                turn_lo(MOE_BLOCKS - 1)
                ahead(n0 + 3 * MOE_BLOCKS)

            def soft_max_in(b, a, mask, scale):
                s = a % 2
                dve.wait_ge(s_full, b["sc"] + a + 1)
                dve.scalar_tensor_tensor(prob[:, s, :], gu[:, s, 0:384], scale, cst(mask),
                                         ALU.mult, ALU.add).then_inc(s_free, 1)
                dve.wait_ge(s_free, b["sc"] + a + 1)
                dve.tensor_reduce(nmax[:, s, 0:1], prob[:, s, 0:128], AX, ALU.max, negate=True)
                dve.tensor_reduce(nmax[:, s, 1:2], prob[:, s, 128:384], AX, ALU.max, negate=True).then_inc(m_ready, 1)

            def turn_prob(b, h):
                dve.wait_ge(tr_full, b["u"] + h + 1)
                if h >= 2:
                    dve.wait_ge(o_full, b["ov"] + h - 1)
                dve.tensor_copy(probT[:, h % 2, :], tr[:, (b["u"] + h) % 2, 0:384]).then_inc(tr_free, 1)

            def rotate(x1, x2, cos, sin, w, o1=None, o2=None):
                shape = x1.shape[1:]
                def tmp(i):
                    v = rope_t[:, i, 0:w]
                    return v.rearrange("p (h f) -> p h f", h=shape[0]) if len(shape) == 2 else v
                dve.tensor_tensor(tmp(0), x1, cos, ALU.mult)
                dve.tensor_tensor(tmp(1), x2, sin, ALU.mult)
                dve.tensor_tensor(tmp(2), x1, sin, ALU.mult)
                own(dve.tensor_tensor(tmp(3), x2, cos, ALU.mult))
                dve.tensor_tensor(x1 if o1 is None else o1, tmp(0), tmp(1), ALU.subtract)
                own(dve.tensor_tensor(x2 if o2 is None else o2, tmp(2), tmp(3), ALU.add))

            for step, b in plan:
                kind = step[0]
                if kind == "norm":
                    k = step[1]
                    dve.wait_ge(tr_free, b["u"] + 2)
                    factors(k)
                    if k:
                        dve.wait_ge(x_ready, NT * k)
                    for t in range(NT):
                        dve.wait_ge(rs_done, b["req"] + t + 1)
                        ins = dve.tensor_scalar(tok[:, t, :], x[:, t, :], rs[:, t:t + 1], None, ALU.mult)
                    ins.then_inc(src_ready, 1)
                    take_lo(b, 4, hT_hi, hT_lo,
                            lambda c: (mod[:, 3 * k + 1, c:c + 1], mod[:, 3 * k, c:c + 1], ALU.add))
                elif kind == "ffn" and not step[3]:
                    ffn(b, step[1], step[2], False)
                elif kind == "ffn":
                    l = (step[1] - 3 * DEPTH) // 2
                    dve.wait_ge(count_ready, l + 1)
                    most = dve.value_load(fullest_i[0:1, 0:1], min_val=0, max_val=S)
                    with dve.If(most <= P):
                        moe(b, step[1], l)
                    with dve.Else():
                        ffn(b, step[1], step[2], True)
                        dve.wait_ge(tr_free, b["u"] + 2 + 2 + MOE_BLOCKS)
                        dve.nop().then_inc(tr_free, MOE_TURNS - MOE_BLOCKS - 2)
                        dve.nop().then_inc(pick_ready, PAIRS)
                elif kind == "resid":
                    k = step[1]
                    dve.wait_ge(tr_free, b["u"] + 2)
                    for t in range(NT):
                        a = flat(acc[:, 2 * t:2 * t + 2, :])
                        if t:
                            dve.wait_ge(x_ready, NT * k + t)
                        if k < 6:
                            dve.wait_ge(rs_done, b["req"] + t + 1)
                            own(dve.scalar_tensor_tensor(tok[:, 1, :], a, rs[:, NT + t:NT + t + 1], tok[:, 0, :],
                                                         ALU.mult, ALU.mult))
                        else:
                            dve.wait_ge(pe_used, b["n"] + PARTS) if t else dve.wait_ge(half_done, k + 1)
                            own(dve.tensor_tensor(tok[:, 1, :], a, tok[:, 0, :], ALU.mult))
                        dve.tensor_tensor(x[:, t, :], x[:, t, :], tok[:, 1, :], ALU.add).then_inc(x_ready, 1)
                elif kind == "proj":
                    for j in range(2, 2 * step[1]):
                        lo(b["n"] + j)
                        if step[1] == 6 and j in (9, 11):
                            t = (j - 9) // 2
                            dve.wait_ge(sq_ready, b["sq"] + t + 1)
                            dve.tensor_reduce(ss[:, 32 * t:32 * t + 32], flat(tok[:]).rearrange("p (h e) -> p h e", e=HD),
                                              AX, ALU.add).then_inc(sq_used if t < NT - 1 else rs_req, 1)
                elif kind == "rope_p":
                    dve.wait_ge(ev_ready, b["ev"])
                    half = ROT // 2
                    for t in range(NT):
                        heads = proj[:, t, 0:1024].rearrange("p (h e) -> p h e", e=HD)
                        c = CONST["cos_p"][0] + t * half
                        cos = const[:, c:c + half].unsqueeze(1).to_broadcast([P, 16, half])
                        c = CONST["sin_p"][0] + t * half
                        sin = const[:, c:c + half].unsqueeze(1).to_broadcast([P, 16, half])
                        rotate(heads[:, :, 0:half], heads[:, :, half:ROT], cos, sin, 16 * half)
                    dve.nop().then_inc(src_ready, 1)
                elif kind == "rope_m":
                    dve.wait_ge(ev_ready, b["ev"])
                    half = ROPE // 2
                    for t in range(NT):
                        c, s_ = CONST["cos_m"][0] + t * half, CONST["sin_m"][0] + t * half
                        kr = proj[:, t, PROJ_W - ROPE:PROJ_W]
                        rotate(kr[:, 0:half], kr[:, half:ROPE], const[:, c:c + half], const[:, s_:s_ + half], half)
                        cos = const[:, c:c + half].unsqueeze(1).to_broadcast([P, NH, half])
                        sin = const[:, s_:s_ + half].unsqueeze(1).to_broadcast([P, NH, half])
                        q = proj[:, t, MQ:MQ + 768].rearrange("p (h e) -> p h e", h=NH)
                        rotate(q[:, :, NOPE:NOPE + half], q[:, :, NOPE + half:QK_C], cos, sin, NH * half)
                        km = proj[:, t, MK:MK + 768].rearrange("p (h e) -> p h e", h=NH)
                        own(dve.tensor_copy(km[:, :, NOPE:QK_C], kr.unsqueeze(1).to_broadcast([P, NH, ROPE])))
                    dve.nop().then_inc(src_ready, 1)
                elif kind == "qkT":
                    rounds = 4 if step[1] == "pairs" else 8
                    rows = QK_C if step[1] == "mla" else P
                    for r in range(rounds):
                        u = b["u"] + r
                        dve.wait_ge(tr_full, u + 1)
                        dst, src = flat(qk[0:rows, 2 * r:2 * r + 2, :]), tr[0:rows, u % 2, :]
                        if step[1] != "wide":
                            dve.tensor_copy(dst, src).then_inc(tr_free, 1)
                        elif r < 4:
                            dve.tensor_scalar(dst, src, col(step[4] + "_q", 0), HD ** -0.5,
                                              ALU.mult, ALU.mult).then_inc(tr_free, 1)
                        else:
                            dve.tensor_scalar(dst, src, col(step[4] + "_k", 0), None, ALU.mult).then_inc(tr_free, 1)
                    if step[2] != 1536:
                        ahead(b["n"])
                elif kind == "soft":
                    which = step[1]
                    heads, mask, scale, out_col = {
                        "moba": (NH, "causal", HD ** -0.5, Y_COL[0]), "mla": (NH, "causal", QK_C ** -0.5, Y_COL[2]),
                        "band": (16, "chunked", 1.0, 0)}[which]
                    inv_at = {}

                    def emit_out(h):
                        s = h % 2
                        dve.wait_ge(o_full, b["ov"] + h + 1)
                        dve.wait_ge(dve_up, inv_at[h])
                        for q in range(NT):
                            ins = dve.tensor_scalar(proj[:, q, out_col + h * HD:out_col + (h + 1) * HD],
                                                    acc[:, s, q * P:q * P + HD], rinv[:, s, q:q + 1], None, ALU.mult)
                        ins.then_inc(o_free, 1)

                    for h in range(heads + 2):
                        if h < heads:
                            soft_max_in(b, h, mask, scale)
                        if 1 <= h <= heads:
                            turn_prob(b, h - 1)
                            ups += 1
                            inv_at[h - 1] = ups
                            if h >= 3:
                                dve.wait_ge(o_free, b["ov"] + h - 2)
                            dve.reciprocal(rinv[:, (h - 1) % 2, :], rsum[:, (h - 1) % 2, :]).then_inc(dve_up, 1)
                        if h >= 2:
                            emit_out(h - 2)
                elif kind == "diff":
                    def combine(h):
                        dve.wait_ge(p_ready, b["pr"] + 2 * h + 2)
                        own(dve.reciprocal(rinv[:], rsum[:]))
                        own(dve.tensor_scalar(rinv[:, 1, :], rinv[:, 1, :], lam_s[:, 0:1], None, ALU.mult))
                        segs = ((0, 128), (128, 384))
                        for q, (lo_, hi_) in enumerate(segs):
                            ins = dve.tensor_scalar(mixp[:, lo_:hi_], prob[:, 1, lo_:hi_], rinv[:, 1, q:q + 1], None,
                                                    ALU.mult)
                        own(ins)
                        for q, (lo_, hi_) in enumerate(segs):
                            ins = dve.scalar_tensor_tensor(mixp[:, lo_:hi_], prob[:, 0, lo_:hi_], rinv[:, 0, q:q + 1],
                                                           mixp[:, lo_:hi_], ALU.mult, ALU.add)
                        ins.then_inc(a_ready, 1)

                    def emit_diff(h):
                        dve.wait_ge(o_full, b["ov"] + h + 1)
                        o = acc[:, h % 2, 0:256].rearrange("p (q e) -> p q e", q=NT)
                        dve.tensor_copy(proj[:, :, h * 128:(h + 1) * 128], o).then_inc(o_free, 1)

                    for h in range(10):
                        if h < 8:
                            if h:
                                dve.wait_ge(a_ready, h)
                            soft_max_in(b, 2 * h, "chunked", 1.0)
                            soft_max_in(b, 2 * h + 1, "chunked", 1.0)
                        if 1 <= h <= 8:
                            turn_prob(b, h - 1)
                        if h >= 2:
                            emit_diff(h - 2)
                        if h < 8:
                            combine(h)
                elif kind == "stick":
                    def take_z(a):
                        s = a % 2
                        dve.wait_ge(s_full, b["sc"] + a + 1)
                        if a >= 2:
                            dve.wait_ge(p_ready, b["pr"] + a - 1)
                        dve.scalar_tensor_tensor(prob[:, s, :], gu[:, s, 0:384], HD ** -0.5, cst("strict"),
                                                 ALU.mult, ALU.add).then_inc(s_free, 1)

                    def emit_stick(a):
                        dve.wait_ge(o_full, b["ov"] + a + 1)
                        o = acc[:, a % 2, 0:256].rearrange("p (q e) -> p q e", q=NT)[:, :, 0:HD]
                        dve.tensor_copy(proj[:, :, Y_COL[1] + a * HD:Y_COL[1] + (a + 1) * HD], o).then_inc(o_free, 1)

                    take_z(0)
                    for a in range(NH):
                        s = a % 2
                        dve.wait_ge(soft_ready, b["st"] + a + 1)
                        dve.scalar_tensor_tensor(tok[:, s, 0:384], prob[:, s, :], 0.0, tok[:, s, 0:384],
                                                 ALU.max, ALU.add).then_inc(sp_ready, 1)
                        if a + 1 < NH:
                            take_z(a + 1)
                        dve.wait_ge(c_full, b["st"] + a + 1)
                        dve.tensor_tensor(prob[:, s, :], prob[:, s, :], acc[:, 2 + s, 0:384],
                                          ALU.subtract).then_inc(arg_ready, 1)
                        if a:
                            emit_stick(a - 1)
                    emit_stick(NH - 1)
                elif kind == "mla_norm":
                    dve.wait_ge(rs_done, b["req"] + 1)
                    c0 = 6 * 512
                    for i, (o, w) in enumerate(((0, QL), (QL, KVL))):
                        for t in range(NT):
                            v = proj[:, t, c0 + o:c0 + o + w]
                            ins = dve.tensor_scalar(v, v, rs[:, 2 * i + t:2 * i + t + 1], None, ALU.mult)
                    ins.then_inc(src_ready, 1)
                elif kind == "mla_T":
                    l = step[1]
                    take_lo(b, 2, yT_hi, yT_lo,
                            lambda c: (col("q_norm", 2 * l + c) if c < 2 else col("kv_norm", l), None, ALU.bypass),
                            (512, 256))
                elif kind == "merge":
                    l = step[1]
                    flat4 = pair[:].rearrange("p a t c -> p a (t c)")

                    def finish(j):
                        n = b["n"] + 3 * j
                        dve.wait_ge(e_ready, b["mg"] + j + 1)
                        dve.wait_ge(pe_used, n + 3 + PARTS)
                        half = tok[:, :, 512 * (j % 2):512 * (j % 2) + 512]
                        br = acc[:, 2 * (j % 2):2 * (j % 2) + 2, :]
                        if j < 2:
                            dve.tensor_tensor(half, flat4, br, ALU.mult).then_inc(mg_ready, 1)
                        else:
                            own(dve.tensor_tensor(flat4, flat4, br, ALU.mult))
                            dve.tensor_tensor(half, half, flat4, ALU.add).then_inc(mg_ready, 1)

                    for j in range(6):
                        n = b["n"] + 3 * j
                        if j:
                            lo(n)
                            finish(j - 1)
                            lo(n + 1)
                        lo(n + 2)
                        if j % 2 == 0:
                            for r in range(2):
                                dve.wait_ge(th_ready, b["th"] + j + r + 1)
                                dve.tensor_tensor(flat(yT_lo[:, 2 * r:2 * r + 2, :]), tr[:, (b["u"] + j + r) % 2, :],
                                                  flat(yT_hi[:, 2 * r:2 * r + 2, :]).bitcast(F32),
                                                  ALU.subtract).then_inc(tr_free, 1)
                        dve.wait_ge(pe_used, n + 2 + PARTS)
                        dve.wait_ge(bg_in[j % 2], 16 * (3 * l + j // 2 + 1))
                        bias = tf[:, j % 2, :].unsqueeze(1).to_broadcast([P, 2, 512])
                        if j:
                            dve.wait_ge(mg_ready, b["mg"] + j)
                        dve.tensor_tensor(flat4, gu[:], bias, ALU.add).then_inc(z_ready, 1)
                    ahead(b["n"] + 18)
                    finish(5)
                elif kind == "backT":
                    if step[1] == "subln":
                        take_lo(b, 4, hT_hi, hT_lo, lambda c: (col("subln", 0), 0.8, ALU.mult))
                    else:
                        take_lo(b, 4, hT_hi, hT_lo)
                elif kind == "out":
                    gate_row(b, step[1], b["u"])
                    lo(b["n"] + 2)
                    lo(b["n"] + 3)
                    ahead(b["n"] + 4)
                elif kind == "head_norm":
                    dve.wait_ge(rs_done, b["req"] + 1)
                    for t in range(NT):
                        v = proj[:, t, 0:2048].rearrange("p (h e) -> p h e", e=HD)
                        f = rs[:, 32 * t:32 * t + 32].unsqueeze(2).to_broadcast([P, 32, HD])
                        ins = dve.tensor_tensor(v, v, f, ALU.mult)
                    ins.then_inc(src_ready, 1)
                elif kind == "out_norm":
                    dve.wait_ge(sq_ready, b["sq"] + 1)
                    dve.tensor_reduce(ss[:, 0:16], flat(tok[:]).rearrange("p (h e) -> p h e", e=128), AX,
                                      ALU.add).then_inc(rs_req, 1)
                    dve.wait_ge(rs_done, b["req"] + 1)
                    for t in range(NT):
                        v = proj[:, t, 0:D].rearrange("p (h e) -> p h e", e=128)
                        f = rs[:, 8 * t:8 * t + 8].unsqueeze(2).to_broadcast([P, 8, 128])
                        ins = dve.tensor_tensor(v, v, f, ALU.mult)
                    ins.then_inc(src_ready, 1)
                elif kind == "route":
                    R = NT * EXP
                    sc, sel, key, oh1, oh2, cmp_ = (rt[:, i, 0:R] for i in (0, 1, 2, 3, 4, 5))
                    small = rt[:, 6, :]
                    pairs = rt[:, 7, :]

                    def by_t(v, w=EXP):
                        return v.rearrange("p (t e) -> p t e", t=NT)

                    def over(v, w):
                        return v.unsqueeze(2).to_broadcast([P, v.shape[1], w])

                    dve.wait_ge(th_ready, b["th"] + 1)
                    dve.tensor_scalar(sc, sc, 1.0, None, ALU.add).then_inc(tr_free, 1)
                    dve.wait_ge(tr_free, b["u"] + 1 + 2)
                    own(dve.reciprocal(sc, sc))
                    own(dve.tensor_tensor(by_t(sel), by_t(sc), rbias[:].unsqueeze(1).to_broadcast([P, NT, EXP]), ALU.add))
                    s4 = sel.rearrange("p (g e) -> p g e", e=4)
                    best, tmp3 = small[:, 0:8], pairs[:, 0:24].rearrange("p (g e) -> p g e", e=3)
                    tmp2 = key[:, 0:16].rearrange("p (g e) -> p g e", e=2)
                    dve.tensor_tensor(tmp3, s4[:, :, 0:3], s4[:, :, 1:4], ALU.add)
                    own(dve.tensor_tensor(tmp2, s4[:, :, 0:2], s4[:, :, 2:4], ALU.add))
                    dve.tensor_reduce(best, tmp3, AX, ALU.max)
                    own(dve.tensor_reduce(small[:, 8:16], tmp2, AX, ALU.max))
                    own(dve.tensor_tensor(best, best, small[:, 8:16], ALU.max))
                    last = small[:, 8:16].unsqueeze(2)
                    own(dve.tensor_tensor(last, s4[:, :, 0:1], s4[:, :, 3:4], ALU.add))
                    own(dve.tensor_tensor(best, best, small[:, 8:16], ALU.max))

                    def first_of_max(v, ranks, w, onehot, m):
                        v3 = v.rearrange("p (t e) -> p t e", t=NT)
                        k3 = key[:, 0:NT * w].rearrange("p (t e) -> p t e", t=NT)
                        o3 = onehot.rearrange("p (t e) -> p t e", t=NT)
                        own(dve.tensor_reduce(m, v3, AX, ALU.max))
                        own(dve.tensor_tensor(k3, v3, over(m, w), ALU.is_equal))
                        own(dve.tensor_tensor(key[:, 0:NT * w], key[:, 0:NT * w], ranks, ALU.mult))
                        own(dve.tensor_reduce(m, k3, AX, ALU.max))
                        own(dve.tensor_tensor(o3, k3, over(m, w), ALU.is_equal))

                    gm = small[:, 8:16]
                    first_of_max(best, cst("grank"), GROUPS, gm, small[:, 16:18])
                    s4m = cmp_.rearrange("p (g e) -> p g e", e=4)
                    own(dve.tensor_tensor(s4m, s4, over(gm, 4), ALU.mult))
                    own(dve.tensor_scalar(gm, gm, BIG, -BIG, ALU.mult, ALU.add))
                    own(dve.tensor_tensor(s4m, s4m, over(gm, 4), ALU.add))
                    first_of_max(cmp_, cst("rank"), EXP, oh1, small[:, 16:18])
                    own(dve.scalar_tensor_tensor(cmp_, oh1, -3 * BIG, cmp_, ALU.mult, ALU.add))
                    first_of_max(cmp_, cst("rank"), EXP, oh2, small[:, 16:18])
                    own(dve.tensor_tensor(oh1, oh1, oh2, ALU.add))
                    dve.nop().then_inc(sent_ready, 1)
                    own(dve.tensor_tensor(sc, sc, oh1, ALU.mult))
                    own(dve.tensor_reduce(small[:, 16:18], by_t(sc), AX, ALU.add))
                    own(dve.reciprocal(small[:, 16:18], small[:, 16:18]))
                    own(dve.tensor_tensor(gates[:], by_t(sc), over(small[:, 16:18], EXP), ALU.mult))
                    u = b["u"] + 1
                    dve.wait_ge(tr_full, u + 1)
                    rank_f = rank[:].rearrange("p t e -> p (t e)")
                    dve.tensor_reduce(fullest[:], tr[:, u % 2, R:R + EXP], AX, ALU.max)
                    own(dve.scalar_tensor_tensor(rank_f, tr[:, u % 2, 0:R], 1.0, oh1, ALU.add, ALU.mult))
                    dve.tensor_scalar(rank_f, rank_f, -1.0, None, ALU.add).then_inc(tr_free, 1)
                    dve.tensor_copy(fullest_i[:], fullest[:]).then_inc(count_ready, 1)

        @block.tensor
        def _(pe):
            def mm3(dst, l_hi, l_lo, r_hi, r_lo, start, stop):
                pe.matmul(dst, l_hi, r_hi, start=start, stop=False, skip_group_check=True)
                pe.matmul(dst, l_hi, r_lo, start=False, stop=False, skip_group_check=True)
                return pe.matmul(dst, l_lo, r_hi, start=False, stop=stop, skip_group_check=True)

            def chunk_wait(n, i=0, rounds=1):
                pe.wait_ge(chunk_ready, n + 1 + STAGES * rounds * i)

            def columns(n, dst, k0, kts, first, last, width=512, src=(hT_hi, hT_lo), i=0, pitch=512):
                chunk_wait(n, i)
                s = n % PARTS
                for t in range(NT):
                    for k in range(kts):
                        c = slice(k * pitch, k * pitch + width)
                        lhs = [v[:, k0 + k, t * P:(t + 1) * P] for v in src]
                        ins = mm3(dst(t), lhs[0], lhs[1], w_hi[:, s, c], w_lo[:, s, c], first and k == 0, last and k == kts - 1)
                ins.then_inc(pe_used, 1)

            def rows(n, lhs, first, last, i=0, rounds=1):
                chunk_wait(n, i, rounds)
                s = n % PARTS
                for t in range(NT):
                    for k in range(2):
                        l_hi, l_lo = lhs(k, t)
                        for h in range(2):
                            c = slice(k * D + h * 512, k * D + (h + 1) * 512)
                            ins = mm3(acc[:, 2 * t + h, :], l_hi, l_lo, w_hi[:, s, c], w_lo[:, s, c],
                                      first and k == 0, last and k == 1)
                    if last and t == 0:
                        ins.then_inc(half_done, 1)
                ins.then_inc(pe_used, 1)

            def turn(u, srcs, i=0, per=0):
                pe.wait_ge(tr_free, u + 1 + per * i)
                for j, src in enumerate(srcs):
                    rows_ = src.shape[-1]
                    ins = pe.transpose(tr[0:rows_, u % 2, j * P:(j + 1) * P], src, ident)
                ins.then_inc(tr_full, 1)

            def gate_row(b, u):
                for r in range(2):
                    pe.wait_ge(tf_ready, b["tf"] + r + 1)
                    pe.wait_ge(tr_free, u + r + 1)
                    pe.matmul(tr[:, (u + r) % 2, :], ones, tf[:, (b["tf"] + r) % 2, :], start=True,
                              stop=True).then_inc(tr_full, 1)

            def ffn(b, nb, k=None):
                peeled, turns = block_order(nb)
                n0, g0 = b["n"], b["hid"]
                u_of, u_unit, per_turn = ffn_order(b["u"], k is not None)

                def up(n, half, g, i=0):
                    if half == 0:
                        pe.wait_ge(hid_ready, g0 + g + 2 * i)
                    columns(n, lambda t: gu[:, t, :], 4 * half, 4, half == 0, half == 1, i=i)

                def turn_hidden(g, i=0):
                    hid = pair[:, 1]
                    pe.wait_ge(hid_ready, g0 + g + 1 + 2 * i)
                    turn(u_of(g), [hid[:, t, c * P:(c + 1) * P] for c in range(2) for t in range(NT)], i, per_turn)

                def down(n, g, first=False, last=False, i=0):
                    pe.wait_ge(tr_free, u_of(g) + 1 + 2 + per_turn * i)
                    rows(n, lambda k, t: tuple(v[:, (2 * k + t) * P:(2 * k + t + 1) * P] for v in (hid_hi, hid_lo)),
                         first, last, i)

                def sum_unit(g, i=0):
                    unit, u = unit_base[k] + g - 2, u_unit(g)
                    pe.wait_ge(slice_sum, SLICES * (unit + 1) + 2 * SLICES * i)
                    pe.wait_ge(tr_free, u + 1 + per_turn * i)
                    for j in range(UC):
                        ins = pe.matmul(tr[:, u % 2, j:j + 1], ada_acc[:, unit % 2, j * P:(j + 1) * P], ones[:, 0:1],
                                        start=True, stop=True)
                    ins.then_inc(tr_full, 1)

                def block_(g, i=0):
                    up(n0 + 3 * g - 1, 0, g, i)
                    turn_hidden(g - 1, i)
                    if k is not None and g >= 3:
                        sum_unit(g - 1, i)
                    up(n0 + 3 * g, 1, g, i)
                    down(n0 + 3 * g + 1, g - 1, isinstance(i, int) and g == 1, False, i)

                for half in range(2):
                    pe.wait_ge(tr_free, b["u"] + 2 * half)
                    up(n0 + half, half, 0)
                gate_row(b, b["u"])
                for g in range(1, 1 + peeled):
                    block_(g)
                with pe.Fori(0, turns) as i:
                    block_(1 + peeled, i)
                    block_(2 + peeled, i)
                turn_hidden(nb - 1)
                if k is not None:
                    sum_unit(nb - 1)
                down(n0 + 3 * nb - 1, nb - 1, False, True)

            def moe(b, l):
                n0, g0 = b["n"], b["hid"]
                gather_u, scatter_u = moe_order(b["u"] + 2 + 8, 13)

                def gather(p, r, i=0):
                    u = gather_u(p, r)
                    if r == KT:
                        turn(u, [pickg[:, t, e * P:(e + 1) * P] for e in range(2) for t in range(NT)], i, 26)
                        return
                    if r == 0:
                        pe.wait_ge(pick_ready, l * PAIRS + p + 1 + 2 * i)
                    pe.wait_ge(tr_free, u + 1 + 26 * i)
                    for part, h in enumerate((h_hi, h_lo)):
                        for t in range(NT):
                            ins = pe.matmul(tr[:, u % 2, part * S:(part + 1) * S], h[:, t, r * P:(r + 1) * P],
                                            pick[:, t, :], start=(t == 0), stop=(t == NT - 1), skip_group_check=True)
                    ins.then_inc(tr_full, 1)

                def up(g, half, i=0):
                    p, n = g // 4, (n0 if g == 0 else n0 + 3 * g - 1) + half
                    if half == 0:
                        if g % 4 == 0:
                            pe.wait_ge(tr_free, gather_u(p, KT) + 1 + 2 + 26 * i)
                        if not isinstance(i, int) or g >= 2:
                            pe.wait_ge(hid_ready, g0 + g - 1 + 8 * i)
                    chunk_wait(n, i, 4)
                    slots = slice((g // 2 % 2) * P, (g // 2 % 2 + 1) * P)
                    src_hi, src_lo = gathered[p % 2]
                    for k in range(4):
                        c = slice(k * 512, (k + 1) * 512)
                        ins = mm3(gu[:, g % 2, :], src_hi[:, 4 * half + k, slots], src_lo[:, 4 * half + k, slots],
                                  w_hi[:, n % PARTS, c], w_lo[:, n % PARTS, c], half == 0 and k == 0, half == 1 and k == 3)
                    ins.then_inc(pe_used, 1)

                def scatter(g, i=0):
                    u = scatter_u(g)
                    pe.wait_ge(hid_ready, g0 + g + 1 + 8 * i)
                    pe.wait_ge(tr_free, u + 1 + 26 * i)
                    e = g // 2 % 2
                    for k in range(2):
                        ins = pe.matmul(tr[:, u % 2, k * S:(k + 1) * S], pair[:, 1, g % 2, k * P:(k + 1) * P],
                                        pickT[:, (g // 4) % 2, e * S:(e + 1) * S], start=True, stop=True)
                    ins.then_inc(tr_full, 1)

                def down(g, first=False, last=False, i=0):
                    pe.wait_ge(tr_free, scatter_u(g) + 1 + 2 + 26 * i)
                    n = n0 + 3 * g + (4 if g < MOE_BLOCKS - 1 else 2)
                    rows(n, lambda k, t: tuple(v[:, (2 * k + t) * P:(2 * k + t + 1) * P] for v in (hid_hi, hid_lo)),
                         first, last, i, 4)

                def pair_of(p, i=0):
                    for j in range(4):
                        g = 4 * p + j
                        up(g, 0, i)
                        if g:
                            scatter(g - 1, i)
                        up(g, 1, i)
                        if p < PAIRS - 1:
                            for r in (2 * j, 2 * j + 1) + ((KT,) if j == 3 else ()):
                                gather(p + 1, r, i)
                        if g:
                            down(g - 1, g == 1, False, i)

                gate_row(b, b["u"])
                for r in range(8):
                    part, t, half = r // 4, r // 2 % 2, r % 2
                    src = (hT_hi, hT_lo)[part]
                    turn(b["u"] + 2 + r, [src[:, 4 * half + k, t * P:(t + 1) * P].bitcast(F32) for k in range(4)])
                for r in range(KT + 1):
                    gather(0, r)
                pair_of(0)
                with pe.Fori(0, (PAIRS - 2) // 2) as i:
                    pair_of(1, i)
                    pair_of(2, i)
                pair_of(PAIRS - 1)
                scatter(MOE_BLOCKS - 1)
                down(MOE_BLOCKS - 1, False, True)

            def small_mm(dst, lhs, rhs, start=True, stop=True):
                return pe.matmul(dst, lhs, rhs, start=start, stop=stop, skip_group_check=True)

            def value_mm(b, h, pT, v, width):
                if h >= 2:
                    pe.wait_ge(o_free, b["ov"] + h - 1)
                o = acc[:, h % 2, :]
                small_mm(o[:, 0:width], pT[:, 0:128], v(0))
                small_mm(o[:, P:P + width], pT[:, 128:256], v(0), True, False)
                small_mm(o[:, P:P + width], pT[:, 256:384], v(1), False, True).then_inc(o_full, 1)

            pe.nop().then_inc(pe_used, PARTS)
            pe.nop().then_inc(ada_sum, 2)
            pe.wait_ge(ld, 16 * 8)
            pe.matmul(tr[0:8, 0, :], t5[:], t5hot, start=True, stop=True).then_inc(t5_mm, 1)
            for unit in range(FIRST_UNITS):
                pe.wait_ge(slice_sum, SLICES * (unit + 1))
                for j in range(UC):
                    at = unit * UC + j
                    ins = pe.matmul(acc[:, 0, at:at + 1], ada_acc[:, unit % 2, j * P:(j + 1) * P], ones[:, 0:1],
                                    start=True, stop=True)
                ins.then_inc(ada_sum, 1)
            pe.wait_ge(t5_sb, 1)

            for step, b in plan:
                kind = step[0]
                if kind == "norm":
                    pe.wait_ge(src_ready, b["src"] + 1)
                    for r in range(4):
                        turn(b["u"] + r, [tok[:, t, (2 * r + k) * P:(2 * r + k + 1) * P] for k in range(2) for t in range(NT)])
                elif kind == "ffn" and not step[3]:
                    ffn(b, step[2], step[1])
                elif kind == "ffn":
                    l = (step[1] - 3 * DEPTH) // 2
                    pe.wait_ge(count_ready, l + 1)
                    most = pe.value_load(fullest_i[0:1, 0:1], min_val=0, max_val=S)
                    with pe.If(most <= P):
                        moe(b, l)
                    with pe.Else():
                        ffn(b, step[2])
                        pe.wait_ge(tr_full, b["u"] + 2 + MOE_BLOCKS)
                        pe.nop().then_inc(tr_full, MOE_TURNS - MOE_BLOCKS - 2)
                elif kind == "proj":
                    for j in range(step[1]):
                        if j >= 2:
                            pe.wait_ge(ev_ready, b["ev"] + j - 1)
                        w = 512 if j < 6 else PROJ_W - 6 * 512
                        for half in range(2):
                            if j == 0:
                                pe.wait_ge(tr_free, b["u"] + 2 * half)
                            columns(b["n"] + 2 * j + half, lambda t: acc[:, 2 * (j % 2) + t, 0:w], 4 * half, 4,
                                    half == 0, half == 1, w)
                elif kind == "qkT":
                    pe.wait_ge(src_ready, b["src"])
                    pe.wait_ge(ev_ready, b["ev"])
                    _, how, q0, k0, _ = step
                    w = QK_C if how == "mla" else P
                    nq = 4 if how == "pairs" else 8
                    cols = [q0 + w * j for j in range(nq)] + [k0 + w * j for j in range(nq)]
                    for r in range(nq):
                        turn(b["u"] + r, [proj[:, t, c:c + w] for c in cols[2 * r:2 * r + 2] for t in range(NT)])
                elif kind in ("soft", "diff", "stick"):
                    which = step[1] if kind == "soft" else kind
                    heads = {"band": 16, "diff": 16}.get(which, NH)
                    nq = 4 if which in ("moba", "stick") else 8

                    def head(a):
                        if which == "mla":
                            return qk[0:QK_C, a, :], qk[0:QK_C, nq + a, :]
                        p = slice(HD * (a % 2), HD * (a % 2) + HD)
                        return qk[p, a // 2, :], qk[p, nq + a // 2, :]

                    def scores(a):
                        q, k = head(a)
                        s = gu[:, a % 2, :]
                        biased = which in ("band", "diff")
                        if a == 0:
                            pe.wait_ge(tr_free, b["u"] + 2)
                        if a >= 2:
                            pe.wait_ge(s_free, b["sc"] + a - 1)
                        if which == "band" or (which == "diff" and a % 2 == 0):
                            h = a if which == "band" else a // 2
                            before = (4 if which == "band" else 0) + h // 2 + 1
                            pe.wait_ge(bias_ld[h % 2], 32 * before)
                        for qt, (o, w) in enumerate(((0, 128), (128, 256))):
                            ins = small_mm(s[:, o:o + w], q[:, qt * P:(qt + 1) * P], k[:, 0:w], True, not biased)
                            if biased:
                                h = a if which == "band" else a // 2
                                ins = small_mm(s[:, o:o + w], flip, bias_in[:, h % 2, o:o + w], False, True)
                        ins.then_inc(s_full, 1)

                    def scores_T(a):
                        q, k = head(a)
                        s = gu[:, a % 2, :]
                        if a == 0:
                            pe.wait_ge(tr_free, b["u"] + 2)
                        if a >= 2:
                            pe.wait_ge(s_free, b["sc"] + a - 1)
                        small_mm(s[:, 0:256], k[:, 0:P], q[:, 0:S])
                        small_mm(s[:, 256:384], k[:, P:S], q[:, P:S]).then_inc(s_full, 1)

                    def values(c0, width):
                        return lambda h: (lambda kt: proj[:, kt, c0 + h * width:c0 + (h + 1) * width])

                    if which == "stick":
                        v = values(2560, HD)

                        def suffix(a):
                            sp = tok[:, a % 2, 0:384]
                            c = acc[:, 2 + a % 2, :]
                            pe.wait_ge(sp_ready, b["st"] + a + 1)
                            if a >= 2:
                                pe.wait_ge(arg_ready, b["st"] + a - 1)
                            small_mm(c[:, 256:384], tri, sp[:, 256:384])
                            small_mm(c[:, 0:256], tri, sp[:, 0:256], True, False)
                            small_mm(c[:, 128:256], ones, sp[:, 256:384], False, True).then_inc(c_full, 1)

                        def stick_out(a):
                            pe.wait_ge(p_ready, b["pr"] + a + 1)
                            value_mm(b, a, probT[:, a % 2, :], v(a), HD)

                        scores_T(0)
                        for a in range(NH):
                            if a + 1 < NH:
                                scores_T(a + 1)
                            suffix(a)
                            if a:
                                stick_out(a - 1)
                        stick_out(NH - 1)
                    else:
                        v = {"moba": values(1024, HD), "mla": lambda h: (lambda kt: proj[:, kt, mla_value_col(h):mla_value_col(h) + HD]), "band": values(2048, HD),
                             "diff": values(2048, 128)}[which]
                        width = 128 if which == "diff" else HD

                        def turn_head(h):
                            if which == "diff":
                                pe.wait_ge(a_ready, h + 1)
                                p = mixp
                                src = [p[:, j * P:(j + 1) * P] for j in range(3)]
                            else:
                                pe.wait_ge(p_ready, b["pr"] + h + 1)
                                src = [prob[:, h % 2, j * P:(j + 1) * P] for j in range(3)]
                            turn(b["u"] + h, src)

                        def out_head(h):
                            pe.wait_ge(tr_free, b["u"] + h + 1 + 2)
                            value_mm(b, h, probT[:, h % 2, :], v(h), width)

                        if which == "diff":
                            for h in range(10):
                                if h < 8:
                                    scores(2 * h)
                                    scores(2 * h + 1)
                                if 1 <= h <= 8:
                                    turn_head(h - 1)
                                if h >= 2:
                                    out_head(h - 2)
                        else:
                            for h in range(heads + 2):
                                if h < heads:
                                    scores(h)
                                if 1 <= h <= heads:
                                    turn_head(h - 1)
                                if h >= 2:
                                    out_head(h - 2)
                elif kind == "mla_T":
                    pe.wait_ge(src_ready, b["src"])
                    c0 = 6 * 512
                    turn(b["u"], [proj[:, t, c0 + k * P:c0 + (k + 1) * P] for k in range(2) for t in range(NT)])
                    turn(b["u"] + 1, [proj[:, t, c0 + QL:c0 + QL + P] for t in range(NT)])
                elif kind == "mla_up":
                    n = b["n"]
                    pe.wait_ge(tr_free, b["u"] + 2)
                    pe.wait_ge(o_free, b["ov"])
                    wide = acc[:].rearrange("p (t a) c -> p t a c", t=NT)
                    chunk_wait(n)
                    s = n % PARTS
                    for t in range(NT):
                        for h, w in ((0, 512), (1, 256)):
                            for k in range(2):
                                c = slice(k * 768 + h * 512, k * 768 + h * 512 + w)
                                ins = mm3(wide[:, t, h, 0:w], yT_hi[:, k, t * P:(t + 1) * P], yT_lo[:, k, t * P:(t + 1) * P],
                                          w_hi[:, s, c], w_lo[:, s, c], k == 0, k == 1)
                    ins.then_inc(pe_used, 1)
                    chunk_wait(n + 1)
                    s = (n + 1) % PARTS
                    pe.wait_ge(ev_ready, b["ev"] + 1)
                    for t in range(NT):
                        for h in range(2):
                            c = slice(h * 512, h * 512 + 512)
                            ins = mm3(wide[:, t, h, :], yT_hi[:, 2, t * P:(t + 1) * P], yT_lo[:, 2, t * P:(t + 1) * P],
                                      w_hi[:, s, c], w_lo[:, s, c], True, True)
                    ins.then_inc(pe_used, 1)
                elif kind == "merge":
                    pe.wait_ge(o_free, b["ov"])
                    for j in range(6):
                        n = b["n"] + 3 * j
                        if j % 2 == 0:
                            for r in range(2):
                                c0 = Y_COL[j // 2] + 2 * r * P
                                turn(b["u"] + j + r, [proj[:, t, c0 + k * P:c0 + (k + 1) * P] for k in range(2) for t in range(NT)])
                        if j:
                            pe.wait_ge(z_ready, b["mg"] + j)
                        columns(n, lambda t: gu[:, t, :], 0, 4, True, False)
                        columns(n + 1, lambda t: gu[:, t, :], 4, 4, False, True)
                        if j >= 2:
                            pe.wait_ge(mg_ready, b["mg"] + j - 1)
                        pe.wait_ge(tr_free, b["u"] + 2 * (j // 2 + 1) + 2)
                        columns(n + 2, lambda t: acc[:, 2 * (j % 2) + t, :], 0, 4, True, True, src=(yT_hi, yT_lo))
                elif kind == "backT":
                    src = tok if step[1] == "merged" else proj
                    pe.wait_ge(mg_ready, b["mg"]) if step[1] == "merged" else pe.wait_ge(o_free, b["ov"])
                    if step[1] == "subln":
                        pe.wait_ge(src_ready, b["src"])
                    for r in range(4):
                        turn(b["u"] + r, [src[:, t, (2 * r + k) * P:(2 * r + k + 1) * P] for k in range(2) for t in range(NT)])
                elif kind == "out":
                    for c in range(4):
                        pe.wait_ge(tr_free, b["u"] + c - 1)
                        rows(b["n"] + c, lambda k, t: tuple(v[:, 2 * c + k, t * P:(t + 1) * P] for v in (hT_hi, hT_lo)),
                             c == 0, c == 3)
                        if c == 1:
                            gate_row(b, b["u"])
                elif kind == "route":
                    pe.wait_ge(rw_ready, 1)
                    pe.wait_ge(tr_free, b["u"] + 2)
                    for t in range(NT):
                        for k in range(KT):
                            ins = mm3(tr[:, b["u"] % 2, t * EXP:(t + 1) * EXP], hT_hi[:, k, t * P:(t + 1) * P],
                                      hT_lo[:, k, t * P:(t + 1) * P], rw_hi[:, k * EXP:(k + 1) * EXP],
                                      rw_lo[:, k * EXP:(k + 1) * EXP], k == 0, k == KT - 1)
                    ins.then_inc(tr_full, 1)
                    l = step[1]
                    pe.wait_ge(sent_ready, l + 1)
                    pe.wait_ge(tr_free, b["u"] + 2)
                    bank, sent, before = tr[:, (b["u"] + 1) % 2, :], rt[:, 3, :], cst("before")
                    s0, s1 = sent[:, 0:EXP], sent[:, EXP:2 * EXP]
                    for dst, terms in ((0, ((before, s0),)), (EXP, ((before, s1), (ones, s0))),
                                       (2 * EXP, ((ones, s0), (ones, s1)))):
                        for j, (lhs, rhs) in enumerate(terms):
                            ins = small_mm(bank[:, dst:dst + EXP], lhs, rhs, j == 0, j == len(terms) - 1)
                    ins.then_inc(tr_full, 1)


def constants():
    c = np.zeros((P, N_CONST), np.float32)

    def put(name, v):
        c[:, CONST[name][0]:CONST[name][1]] = np.asarray(v, np.float32).reshape(P, -1)

    r = np.arange(P)
    put("ident", np.eye(P))
    put("flip", np.eye(P)[::-1])
    put("ones", np.ones((P, P)))
    put("tri", (r[:, None] >= r[None, :]))
    put("before", (r[:, None] < r[None, :]))
    put("slots", np.tile(r, (P, 1)))
    keep = r[None, :] <= r[:, None]
    put("causal", np.where(np.concatenate([keep, np.ones((P, P), bool), keep], 1), 0.0, -BIG))
    keep = r[:, None] < r[None, :]
    put("strict", np.where(np.concatenate([keep, np.ones((P, P), bool), keep], 1), 0.0, -BIG))
    keep = (r[None, :] // BAND_CHUNK) <= (r[:, None] // BAND_CHUNK)
    put("chunked", np.where(np.concatenate([keep, np.ones((P, P), bool), keep], 1), 0.0, -BIG))
    for name, rot in (("p", ROT), ("m", ROPE)):
        inv = np.power(np.float32(THETA), -np.arange(0, rot, 2, dtype=np.float32) / np.float32(rot)).astype(np.float32)
        ang = np.arange(S, dtype=np.float32)[:, None] * inv[None, :]
        for f, fn in (("cos", np.cos), ("sin", np.sin)):
            put(f"{f}_{name}", fn(ang).astype(np.float32).reshape(NT, P, rot // 2).transpose(1, 0, 2))
    put("rank", np.tile(np.arange(EXP, 0, -1), (P, NT)))
    put("grank", np.tile(np.arange(GROUPS, 0, -1), (P, NT)))
    rel = np.arange(512) - 256
    n = np.abs(rel)
    large = 8 + (np.log(np.maximum(n, 1).astype(np.float32) / np.float32(8)) / math.log(1024 / 8) * 8).astype(np.int32)
    bucket = np.where(rel > 0, 16, 0) + np.where(n < 8, n, np.minimum(large, 15))
    return c, (np.arange(32)[:, None] == bucket[None, :]).astype(np.float32)


def weight_stream(a):
    n_chunks = make_plan()[-1][1]["n"]
    w = np.zeros((n_chunks, P, CW), np.float32)
    at = 0

    def tiles(m, kt, width):
        return m.reshape(kt, P, width).transpose(1, 0, 2)

    def add(block, pitch=None):
        nonlocal at
        kt, width = block.shape[1], block.shape[2]
        pitch = pitch or width
        w[at].reshape(P, CW)[:, :kt * pitch].reshape(P, kt, pitch)[:, :, :width] = block
        at += 1

    def ffn(blocks):
        held = None
        for g, u, d in blocks:
            for half in range(2):
                r = slice(512 * half, 512 * half + 512)
                add(np.concatenate([tiles(g[r], 4, BLK), tiles(u[r], 4, BLK)], 2))
            if held is not None:
                add(held)
            held = tiles(d, 2, D)
        add(held)

    def dense_ffn(l, s):
        ffn((a["ffn_w_gate"][l, s][:, c:c + BLK], a["ffn_w_up"][l, s][:, c:c + BLK], a["ffn_w_down"][l, s][c:c + BLK])
            for c in range(0, FF, BLK))

    def col_blocks(m, width=512):
        for half in range(2):
            add(tiles(m[512 * half:512 * half + 512], 4, width), 512)

    for l in range(DEPTH):
        dense_ffn(l, 0)
        w_in = a["mix_w_in"][l]
        for j in range(6):
            col_blocks(w_in[:, 512 * j:512 * j + 512])
        col_blocks(w_in[:, 3072:PROJ_W], PROJ_W - 3072)
        add(tiles(a["mla_w_uq"][l], 2, 768))
        add(tiles(a["mla_w_ukv"][l], 1, 1024))
        for n in range(3):
            for half in range(2):
                c = PROJ_W + n * D + half * 512
                col_blocks(w_in[:, c:c + 512])
                add(tiles(a["mix_w_branch"][l, n][:, half * 512:half * 512 + 512], 4, 512))
        for c in range(4):
            add(tiles(a["mix_w_out"][l][256 * c:256 * c + 256], 2, D))
        dense_ffn(l, 1)
    for l, which in enumerate("ab"):
        for j in range(6):
            col_blocks(a[f"{which}_w_qkv_2"][0][:, 512 * j:512 * j + 512])
        for c in range(4):
            add(tiles(a[f"{which}_w_o_2"][0][256 * c:256 * c + 256], 2, D))
        ffn((a["moe_w_gate_2"][l, e][:, c:c + BLK], a["moe_w_up_2"][l, e][:, c:c + BLK], a["moe_w_down_2"][l, e][c:c + BLK])
            for e in range(EXP) for c in range(0, EF, BLK))
    assert at == n_chunks, (at, n_chunks)
    return w


def modulation_stream(a):
    w = np.concatenate([a[name][l] for name in ("ada_w", "ada_w_2") for l in range(DEPTH)], 1)
    w = w.reshape(SLICES, 2, P, UNITS, UW).transpose(3, 0, 2, 1, 4)
    return w.reshape(UNITS * SLICES, P, 2 * UW)


def column_vectors(a):
    v = np.zeros((P, N_VEC), np.float32)

    def put(name, *parts):
        cols = np.concatenate([np.asarray(p).reshape(-1, P).T for p in parts], 1)
        v[:, VEC[name][0]:VEC[name][1]] = cols

    put("c", a["c"])
    put("c_2", a["c_2"])
    put("ada_b", a["ada_b"], a["ada_b_2"])
    second = [p for l in range(DEPTH) for p in (a["norm_mix_g_2"][l], a["norm_ffn_g_2"][l])]
    put("pre", a["norm_pre"], *second)
    put("post", a["norm_post"])
    put("q_norm", a["mla_q_norm"])
    put("kv_norm", a["mla_kv_norm"])
    for name, src in (("a_q", "a_q_gain_2"), ("a_k", "a_k_gain_2"), ("b_q", "b_q_gain_2"), ("b_k", "b_k_gain_2")):
        put(name, np.tile(a[src][0], 2))
    put("subln", a["a_subln_g_2"])
    return v


def kernel(**inputs):
    import concourse.bacc as _bacc
    from concourse.bass_utils import run_bass_kernel_spmd as _run

    a = {k: np.asarray(v) for k, v in inputs.items()}
    const, t5hot = constants()
    rw = a["router_w_2"].reshape(KT, P, EXP).transpose(1, 0, 2).reshape(P, KT * EXP)
    arrays = {
        "wstream": weight_stream(a), "ada_stream": modulation_stream(a), "x_in": a["x"][0], "const_in": const, "vec_in": column_vectors(a),
        "bgate_in": a["mix_b_gate"].reshape(DEPTH, 3 * D), "lam_in": a["a_lambda_2"].reshape(4 * HD),
        "rbias_in": a["router_bias_2"], "t5_in": a["t5_bias_2"], "t5hot_in": t5hot, "rel_in": a["b_rel_bias_2"][0],
        "rw_in": rw,
    }
    arrays = {k: np.ascontiguousarray(v) for k, v in arrays.items()}
    nc = _bacc.Bacc("TRN2", target_bir_lowering=False, num_devices=1)
    aps = [nc.dram_tensor(k, v.shape, mybir.dt.from_np(v.dtype), kind="ExternalInput").ap() for k, v in arrays.items()]
    out = nc.dram_tensor("x_out", (S, D), F32, kind="ExternalOutput").ap()
    build(nc, *aps, out)
    r = _run(nc, [arrays], core_ids=[0])
    return r.results[0]["x_out"].reshape(1, S, D)
```

```python
from contextlib import ExitStack
import math

import numpy as np
import concourse.bass as bass
from concourse import mybir

F32 = mybir.dt.float32
F32R = mybir.dt.float32r
ACT = mybir.ActivationFunctionType
ALU = mybir.AluOpType
AX = mybir.AxisListType.X

P = 128
S = 256
NT = S // P
D = 1024
KT = D // P
DEPTH = 2
FF = 2816
HD = 64
NH = 8
W_BR = NH * HD
QL, KVL, ROPE, NOPE = 256, 128, 32, 64
QK_C = NOPE + ROPE
ROT = HD // 4
THETA = 500000.0
EXP, EF = 16, 512
GROUPS = 4
BAND_CHUNK = 64
EPS = 1e-6
BIG = 1e30
BLK = 256
CW = 2048

STAGES = 6
PARTS = 3
NVEC = DEPTH * 9 + DEPTH * 6
UW = 768
UC = UW // P
UNITS = NVEC * D // UW
FIRST_UNITS = 3 * D // UW
SLICES = 4
FFN_UNITS = 9
NSUB = DEPTH * 3 + DEPTH * 2
FFN_BLOCKS = FF // BLK
MOE_BLOCKS = EXP * EF // BLK
PROJ_W = 6 * 512 + QL + KVL + ROPE

Y_COL = (0, 1536, 512)
MQ, MK = 512, 2048


def mla_value_col(h):
    return (MQ if h < 4 else MK) + NH * QK_C + (h % 4) * HD



CONST = {}
_at = 0
for _name, _w in (("ident", P), ("flip", P), ("ones", P), ("tri", P), ("before", P), ("slots", P), ("causal", 384), ("strict", 384), ("chunked", 384),
                  ("cos_p", NT * 8), ("sin_p", NT * 8), ("cos_m", NT * 16), ("sin_m", NT * 16),
                  ("rank", NT * EXP), ("grank", NT * GROUPS)):
    CONST[_name] = (_at, _at + _w)
    _at += _w
N_CONST = _at
VEC = {}
_at = 0
for _name, _w in (("c", KT), ("c_2", KT), ("ada_b", NVEC * KT), ("pre", NSUB * KT), ("post", DEPTH * 3 * KT),
                  ("q_norm", DEPTH * 2), ("kv_norm", DEPTH), ("a_q", 1), ("a_k", 1), ("subln", 1), ("b_q", 1), ("b_k", 1)):
    VEC[_name] = (_at, _at + _w)
    _at += _w
N_VEC = _at


def make_plan():
    steps = []
    for l in range(DEPTH):
        steps += [("norm", 3 * l), ("ffn", 3 * l, FFN_BLOCKS, None), ("resid", 3 * l)]
        k = 3 * l + 1
        steps += [("norm", k), ("proj", 7), ("rope_p",),
                  ("qkT", "pairs", 0, 512, None), ("soft", "moba"),
                  ("qkT", "pairs", 1536, 2048, None), ("stick",),
                  ("mla_norm", l), ("mla_T", l), ("mla_up",), ("rope_m",), ("qkT", "mla", MQ, MK, None), ("soft", "mla"),
                  ("merge", l), ("backT", "merged"), ("out", k), ("resid", k)]
        steps += [("norm", 3 * l + 2), ("ffn", 3 * l + 2, FFN_BLOCKS, None), ("resid", 3 * l + 2)]
    for l in range(DEPTH):
        k = 3 * DEPTH + 2 * l
        which = "ab"[l]
        steps += [("norm", k), ("proj", 6), ("head_norm",),
                  ("qkT", "wide", 0, 1024, which), ("diff" if l == 0 else "soft", "band")]
        steps += [("out_norm",)] if l == 0 else []
        steps += [("backT", "subln" if l == 0 else "y"), ("out", k), ("resid", k)]
        steps += [("norm", k + 1), ("route", l), ("ffn", k + 1, MOE_BLOCKS, "moe"), ("resid", k + 1)]
    kinds = ("n", "u", "th", "tf", "hid", "req", "src", "x", "ev", "sc", "pr", "ov", "st", "mg", "sq", "mx", "hn")
    at = dict.fromkeys(kinds, 0)
    plan = []
    for step in steps:
        plan.append((step, dict(at)))
        kind = step[0]
        uses = {
            "norm": dict(u=4, th=4, tf=4, req=NT, src=1),
            "rope_p": dict(src=1), "rope_m": dict(src=1), "mla_norm": dict(req=1, src=1),
            "mla_T": dict(u=2, th=2, tf=2), "mla_up": dict(n=2, ev=2),
            "qkT": dict(u=4 if "pairs" in step else 8),
            "stick": dict(sc=8, pr=8, ov=8, st=8),
            "merge": dict(n=18, u=6, th=6, mg=6), "out": dict(n=4, u=2, tf=2),
            "head_norm": dict(req=1, src=1), "out_norm": dict(req=1, src=1, sq=1),
            "diff": dict(sc=16, mx=16, pr=16, u=8, ov=8), "route": dict(u=3, th=1),
        }
        if kind == "ffn":
            nb = step[2]
            used = dict(n=3 * nb, u=nb + 2 + (0 if step[3] else FFN_UNITS), th=nb, tf=2, hid=nb)
            if step[3]:
                used.update(u=MOE_TURNS, th=MOE_HIGHS)
        elif kind == "proj":
            used = dict(n=2 * step[1], ev=step[1])
            if step[1] == 6:
                used.update(sq=2, hn=1)
        elif kind == "resid":
            used = dict(req=NT if step[1] < 6 else 0)
        elif kind == "soft":
            h = 16 if step[1] == "band" else 8
            used = dict(sc=h, mx=h, pr=h, u=h, ov=h)
        elif kind == "backT":
            used = dict(u=4, th=4, tf=4) if step[1] == "subln" else dict(u=4, th=4)
        else:
            used = uses[kind]
        for name, c in used.items():
            at[name] += c
    plan.append((("end",), dict(at)))
    return plan


PAIRS = EXP // 2
PAIRS = EXP // 2


def moe_events():
    tr_at, high_at = {}, {}

    def event(*what, high=True):
        tr_at[what] = len(tr_at)
        if high:
            high_at[what] = len(high_at)

    def tail(p):
        event("pick", p, high=False)
        event("weight", p, high=False)

    for r in range(KT):
        event("g", 0, r)
    tail(0)
    for e in range(EXP + 1):
        rounds = [("g", e // 2 + 1, 4 * (e % 2) + r) for r in range(4)] if e < EXP - 2 else []
        if e:
            event("hid", e - 1)
            event("y", e - 1, 0)
            event("y", e - 1, 1)
        for r in rounds:
            event(*r)
        if rounds and e % 2:
            tail(e // 2 + 1)
    return tr_at, high_at


MOE_TR, MOE_HIGH = moe_events()
MOE_TURNS = 2 + len(MOE_TR)
MOE_HIGHS = len(MOE_HIGH)
PAIR_TR = MOE_TR["hid", 2] - MOE_TR["hid", 0]
PAIR_HIGH = MOE_HIGH["hid", 2] - MOE_HIGH["hid", 0]


def moe_up_at(n0, e, j):
    return n0 + 2 * j if e == 0 else n0 + 6 * e - 2 + 4 * j


def moe_down_at(n0, e, h):
    return n0 + 6 * e + (6 if e < EXP - 1 else 4) + h


def ffn_order(start, units):
    if not units:
        return (lambda g: start + 2 + g), None, 2
    return (lambda g: start + 2 + (g if g < 2 else 2 * g - 2)), (lambda g: start + 2 + 2 * g - 1), 4


def block_order(nb):
    peeled = 1 if nb % 2 == 0 else 2
    return peeled, (nb - 1 - peeled) // 2


def build(nc, wstream, ada_stream, xin, const_in, vec_in, bgate_in, lam_in, rbias_in, t5_in, t5hot_in, rel_in, rw_in, out):
    plan = make_plan()
    n_chunks = plan[-1][1]["n"]
    dense_steps = [(step[1], b["n"]) for step, b in plan if step[0] == "ffn" and not step[3]]
    unit_base = {k: FIRST_UNITS + FFN_UNITS * i for i, (k, _) in enumerate(dense_steps)}
    assert FIRST_UNITS + FFN_UNITS * len(dense_steps) == UNITS and FFN_BLOCKS == FFN_UNITS + 2
    assert block_order(FFN_BLOCKS)[0] == 2

    with ExitStack() as ctx:
        def sb(name, shape, dt=F32):
            return ctx.enter_context(nc.sbuf_tensor(name, shape, dt))

        def sem(name):
            return ctx.enter_context(nc.semaphore(name))

        stage = sb("stage", [P, STAGES, CW])
        w_hi = sb("w_hi", [P, PARTS, CW], F32R)
        w_lo = sb("w_lo", [P, PARTS, CW], F32R)
        x = sb("x_tok", [P, NT, D])
        tok = sb("tok", [P, NT, D])
        hT_hi = sb("hT_hi", [P, KT, S], F32R)
        hT_lo = sb("hT_lo", [P, KT, S], F32R)
        proj_at = nc.sbuf_base
        proj = sb("proj", [P, NT, PROJ_W])
        h_hi = nc.alloc_sbuf_tensor_at("h_hi", [P, NT, D], F32R, offset=proj_at)
        h_lo = nc.alloc_sbuf_tensor_at("h_lo", [P, NT, D], F32R, offset=proj_at + NT * D * 4)
        pick = nc.alloc_sbuf_tensor_at("pick", [P, NT, 2 * P], F32R, offset=proj_at + 2 * NT * D * 4)
        g_lo = nc.alloc_sbuf_tensor_at("g_lo", [P, KT, S], F32R, offset=proj_at + 2 * NT * (D + P) * 4)
        yT_hi = sb("yT_hi", [P, 4, S], F32R)
        yT_lo = sb("yT_lo", [P, 4, S], F32R)
        qk_at = nc.sbuf_base
        qk = sb("qk", [P, 16, S])
        g_hi = nc.alloc_sbuf_tensor_at("g_hi", [P, KT, S], F32R, offset=qk_at)
        pair = sb("pair", [P, 2, NT, BLK])
        hid_hi = yT_hi[:, 0:2, :].rearrange("p a s -> p (a s)")
        hid_lo = yT_lo[:, 0:2, :].rearrange("p a s -> p (a s)")
        tf_at = nc.sbuf_base
        tf = sb("tf", [P, 2, 512])
        prob = tok[:, :, 512:896]
        probT = pair[:].rearrange("p a t c -> p a (t c)")[:, :, 0:384]
        mixp = tf[:, 0, 0:384]
        bias_in = proj[:, :, 3072:3456]
        rope_t = pair[:, 0].rearrange("p t c -> p (t c)").rearrange("p (i w) -> p i w", i=4)
        pickT = nc.alloc_sbuf_tensor_at("pickT", [P, 2, 4 * P], F32R, offset=qk_at + KT * S * 4)
        pickg = qk[:, 12:14, :]
        y1 = nc.alloc_sbuf_tensor_at("y1", [P, 2, 512], F32R, offset=tf_at)
        y_parts = (tuple(v[:, 2:4, :].rearrange("p a s -> p (a s)") for v in (yT_hi, yT_lo)), (y1[:, 0, :], y1[:, 1, :]))
        gathered = ((hT_hi, hT_lo), (g_hi, g_lo))
        ada_stage = proj[:].rearrange("p t c -> p (t c)")[:, 0:SLICES * 2 * UW].rearrange("p (q c) -> p q c", q=SLICES)
        ada_acc = qk[:, 0:6, :].rearrange("p a s -> p (a s)").rearrange("p (b c) -> p b c", b=2)
        const = sb("const", [P, N_CONST])
        vec = sb("vec", [P, N_VEC])
        mod = sb("mod", [P, NVEC, KT])
        c_act = sb("c_act", [P, 2 * KT])
        c_unit = sb("c_unit", [P, UNITS, KT])
        c_tmp = sb("c_tmp", [P, 2 * KT])
        ss = sb("ss", [P, 64])
        rs = sb("rs", [P, 64])
        mhalf = sb("mhalf", [P, 64])
        nmax = sb("nmax", [P, 2, 2])
        rsum = sb("rsum", [P, 2, 2])
        rinv = sb("rinv", [P, 2, 2])
        lam = sb("lam", [P, 4 * HD])
        lam_s = sb("lam_s", [P, 4])
        rw = sb("rw", [P, KT * EXP])
        rw_hi = sb("rw_hi", [P, KT * EXP], F32R)
        rw_lo = sb("rw_lo", [P, KT * EXP], F32R)
        rbias = sb("rbias", [P, EXP])
        gates = sb("gates", [P, NT, EXP])
        slot_w = sb("slot_w", [P, 2, 2])
        rank = sb("rank", [P, NT, EXP])
        fullest = sb("fullest", [P, 1])
        fullest_i = sb("fullest_i", [P, 1], mybir.dt.int32)
        rt = sb("rt", [P, 8, NT * EXP])
        t5 = sb("t5", [32, 8])
        t5hot = tf[0:32, 1, :]
        t5row = tf[0:8, 0, :]
        t5_dram = nc.dram_tensor("t5_rows", [8, 512], F32)

        acc = ctx.enter_context(nc.psum_tensor("acc", [P, 4, 512], F32))
        gu = ctx.enter_context(nc.psum_tensor("gu", [P, 2, 512], F32))
        tr = ctx.enter_context(nc.psum_tensor("tr", [P, 2, 512], F32))

        h_banks = [acc[:, j, :] for j in range(4)] + [gu[:, j, :] for j in range(2)]

        landed = [sem(f"landed{i}") for i in range(STAGES)]
        chunk_ready = sem("chunk_ready")
        hi_ready = sem("hi_ready")
        pe_used = sem("pe_used")
        tr_full = sem("tr_full")
        tr_free = sem("tr_free")
        th_ready = sem("th_ready")
        tf_ready = sem("tf_ready")
        sg_ready = sem("sg_ready")
        hid_ready = sem("hid_ready")
        rs_req = sem("rs_req")
        rs_done = sem("rs_done")
        src_ready = sem("src_ready")
        x_ready = sem("x_ready")
        whole_done = sem("whole_done")
        half_done = sem("half_done")
        ev_ready = sem("ev_ready")
        s_full = sem("s_full")
        s_free = sem("s_free")
        m_ready = sem("m_ready")
        p_ready = sem("p_ready")
        a_ready = sem("a_ready")
        o_full = sem("o_full")
        o_free = sem("o_free")
        soft_ready = sem("soft_ready")
        sp_ready = sem("sp_ready")
        c_full = sem("c_full")
        arg_ready = sem("arg_ready")
        z_ready = sem("z_ready")
        e_ready = sem("e_ready")
        mg_ready = sem("mg_ready")
        bg_in = [sem("bg_in0"), sem("bg_in1")]
        bias_ld = [sem("bias_ld0"), sem("bias_ld1")]
        vec_ld = sem("vec_ld")
        ld = sem("ld")
        act_up = sem("act_up")
        dve_up = sem("dve_up")
        pool_up = sem("pool_up")
        c_exp = sem("c_exp")
        ada_landed = [sem(f"ada_landed{q}") for q in range(SLICES)]
        half_sum = sem("half_sum")
        slice_sum = sem("slice_sum")
        sq_ready = sem("sq_ready")
        sq_used = sem("sq_used")
        ada_sum = sem("ada_sum")
        h_full = sem("h_full")
        h_ready = sem("h_ready")
        sent_ready = sem("sent_ready")
        count_ready = sem("count_ready")
        pick_ready = sem("pick_ready")
        rwhi_ready = sem("rwhi_ready")
        rw_ready = sem("rw_ready")
        t5_mm = sem("t5_mm")
        t5_sb = sem("t5_sb")
        t5_st = sem("t5_st")
        lam_dot = sem("lam_dot")
        lam_exp = sem("lam_exp")
        mh_ready = sem("mh_ready")
        st_out = sem("st_out")
        N_LD = 7

        def cst(name):
            return const[:, CONST[name][0]:CONST[name][1]]

        def col(name, i):
            return vec[:, VEC[name][0] + i:VEC[name][0] + i + 1]

        ident, flip, ones, tri = cst("ident"), cst("flip"), cst("ones"), cst("tri")
        block = ctx.enter_context(nc.Block())

        @block.sync
        def _(sp):
            def chunk(n, i=0, rounds=1):
                if not isinstance(i, int) or n >= STAGES:
                    sp.wait_ge(chunk_ready, n + 1 - STAGES + STAGES * rounds * i)
                at = bass.ds(n + STAGES * rounds * i, 1)
                sp.dma_start(stage[:, n % STAGES, :], wstream[at].rearrange("a p c -> (a p) c")).then_inc(
                    landed[n % STAGES], 16)

            def ada_slice(unit, q, i=0):
                m = SLICES * unit + q
                if not isinstance(i, int) or m >= SLICES:
                    sp.wait_ge(slice_sum, m + 1 - SLICES + 2 * SLICES * i)
                at = bass.ds(m + 2 * SLICES * i, 1)
                sp.dma_start(ada_stage[:, q, :], ada_stream[at].rearrange("a p c -> (a p) c")).then_inc(
                    ada_landed[q], 16)

            def stream(n, end):
                turns = (end - n) // STAGES
                if turns > 1:
                    with sp.Fori(0, turns) as i:
                        for s in range(STAGES):
                            chunk(n + s, i)
                    n += turns * STAGES
                for m in range(n, end):
                    chunk(m)

            for unit in range(FIRST_UNITS + 1):
                for q in range(SLICES):
                    ada_slice(unit, q)
                    if unit >= FIRST_UNITS - 1 and q % 4 < 3:
                        chunk(3 * (unit - FIRST_UNITS + 1) + q)
            n = STAGES
            for k, n0 in dense_steps:
                stream(n, n0 + 8)
                if k:
                    sp.wait_ge(x_ready, NT * k)
                    for q in range(SLICES):
                        ada_slice(unit_base[k], q)
                stream(n0 + 8, n0 + 12)
                with sp.Fori(0, (FFN_UNITS - 1) // 2) as i:
                    for a in range(2):
                        for q in range(SLICES):
                            if q < 3:
                                chunk(n0 + 12 + 3 * a + q, i)
                            ada_slice(unit_base[k] + 1 + a, q, i)
                n = n0 + 12 + 3 * (FFN_UNITS - 1)
            stream(n, n_chunks)
            sp.wait_ge(x_ready, NT * NSUB)
            sp.dma_start(out.rearrange("(t p) d -> p t d", p=P), x[:]).then_inc(st_out, 16)
            sp.wait_ge(st_out, 16)

        @block.gpsimd
        def _(pool):
            pool.dma_start(vec[:], vec_in).then_inc(vec_ld, 16)
            pool.dma_start(const[:], const_in).then_inc(ld, 16)
            pool.dma_start(x[:], xin.rearrange("(t p) d -> p t d", p=P)).then_inc(ld, 16)
            pool.dma_start(rw[:], rw_in).then_inc(ld, 16)
            pool.dma_start(rbias[:], rbias_in.partition_broadcast(P)).then_inc(ld, 16)
            pool.dma_start(lam[:], lam_in.partition_broadcast(P)).then_inc(ld, 16)
            pool.dma_start(t5[:], t5_in).then_inc(ld, 16)
            pool.dma_start(t5hot, t5hot_in).then_inc(ld, 16)
            pool.memset(mhalf[:], -0.5).then_inc(mh_ready, 1)
            pool.wait_ge(mh_ready, 1)
            pool.wait_ge(t5_sb, 1)
            pool.dma_start(t5_dram.ap(), t5row).then_inc(t5_st, 16)
            pool.wait_ge(t5_st, 16)
            ups = 0

            def root(b, w, at=0, nth=0):
                nonlocal ups
                c = slice(at, at + w)
                pool.wait_ge(rs_req, b["req"] + nth + 1)
                pool.tensor_scalar(ss[:, c], ss[:, c], EPS, None, ALU.add).then_inc(pool_up, 1)
                ups += 1
                pool.wait_ge(pool_up, ups)
                pool.tensor_tensor(rs[:, c], ss[:, c], mhalf[:, c], ALU.pow).then_inc(rs_done, 1)

            loads = 0
            for step, b in plan:
                kind = step[0]
                if kind == "norm" or (kind == "resid" and step[1] < 6):
                    for t in range(NT):
                        root(b, 1, t + (NT if kind == "resid" else 0), t)
                elif kind == "mla_norm":
                    root(b, 4)
                elif kind == "head_norm":
                    root(b, 64)
                elif kind == "out_norm":
                    root(b, 16)
                elif (kind == "soft" and step[1] == "band") or kind == "diff":
                    table, pitch, heads = (t5_dram, 512, 8) if kind == "diff" else (rel_in.tensor, 513, 16)
                    per = 2 if kind == "diff" else 1
                    for h in range(heads):
                        if h >= 2:
                            pool.wait_ge(s_full, b["sc"] + per * (h - 1))
                        for q, (a, w) in enumerate(((0, 128), (128, 256))):
                            win = bass.AP(table, h * pitch + 129 - 128 * q, [[1, P], [1, w]])
                            pool.dma_start(bias_in[:, h % 2, a:a + w], win).then_inc(bias_ld[h % 2], 16)
                        loads += 1

        @block.scalar
        def _(act):
            ups = 0

            def hi(n, i=0, rounds=1):
                act.wait_ge(landed[n % STAGES], 16 * (n // STAGES + 1) + 16 * rounds * i)
                act.wait_ge(pe_used, n + 1 + STAGES * rounds * i)
                act.activation(w_hi[:, n % PARTS, :], stage[:, n % STAGES, :], ACT.Copy).then_inc(hi_ready, 1)

            def ahead(n):
                if n < n_chunks:
                    hi(n)
                    hi(n + 1)

            def own(ins):
                nonlocal ups
                ups += 1
                ins.then_inc(act_up, 1)
                act.wait_ge(act_up, ups)

            act.wait_ge(vec_ld, 16)
            act.activation(c_tmp[:], vec[:, 0:2 * KT], ACT.Exp, scale=-1.0).then_inc(c_exp, 1)
            act.wait_ge(ld, 16 * N_LD)
            act.activation(rw_hi[:], rw[:], ACT.Copy).then_inc(rwhi_ready, 1)
            act.wait_ge(t5_mm, 1)
            act.activation(t5row, tr[0:8, 0, :], ACT.Copy).then_inc(t5_sb, 1)
            act.wait_ge(lam_dot, 1)
            act.activation(lam_s[:, 2:4], lam_s[:, 0:2], ACT.Exp).then_inc(lam_exp, 1)

            def squares(b, srcs):
                for i, (src, width) in enumerate(srcs):
                    ins = act.activation(tok[:, i % 2, 0:width], src, ACT.Square, scale=width ** -0.5,
                                         accum_out=ss[:, i:i + 1])
                    if i < len(srcs) - 1:
                        own(ins)
                ins.then_inc(rs_req, 1)

            def mean_square(b, t, src, at):
                if b["req"] + t:
                    act.wait_ge(rs_req, b["req"] + t)
                act.activation(pair[:].rearrange("p a t c -> p (a t c)"), src, ACT.Square, scale=D ** -0.5,
                               accum_out=ss[:, at:at + 1]).then_inc(rs_req, 1)

            def take_hi(b, rounds, dst, plain, width=512):
                for r in range(rounds):
                    if plain:
                        act.wait_ge(tr_full, b["u"] + r + 1)
                        src = tr[:, (b["u"] + r) % 2, :]
                    else:
                        act.wait_ge(tf_ready, b["tf"] + r + 1)
                        src = tf[:, (b["tf"] + r) % 2, :]
                    w = width[r] if isinstance(width, tuple) else width
                    d = dst[:, 2 * r:2 * r + w // S, :].rearrange("p a s -> p (a s)")
                    act.activation(d, src[:, 0:w], ACT.Copy).then_inc(th_ready, 1)

            def ffn(b, nb, units):
                peeled, turns = block_order(nb)
                n0, g0 = b["n"], b["hid"]
                u_of, _, per_turn = ffn_order(b["u"], units)

                def silu(g, i=0):
                    act.wait_ge(pe_used, n_b(g) + 1 + PARTS + STAGES * i)
                    if not isinstance(i, int) or g >= 1:
                        act.wait_ge(hid_ready, g0 + g + 2 * i)
                    act.activation(pair[:, 0], gu[:, :, 0:BLK], ACT.Silu).then_inc(sg_ready, 1)

                def n_b(g):
                    return n0 + 1 if g == 0 else n0 + 3 * g

                def turn_hi(g, u, i=0):
                    act.wait_ge(tr_full, u + 1 + per_turn * i)
                    if not isinstance(i, int) or g >= 1:
                        act.wait_ge(pe_used, n0 + 3 * g + 1 + 1 + PARTS + STAGES * i)
                    act.activation(hid_hi, tr[:, u % 2, :], ACT.Copy).then_inc(th_ready, 1)

                def block_(g, i=0):
                    hi(n0 + 3 * g - 1, i)
                    silu(g - 1, i)
                    hi(n0 + 3 * g, i)
                    hi(n0 + 3 * g + 1, i)
                    turn_hi(g - 1, u_of(g - 1), i)

                for g in range(1, 1 + peeled):
                    block_(g)
                with act.Fori(0, turns) as i:
                    block_(1 + peeled, i)
                    block_(2 + peeled, i)
                silu(nb - 1)
                hi(n0 + 3 * nb - 1)
                turn_hi(nb - 1, u_of(nb - 1))
                ahead(n0 + 3 * nb)

            def moe(b):
                n0, g0 = b["n"], b["hid"]
                u0 = b["u"] + 2

                def silu(e, j, i=0):
                    g = 2 * e + j
                    act.wait_ge(pe_used, moe_up_at(n0, e, j) + 2 + PARTS + 24 * i)
                    if not isinstance(i, int) or g >= 2:
                        act.wait_ge(hid_ready, g0 + g - 1 + 8 * i)
                    act.activation(pair[:, 0, j, :], gu[:, j, 0:BLK], ACT.Silu).then_inc(sg_ready, 1)

                def high(what, dst, width=512, i=0):
                    u = u0 + MOE_TR[what]
                    act.wait_ge(tr_full, u + 1 + 2 * PAIR_TR * i)
                    act.activation(dst, tr[:, u % 2, 0:width], ACT.Copy).then_inc(th_ready, 1)

                def gather_hi(p, r, i=0):
                    high(("g", p, r), gathered[p % 2][0][:, r, :], S, i)

                def expert(e, i=0):
                    rounds = [(e // 2 + 1, 4 * (e % 2) + r) for r in range(4)] if e < EXP - 2 else []
                    up1, next0 = moe_up_at(n0, e, 1), moe_up_at(n0, e + 1, 0)
                    if e:
                        silu(e - 1, 1, i)
                        hi(moe_down_at(n0, e - 1, 0), i, 4)
                        high(("hid", e - 1), hid_hi, i=i)
                        hi(moe_down_at(n0, e - 1, 1), i, 4)
                    hi(up1, i, 4)
                    silu(e, 0, i)
                    if e:
                        high(("y", e - 1, 0), y_parts[0][0], i=i)
                    hi(up1 + 1, i, 4)
                    if e:
                        high(("y", e - 1, 1), y_parts[1][0], i=i)
                    if e < EXP - 1:
                        hi(next0, i, 4)
                    for r in rounds[:2]:
                        gather_hi(*r, i)
                    if e < EXP - 1:
                        hi(next0 + 1, i, 4)
                    for r in rounds[2:]:
                        gather_hi(*r, i)

                for r in range(KT):
                    gather_hi(0, r)
                expert(0)
                expert(1)
                with act.Fori(0, (PAIRS - 2) // 2) as i:
                    for e in range(2, 6):
                        expert(e, i)
                expert(EXP - 2)
                expert(EXP - 1)
                silu(EXP - 1, 1)
                high(("hid", EXP - 1), hid_hi)
                for h in range(2):
                    hi(moe_down_at(n0, EXP - 1, h))
                    high(("y", EXP - 1, h), y_parts[h][0])
                ahead(n0 + 3 * MOE_BLOCKS)

            def moe_dense(b):
                n0, g0, u0 = b["n"], b["hid"], b["u"] + 2

                def silu(g, i=0):
                    act.wait_ge(pe_used, moe_up_at(n0, g // 2, g % 2) + 2 + PARTS + 6 * i)
                    if not isinstance(i, int) or g:
                        act.wait_ge(hid_ready, g0 + g + 2 * i)
                    act.activation(pair[:, 0], gu[:, :, 0:BLK], ACT.Silu).then_inc(sg_ready, 1)

                def turn_hi(g, i=0):
                    act.wait_ge(tr_full, u0 + g + 1 + 2 * i)
                    dst = yT_hi[:, 2 * (g % 2):2 * (g % 2) + 2, :].rearrange("p a s -> p (a s)")
                    act.activation(dst, tr[:, (u0 + g) % 2, :], ACT.Copy).then_inc(th_ready, 1)

                def second(e, i=0):
                    hi(moe_up_at(n0, e, 1), i)
                    silu(2 * e, i)
                    turn_hi(2 * e, i)
                    hi(moe_up_at(n0, e, 1) + 1, i)

                second(0)
                with act.Fori(0, EXP - 1) as i:
                    up0 = moe_up_at(n0, 1, 0)
                    hi(up0, i)
                    silu(1, i)
                    hi(up0 + 1, i)
                    turn_hi(1, i)
                    hi(up0 + 2, i)
                    hi(up0 + 3, i)
                    second(1, i)
                silu(MOE_BLOCKS - 1)
                turn_hi(MOE_BLOCKS - 1)
                hi(moe_down_at(n0, EXP - 1, 0))
                hi(moe_down_at(n0, EXP - 1, 1))
                ahead(n0 + 3 * MOE_BLOCKS)

            def soft(b, heads):
                for a in range(heads):
                    act.wait_ge(m_ready, b["mx"] + a + 1)
                    s = (b["sc"] + a) % 2
                    for q, (lo, w) in enumerate(((0, 128), (128, 256))):
                        ins = act.activation(prob[:, s, lo:lo + w], prob[:, s, lo:lo + w], ACT.Exp,
                                             bias=nmax[:, s, q:q + 1], accum_out=rsum[:, s, q:q + 1])
                    ins.then_inc(p_ready, 1)

            ahead(0)
            for step, b in plan:
                kind = step[0]
                if kind == "norm":
                    k = step[1]
                    for t in range(NT):
                        act.wait_ge(x_ready, NT * (k - 1) + t + 1) if k else act.wait_ge(ld, 16 * N_LD)
                        mean_square(b, t, x[:, t, :], t)
                    take_hi(b, 4, hT_hi, False)
                elif kind == "ffn" and not step[3]:
                    ffn(b, step[2], True)
                elif kind == "ffn":
                    l = (step[1] - 3 * DEPTH) // 2
                    act.wait_ge(count_ready, l + 1)
                    most = act.value_load(fullest_i[0:1, 0:1], min_val=0, max_val=S)
                    with act.If(most <= P):
                        moe(b)
                    with act.Else():
                        moe_dense(b)
                        act.wait_ge(th_ready, b["th"] + MOE_BLOCKS)
                        act.nop().then_inc(th_ready, MOE_HIGHS - MOE_BLOCKS)
                elif kind == "resid" and step[1] < 6:
                    for t in range(NT):
                        act.wait_ge(pe_used, b["n"] + PARTS) if t else act.wait_ge(half_done, step[1] + 1)
                        mean_square(b, t, acc[:, 2 * t:2 * t + 2, :].rearrange("p a c -> p (a c)"), NT + t)
                elif kind == "proj":
                    blocks = step[1]

                    def evac(j):
                        act.wait_ge(pe_used, b["n"] + 2 * j + 2 + PARTS)
                        w = 512 if j < 6 else PROJ_W - 6 * 512
                        act.activation(proj[:, :, 512 * j:512 * j + w], acc[:, 2 * (j % 2):2 * (j % 2) + 2, 0:w],
                                       ACT.Copy).then_inc(ev_ready, 1)

                    for j in range(blocks):
                        if j:
                            hi(b["n"] + 2 * j)
                            hi(b["n"] + 2 * j + 1)
                            evac(j - 1)
                        if blocks == 6 and j >= 4:
                            if j == 4:
                                act.wait_ge(ev_ready, b["ev"] + 4)
                            else:
                                act.wait_ge(sq_used, b["hn"] + 1)
                            act.activation(tok[:].rearrange("p a c -> p (a c)"), proj[:, j - 4, 0:2048], ACT.Square,
                                           scale=HD ** -0.5).then_inc(sq_ready, 1)
                    evac(blocks - 1)
                    ahead(b["n"] + 2 * blocks)
                elif kind == "soft":
                    soft(b, 16 if step[1] == "band" else 8)
                elif kind == "diff":
                    soft(b, 16)
                elif kind == "stick":
                    def soften(a):
                        act.wait_ge(s_free, b["sc"] + a + 1)
                        s = a % 2
                        own(act.activation(mixp_of(a), prob[:, s, :], ACT.Abs))
                        own(act.activation(mixp_of(a), mixp_of(a), ACT.Exp, scale=-1.0))
                        act.activation(mixp_of(a), mixp_of(a), ACT.Ln, bias=1.0).then_inc(soft_ready, 1)

                    def mixp_of(a):
                        return tok[:, a % 2, 0:384]

                    def weigh(a):
                        act.wait_ge(arg_ready, b["st"] + a + 1)
                        if a >= 2:
                            act.wait_ge(o_full, b["ov"] + a - 1)
                        act.activation(probT[:, a % 2, :], prob[:, a % 2, :], ACT.Exp).then_inc(p_ready, 1)

                    soften(0)
                    for a in range(NH):
                        if a + 1 < NH:
                            soften(a + 1)
                        weigh(a)
                elif kind == "mla_norm":
                    act.wait_ge(ev_ready, b["ev"])
                    c0 = 6 * 512
                    act.wait_ge(o_full, b["ov"])
                    squares(b, [(proj[:, t, c0 + o:c0 + o + w], w) for o, w in ((0, QL), (QL, KVL)) for t in range(NT)])
                elif kind == "mla_T":
                    take_hi(b, 2, yT_hi, False, (512, 256))
                elif kind == "mla_up":
                    n = b["n"]
                    q_out = acc[:].rearrange("p (t a) c -> p t (a c)", t=NT)
                    act.wait_ge(pe_used, n + 1 + PARTS)
                    act.activation(proj[:, :, MQ:MQ + NH * QK_C], q_out[:, :, 0:NH * QK_C], ACT.Copy).then_inc(ev_ready, 1)
                    act.wait_ge(pe_used, n + 2 + PARTS)
                    for t in range(NT):
                        kv = q_out[:, t, :].rearrange("p (h e) -> p h e", h=NH)
                        act.activation(proj[:, t, MK:MK + 768].rearrange("p (h e) -> p h e", h=NH)[:, :, 0:NOPE],
                                       kv[:, :, 0:NOPE], ACT.Copy)
                        for h in (0, 4):
                            v = proj[:, t, mla_value_col(h):mla_value_col(h) + 4 * HD]
                            ins = act.activation(v.rearrange("p (h e) -> p h e", h=4), kv[:, h:h + 4, NOPE:128], ACT.Copy)
                    ins.then_inc(ev_ready, 1)
                    ahead(n + 2)
                elif kind == "merge":
                    l = step[1]

                    def load_bias(j):
                        if j >= 2:
                            act.wait_ge(z_ready, b["mg"] + j - 1)
                        c = 512 * j
                        act.dma_start(tf[:, j % 2, :], bgate_in[l, c:c + 512].partition_broadcast(P)).then_inc(
                            bg_in[j % 2], 16)

                    act.wait_ge(tr_free, b["u"] + 2)
                    load_bias(0)
                    load_bias(1)
                    def sigmoid(j):
                        act.wait_ge(z_ready, b["mg"] + j + 1)
                        flat = pair[:].rearrange("p a t c -> p (a t c)")
                        act.activation(flat, flat, ACT.Sigmoid).then_inc(e_ready, 1)
                        if j + 2 < 6:
                            load_bias(j + 2)

                    for j in range(6):
                        n = b["n"] + 3 * j
                        if j:
                            hi(n)
                            sigmoid(j - 1)
                            hi(n + 1)
                        hi(n + 2)
                        if j % 2 == 0:
                            for r in range(2):
                                u = b["u"] + j + r
                                act.wait_ge(tr_full, u + 1)
                                d = yT_hi[:, 2 * r:2 * r + 2, :].rearrange("p a s -> p (a s)")
                                act.activation(d, tr[:, u % 2, :], ACT.Copy).then_inc(th_ready, 1)
                    ahead(b["n"] + 18)
                    sigmoid(5)
                elif kind == "backT":
                    take_hi(b, 4, hT_hi, step[1] != "subln")
                elif kind == "out":
                    for c in range(2, 4):
                        hi(b["n"] + c)
                    ahead(b["n"] + 4)
                elif kind == "out_norm":
                    act.wait_ge(o_free, b["ov"])
                    act.activation(tok[:], proj[:, :, 0:D], ACT.Square, scale=128 ** -0.5).then_inc(sq_ready, 1)
                elif kind == "route":
                    act.wait_ge(tr_full, b["u"] + 1)
                    act.activation(tf[0:EXP, 0, 0:S], tr[0:EXP, b["u"] % 2, 0:S], ACT.Exp, scale=-1.0).then_inc(th_ready, 1)
                    for j in range(8):
                        act.wait_ge(h_full, 8 * step[1] + j + 1)
                        part, t, half = j // 4, j // 2 % 2, j % 2
                        act.activation((h_hi, h_lo)[part][:, t, half * 512:(half + 1) * 512], h_banks[j % 6],
                                       ACT.Copy).then_inc(h_ready, 1)

        @block.vector
        def _(dve):
            ups = 0
            turn, per_turn = 0, 0

            def own(ins):
                nonlocal ups
                ups += 1
                ins.then_inc(dve_up, 1)
                dve.wait_ge(dve_up, ups + per_turn * turn)

            def lo(n, i=0, rounds=1):
                dve.wait_ge(hi_ready, n + 1 + STAGES * rounds * i)
                dve.tensor_tensor(w_lo[:, n % PARTS, :], stage[:, n % STAGES, :], w_hi[:, n % PARTS, :].bitcast(F32),
                                  ALU.subtract).then_inc(chunk_ready, 1)

            def ahead(n):
                if n < n_chunks:
                    lo(n)
                    lo(n + 1)

            def flat(ap):
                return ap.rearrange("p a b -> p (a b)")

            def take_lo(b, rounds, dst_hi, dst_lo, cols=None, width=(512, 512, 512, 512)):
                def rest(r):
                    dve.wait_ge(th_ready, b["th"] + r + 1)
                    w = width[r]
                    src = tf[:, (b["tf"] + r) % 2, 0:w] if cols else tr[:, (b["u"] + r) % 2, 0:w]
                    dve.tensor_tensor(flat(dst_lo[:, 2 * r:2 * r + w // S, :]), src,
                                      flat(dst_hi[:, 2 * r:2 * r + w // S, :]).bitcast(F32),
                                      ALU.subtract).then_inc(tr_free, 1)

                for r in range(rounds):
                    if cols:
                        dve.wait_ge(tr_full, b["u"] + r + 1)
                        if r >= 2:
                            dve.wait_ge(tr_free, b["u"] + r + 1)
                        for a in range(width[r] // S):
                            c0, c1, op1 = cols(2 * r + a)
                            ins = dve.tensor_scalar(tf[:, (b["tf"] + r) % 2, a * S:(a + 1) * S],
                                                    tr[:, (b["u"] + r) % 2, a * S:(a + 1) * S], c0, c1, ALU.mult, op1)
                        ins.then_inc(tf_ready, 1)
                        if r:
                            rest(r - 1)
                    else:
                        rest(r)
                if cols:
                    rest(rounds - 1)

            def gate_row(b, k, u, between=None):
                dve.wait_ge(tr_free, u + 2)
                for r in range(2):
                    for j in range(4):
                        ins = dve.tensor_scalar(tf[:, (b["tf"] + r) % 2, j * P:(j + 1) * P], ident,
                                                mod[:, 3 * k + 2, 4 * r + j:4 * r + j + 1], None, ALU.mult)
                    ins.then_inc(tf_ready, 1)
                if between:
                    between()
                for r in range(2):
                    dve.wait_ge(tr_full, u + r + 1)
                    dve.tensor_copy(tok[:, 0, r * 512:(r + 1) * 512], tr[:, (u + r) % 2, :]).then_inc(tr_free, 1)

            dve.nop().then_inc(tr_free, 2)
            dve.wait_ge(vec_ld, 16)
            dve.wait_ge(c_exp, 1)
            own(dve.tensor_scalar(c_tmp[:], c_tmp[:], 1.0, None, ALU.add))
            own(dve.reciprocal(c_tmp[:], c_tmp[:]))
            own(dve.tensor_tensor(c_act[:], c_tmp[:], vec[:, 0:2 * KT], ALU.mult))

            split_at = DEPTH * 9 * D // UW
            for u_from, u_to, c0 in ((0, split_at, 0), (split_at, UNITS, KT)):
                ins = dve.tensor_copy(c_unit[:, u_from:u_to, :],
                                      c_act[:, c0:c0 + KT].unsqueeze(1).to_broadcast([P, u_to - u_from, KT]))
            own(ins)
            mod_flat, c_flat = flat(mod[:]), flat(c_unit[:])
            mods = mod[:].rearrange("p (k v) c -> p k v c", v=3)

            def ada_add(unit, k, i=0):
                q, j = k // 2, k % 2
                m, total = SLICES * unit + q, ada_acc[:, unit % 2, :]
                if j == 0:
                    dve.wait_ge(ada_landed[q], 16 * (unit + 1) + 32 * i)
                w = ada_stage[:, q, j * UW:(j + 1) * UW]
                at = KT * unit + k
                c = c_flat[:, at:at + 1] if isinstance(i, int) else c_flat[:, bass.ds(at + 2 * KT * i, 1)]
                if j:
                    dve.wait_ge(half_sum, m + 1 + 2 * SLICES * i)
                elif not isinstance(i, int) or m:
                    dve.wait_ge(slice_sum, m + 2 * SLICES * i)
                if k == 0:
                    ins = dve.tensor_scalar(total, w, c, None, ALU.mult)
                else:
                    ins = dve.scalar_tensor_tensor(total, w, c, total, ALU.mult, ALU.add)
                ins.then_inc(slice_sum if j else half_sum, 1)

            def side_constants():
                dve.wait_ge(ld, 16 * N_LD)
                dve.wait_ge(rwhi_ready, 1)
                dve.tensor_tensor(rw_lo[:], rw[:], rw_hi[:].bitcast(F32), ALU.subtract).then_inc(rw_ready, 1)
                lam4 = lam[:].rearrange("p (a b e) -> p a b e", a=2, b=2)
                dots = rope_t[:, 0, :].rearrange("p (a e) -> p a e", a=2)
                own(dve.tensor_tensor(dots, lam4[:, :, 0, :], lam4[:, :, 1, :], ALU.mult))
                dve.tensor_reduce(lam_s[:, 0:2], dots, AX, ALU.add).then_inc(lam_dot, 1)
                dve.wait_ge(lam_exp, 1)
                own(dve.tensor_tensor(lam_s[:, 0:1], lam_s[:, 3:4], lam_s[:, 2:3], ALU.subtract))
                own(dve.tensor_scalar(lam_s[:, 0:1], lam_s[:, 0:1], -0.2, None, ALU.add))

            for unit in range(FIRST_UNITS):
                dve.wait_ge(ada_sum, unit + 1)
                for k in range(KT):
                    ada_add(unit, k)
                if unit == 0:
                    side_constants()
            dve.wait_ge(ada_sum, FIRST_UNITS + 2)
            n_first = FIRST_UNITS * UC
            own(dve.tensor_tensor(mod_flat[:, 0:n_first], acc[:, 0, 0:n_first],
                                  vec[:, VEC["ada_b"][0]:VEC["ada_b"][0] + n_first], ALU.add))
            ahead(0)

            def factors(k):
                scale, gate = mods[:, k, 1, :], mods[:, k, 2, :]
                def gain(name):
                    return vec[:, VEC[name][0] + k * KT:VEC[name][0] + (k + 1) * KT]

                ins = dve.scalar_tensor_tensor(scale, scale, 1.0, gain("pre"), ALU.add, ALU.mult)
                if k < 6:
                    own(dve.scalar_tensor_tensor(gate, gate, 1.0, gain("post"), ALU.add, ALU.mult))
                    if k % 3 != 1:
                        own(dve.tensor_scalar(gate, gate, 0.5, None, ALU.mult))
                else:
                    own(ins)

            def ffn(b, k, nb):
                peeled, turns = block_order(nb)
                n0, g0, th0 = b["n"], b["hid"], b["th"]
                sg, hid = pair[:, 0], pair[:, 1]
                u_of, u_unit, per_turn_u = ffn_order(b["u"], True)

                def silu(g, i=0):
                    dve.wait_ge(sg_ready, g0 + g + 1 + 2 * i)
                    dve.tensor_tensor(hid, sg, gu[:, :, BLK:2 * BLK], ALU.mult).then_inc(hid_ready, 1)

                def turn_lo(g, i=0):
                    dve.wait_ge(th_ready, th0 + g + 1 + 2 * i)
                    dve.tensor_tensor(hid_lo, tr[:, u_of(g) % 2, :], hid_hi.bitcast(F32),
                                      ALU.subtract).then_inc(tr_free, 1)

                def take_unit(g, i=0):
                    at = UC * (unit_base[k] + g - 2)
                    dve.wait_ge(tr_full, u_unit(g) + 1 + per_turn_u * i)
                    if isinstance(i, int):
                        dst, bias = mod_flat[:, at:at + UC], vec[:, VEC["ada_b"][0] + at:VEC["ada_b"][0] + at + UC]
                    else:
                        dst = mod_flat[:, bass.ds(at + 2 * UC * i, UC)]
                        bias = vec[:, bass.ds(VEC["ada_b"][0] + at + 2 * UC * i, UC)]
                    dve.tensor_tensor(dst, tr[:, u_unit(g) % 2, 0:UC], bias, ALU.add).then_inc(tr_free, 1)

                def block_(g, i=0):
                    def add(*tiles):
                        for c in tiles if g >= 2 else ():
                            ada_add(unit_base[k] + g - 2, c, i)

                    add(0)
                    lo(n0 + 3 * g - 1, i)
                    add(1)
                    silu(g - 1, i)
                    add(2)
                    lo(n0 + 3 * g, i)
                    add(3)
                    lo(n0 + 3 * g + 1, i)
                    add(4)
                    turn_lo(g - 1, i)
                    add(5)
                    if g >= 3:
                        take_unit(g - 1, i)
                    add(6, 7)

                gate_row(b, k, b["u"])
                for g in range(1, 1 + peeled):
                    block_(g)
                with dve.Fori(0, turns) as i:
                    block_(1 + peeled, i)
                    block_(2 + peeled, i)
                silu(nb - 1)
                lo(n0 + 3 * nb - 1)
                turn_lo(nb - 1)
                take_unit(nb - 1)
                ahead(n0 + 3 * nb)

            def moe(b, k, l):
                n0, g0, th0 = b["n"], b["hid"], b["th"]
                u0 = b["u"] + 2

                def select(p, i=0):
                    for e in range(2):
                        at = slice(2 * p + e, 2 * p + e + 1) if isinstance(i, int) else bass.ds(4 * i + 2 * p + e, 1)
                        for t in range(NT):
                            dst = slice(e * P, (e + 1) * P)
                            dve.tensor_scalar(pick[:, t, dst], cst("slots"), rank[:, t, at], None, ALU.is_equal)
                            ins = dve.tensor_scalar(pickg[:, t, dst], cst("slots"), rank[:, t, at], gates[:, t, at],
                                                    ALU.is_equal, ALU.mult)
                    ins.then_inc(pick_ready, 1)

                def gather_lo(p, r, i=0):
                    u = u0 + MOE_TR["g", p, r]
                    dve.wait_ge(th_ready, th0 + MOE_HIGH["g", p, r] + 1 + 2 * PAIR_HIGH * i)
                    dve.tensor_copy(gathered[p % 2][1][:, r, :], tr[:, u % 2, S:2 * S]).then_inc(tr_free, 1)

                def gather_end(p, i=0):
                    for what, dst in (("pick", pickT[:, p % 2, :]), ("weight", slot_w[:, p % 2, :])):
                        u = u0 + MOE_TR[what, p]
                        dve.wait_ge(tr_full, u + 1 + 2 * PAIR_TR * i)
                        dve.tensor_copy(dst, tr[:, u % 2, 0:dst.shape[-1]]).then_inc(tr_free, 1)

                def hidden(e, j, i=0):
                    dve.wait_ge(sg_ready, g0 + 2 * e + j + 1 + 8 * i)
                    if j == 0:
                        dve.wait_ge(tr_free, u0 + MOE_TR["weight", e // 2] + 1 + 2 + 2 * PAIR_TR * i)
                    dve.scalar_tensor_tensor(pair[:, 1, j, :], pair[:, 0, j, :], slot_w[:, e // 2 % 2, e % 2:e % 2 + 1],
                                             gu[:, j, BLK:2 * BLK], ALU.mult, ALU.mult).then_inc(hid_ready, 1)

                def low(what, hi_, dst, i=0):
                    u = u0 + MOE_TR[what]
                    dve.wait_ge(th_ready, th0 + MOE_HIGH[what] + 1 + 2 * PAIR_HIGH * i)
                    dve.tensor_tensor(dst, tr[:, u % 2, :], hi_.bitcast(F32), ALU.subtract).then_inc(tr_free, 1)

                def expert(e, i=0):
                    rounds = [(e // 2 + 1, 4 * (e % 2) + r) for r in range(4)] if e < EXP - 2 else []
                    up1, next0 = moe_up_at(n0, e, 1), moe_up_at(n0, e + 1, 0)
                    if e:
                        hidden(e - 1, 1, i)
                    if rounds and e % 2 == 0:
                        select(e // 2 + 1, i)
                    if e:
                        lo(moe_down_at(n0, e - 1, 0), i, 4)
                        low(("hid", e - 1), hid_hi, hid_lo, i)
                        lo(moe_down_at(n0, e - 1, 1), i, 4)
                    lo(up1, i, 4)
                    if e:
                        low(("y", e - 1, 0), *y_parts[0], i)
                    hidden(e, 0, i)
                    if e:
                        low(("y", e - 1, 1), *y_parts[1], i)
                    lo(up1 + 1, i, 4)
                    for r in rounds[:2]:
                        gather_lo(*r, i)
                    if e < EXP - 1:
                        lo(next0, i, 4)
                    for r in rounds[2:3]:
                        gather_lo(*r, i)
                    if e < EXP - 1:
                        lo(next0 + 1, i, 4)
                    for r in rounds[3:]:
                        gather_lo(*r, i)
                    if rounds and e % 2:
                        gather_end(e // 2 + 1, i)

                gate_row(b, k, b["u"], lambda: select(0))
                for r in range(KT):
                    gather_lo(0, r)
                gather_end(0)
                expert(0)
                expert(1)
                with dve.Fori(0, (PAIRS - 2) // 2) as i:
                    for e in range(2, 6):
                        expert(e, i)
                expert(EXP - 2)
                expert(EXP - 1)
                hidden(EXP - 1, 1)
                low(("hid", EXP - 1), hid_hi, hid_lo)
                for h in range(2):
                    lo(moe_down_at(n0, EXP - 1, h))
                    low(("y", EXP - 1, h), *y_parts[h])
                ahead(n0 + 3 * MOE_BLOCKS)

            def moe_dense(b, k):
                n0, g0, th0, u0 = b["n"], b["hid"], b["th"], b["u"] + 2

                def hidden(g, i=0):
                    dve.wait_ge(sg_ready, g0 + g + 1 + 2 * i)
                    for t in range(NT):
                        at = slice(g // 2, g // 2 + 1) if isinstance(i, int) else bass.ds(i + g // 2, 1)
                        ins = dve.scalar_tensor_tensor(pair[:, 1, t, :], pair[:, 0, t, :], gates[:, t, at],
                                                       gu[:, t, BLK:2 * BLK], ALU.mult, ALU.mult)
                    ins.then_inc(hid_ready, 1)

                def turn_lo(g, i=0):
                    dve.wait_ge(th_ready, th0 + g + 1 + 2 * i)
                    at = slice(2 * (g % 2), 2 * (g % 2) + 2)
                    dve.tensor_tensor(flat(yT_lo[:, at, :]), tr[:, (u0 + g) % 2, :], flat(yT_hi[:, at, :]).bitcast(F32),
                                      ALU.subtract).then_inc(tr_free, 1)

                def second(e, i=0):
                    lo(moe_up_at(n0, e, 1), i)
                    hidden(2 * e, i)
                    turn_lo(2 * e, i)
                    lo(moe_up_at(n0, e, 1) + 1, i)

                gate_row(b, k, b["u"])
                second(0)
                with dve.Fori(0, EXP - 1) as i:
                    up0 = moe_up_at(n0, 1, 0)
                    lo(up0, i)
                    hidden(1, i)
                    lo(up0 + 1, i)
                    turn_lo(1, i)
                    lo(up0 + 2, i)
                    lo(up0 + 3, i)
                    second(1, i)
                hidden(MOE_BLOCKS - 1)
                turn_lo(MOE_BLOCKS - 1)
                lo(moe_down_at(n0, EXP - 1, 0))
                lo(moe_down_at(n0, EXP - 1, 1))
                ahead(n0 + 3 * MOE_BLOCKS)

            def soft_max_in(b, a, mask, scale):
                s = a % 2
                dve.wait_ge(s_full, b["sc"] + a + 1)
                dve.scalar_tensor_tensor(prob[:, s, :], gu[:, s, 0:384], scale, cst(mask),
                                         ALU.mult, ALU.add).then_inc(s_free, 1)
                dve.wait_ge(s_free, b["sc"] + a + 1)
                dve.tensor_reduce(nmax[:, s, 0:1], prob[:, s, 0:128], AX, ALU.max, negate=True)
                dve.tensor_reduce(nmax[:, s, 1:2], prob[:, s, 128:384], AX, ALU.max, negate=True).then_inc(m_ready, 1)

            def turn_prob(b, h):
                dve.wait_ge(tr_full, b["u"] + h + 1)
                if h >= 2:
                    dve.wait_ge(o_full, b["ov"] + h - 1)
                dve.tensor_copy(probT[:, h % 2, :], tr[:, (b["u"] + h) % 2, 0:384]).then_inc(tr_free, 1)

            def rotate(x1, x2, cos, sin, w, o1=None, o2=None):
                shape = x1.shape[1:]
                def tmp(i):
                    v = rope_t[:, i, 0:w]
                    return v.rearrange("p (h f) -> p h f", h=shape[0]) if len(shape) == 2 else v
                dve.tensor_tensor(tmp(0), x1, cos, ALU.mult)
                dve.tensor_tensor(tmp(1), x2, sin, ALU.mult)
                dve.tensor_tensor(tmp(2), x1, sin, ALU.mult)
                own(dve.tensor_tensor(tmp(3), x2, cos, ALU.mult))
                dve.tensor_tensor(x1 if o1 is None else o1, tmp(0), tmp(1), ALU.subtract)
                own(dve.tensor_tensor(x2 if o2 is None else o2, tmp(2), tmp(3), ALU.add))

            for step, b in plan:
                kind = step[0]
                if kind == "norm":
                    k = step[1]
                    dve.wait_ge(tr_free, b["u"] + 2)
                    factors(k)
                    if k:
                        dve.wait_ge(x_ready, NT * k)
                    for t in range(NT):
                        dve.wait_ge(rs_done, b["req"] + t + 1)
                        ins = dve.tensor_scalar(tok[:, t, :], x[:, t, :], rs[:, t:t + 1], None, ALU.mult)
                    ins.then_inc(src_ready, 1)
                    take_lo(b, 4, hT_hi, hT_lo,
                            lambda c: (mod[:, 3 * k + 1, c:c + 1], mod[:, 3 * k, c:c + 1], ALU.add))
                elif kind == "ffn" and not step[3]:
                    ffn(b, step[1], step[2])
                elif kind == "ffn":
                    l = (step[1] - 3 * DEPTH) // 2
                    dve.wait_ge(count_ready, l + 1)
                    most = dve.value_load(fullest_i[0:1, 0:1], min_val=0, max_val=S)
                    with dve.If(most <= P):
                        moe(b, step[1], l)
                    with dve.Else():
                        moe_dense(b, step[1])
                        dve.wait_ge(tr_free, b["u"] + 2 + 2 + MOE_BLOCKS)
                        dve.nop().then_inc(tr_free, MOE_TURNS - MOE_BLOCKS - 2)
                        dve.nop().then_inc(pick_ready, PAIRS)
                elif kind == "resid":
                    k = step[1]
                    dve.wait_ge(tr_free, b["u"] + 2)
                    for t in range(NT):
                        a = flat(acc[:, 2 * t:2 * t + 2, :])
                        if t:
                            dve.wait_ge(x_ready, NT * k + t)
                        if k < 6:
                            dve.wait_ge(rs_done, b["req"] + t + 1)
                            own(dve.scalar_tensor_tensor(tok[:, 1, :], a, rs[:, NT + t:NT + t + 1], tok[:, 0, :],
                                                         ALU.mult, ALU.mult))
                        else:
                            if t == 0:
                                dve.wait_ge(half_done, k + 1)
                            elif k % 2:
                                dve.wait_ge(whole_done, (k - 3 * DEPTH) // 2 + 1)
                            else:
                                dve.wait_ge(pe_used, b["n"] + PARTS)
                            own(dve.tensor_tensor(tok[:, 1, :], a, tok[:, 0, :], ALU.mult))
                        dve.tensor_tensor(x[:, t, :], x[:, t, :], tok[:, 1, :], ALU.add).then_inc(x_ready, 1)
                elif kind == "proj":
                    for j in range(2, 2 * step[1]):
                        lo(b["n"] + j)
                        if step[1] == 6 and j in (9, 11):
                            t = (j - 9) // 2
                            dve.wait_ge(sq_ready, b["sq"] + t + 1)
                            dve.tensor_reduce(ss[:, 32 * t:32 * t + 32], flat(tok[:]).rearrange("p (h e) -> p h e", e=HD),
                                              AX, ALU.add).then_inc(sq_used if t < NT - 1 else rs_req, 1)
                elif kind == "rope_p":
                    dve.wait_ge(ev_ready, b["ev"])
                    half = ROT // 2
                    for t in range(NT):
                        heads = proj[:, t, 0:1024].rearrange("p (h e) -> p h e", e=HD)
                        c = CONST["cos_p"][0] + t * half
                        cos = const[:, c:c + half].unsqueeze(1).to_broadcast([P, 16, half])
                        c = CONST["sin_p"][0] + t * half
                        sin = const[:, c:c + half].unsqueeze(1).to_broadcast([P, 16, half])
                        rotate(heads[:, :, 0:half], heads[:, :, half:ROT], cos, sin, 16 * half)
                    dve.nop().then_inc(src_ready, 1)
                elif kind == "rope_m":
                    dve.wait_ge(ev_ready, b["ev"])
                    half = ROPE // 2
                    for t in range(NT):
                        c, s_ = CONST["cos_m"][0] + t * half, CONST["sin_m"][0] + t * half
                        kr = proj[:, t, PROJ_W - ROPE:PROJ_W]
                        rotate(kr[:, 0:half], kr[:, half:ROPE], const[:, c:c + half], const[:, s_:s_ + half], half)
                        cos = const[:, c:c + half].unsqueeze(1).to_broadcast([P, NH, half])
                        sin = const[:, s_:s_ + half].unsqueeze(1).to_broadcast([P, NH, half])
                        q = proj[:, t, MQ:MQ + 768].rearrange("p (h e) -> p h e", h=NH)
                        rotate(q[:, :, NOPE:NOPE + half], q[:, :, NOPE + half:QK_C], cos, sin, NH * half)
                        km = proj[:, t, MK:MK + 768].rearrange("p (h e) -> p h e", h=NH)
                        own(dve.tensor_copy(km[:, :, NOPE:QK_C], kr.unsqueeze(1).to_broadcast([P, NH, ROPE])))
                    dve.nop().then_inc(src_ready, 1)
                elif kind == "qkT":
                    rounds = 4 if step[1] == "pairs" else 8
                    rows = QK_C if step[1] == "mla" else P
                    for r in range(rounds):
                        u = b["u"] + r
                        dve.wait_ge(tr_full, u + 1)
                        dst, src = flat(qk[0:rows, 2 * r:2 * r + 2, :]), tr[0:rows, u % 2, :]
                        if step[1] != "wide":
                            dve.tensor_copy(dst, src).then_inc(tr_free, 1)
                        elif r < 4:
                            dve.tensor_scalar(dst, src, col(step[4] + "_q", 0), HD ** -0.5,
                                              ALU.mult, ALU.mult).then_inc(tr_free, 1)
                        else:
                            dve.tensor_scalar(dst, src, col(step[4] + "_k", 0), None, ALU.mult).then_inc(tr_free, 1)
                    if step[2] != 1536:
                        ahead(b["n"])
                elif kind == "soft":
                    which = step[1]
                    heads, mask, scale, out_col = {
                        "moba": (NH, "causal", HD ** -0.5, Y_COL[0]), "mla": (NH, "causal", QK_C ** -0.5, Y_COL[2]),
                        "band": (16, "chunked", 1.0, 0)}[which]
                    inv_at = {}

                    def emit_out(h):
                        s = h % 2
                        dve.wait_ge(o_full, b["ov"] + h + 1)
                        dve.wait_ge(dve_up, inv_at[h])
                        for q in range(NT):
                            ins = dve.tensor_scalar(proj[:, q, out_col + h * HD:out_col + (h + 1) * HD],
                                                    acc[:, s, q * P:q * P + HD], rinv[:, s, q:q + 1], None, ALU.mult)
                        ins.then_inc(o_free, 1)

                    for h in range(heads + 2):
                        if h < heads:
                            soft_max_in(b, h, mask, scale)
                        if 1 <= h <= heads:
                            turn_prob(b, h - 1)
                            ups += 1
                            inv_at[h - 1] = ups
                            if h >= 3:
                                dve.wait_ge(o_free, b["ov"] + h - 2)
                            dve.reciprocal(rinv[:, (h - 1) % 2, :], rsum[:, (h - 1) % 2, :]).then_inc(dve_up, 1)
                        if h >= 2:
                            emit_out(h - 2)
                elif kind == "diff":
                    def combine(h):
                        dve.wait_ge(p_ready, b["pr"] + 2 * h + 2)
                        own(dve.reciprocal(rinv[:], rsum[:]))
                        own(dve.tensor_scalar(rinv[:, 1, :], rinv[:, 1, :], lam_s[:, 0:1], None, ALU.mult))
                        segs = ((0, 128), (128, 384))
                        for q, (lo_, hi_) in enumerate(segs):
                            ins = dve.tensor_scalar(mixp[:, lo_:hi_], prob[:, 1, lo_:hi_], rinv[:, 1, q:q + 1], None,
                                                    ALU.mult)
                        own(ins)
                        for q, (lo_, hi_) in enumerate(segs):
                            ins = dve.scalar_tensor_tensor(mixp[:, lo_:hi_], prob[:, 0, lo_:hi_], rinv[:, 0, q:q + 1],
                                                           mixp[:, lo_:hi_], ALU.mult, ALU.add)
                        ins.then_inc(a_ready, 1)

                    def emit_diff(h):
                        dve.wait_ge(o_full, b["ov"] + h + 1)
                        o = acc[:, h % 2, 0:256].rearrange("p (q e) -> p q e", q=NT)
                        dve.tensor_copy(proj[:, :, h * 128:(h + 1) * 128], o).then_inc(o_free, 1)

                    for h in range(10):
                        if h < 8:
                            if h:
                                dve.wait_ge(a_ready, h)
                            soft_max_in(b, 2 * h, "chunked", 1.0)
                            soft_max_in(b, 2 * h + 1, "chunked", 1.0)
                        if 1 <= h <= 8:
                            turn_prob(b, h - 1)
                        if h >= 2:
                            emit_diff(h - 2)
                        if h < 8:
                            combine(h)
                elif kind == "stick":
                    def take_z(a):
                        s = a % 2
                        dve.wait_ge(s_full, b["sc"] + a + 1)
                        if a >= 2:
                            dve.wait_ge(p_ready, b["pr"] + a - 1)
                        dve.scalar_tensor_tensor(prob[:, s, :], gu[:, s, 0:384], HD ** -0.5, cst("strict"),
                                                 ALU.mult, ALU.add).then_inc(s_free, 1)

                    def emit_stick(a):
                        dve.wait_ge(o_full, b["ov"] + a + 1)
                        o = acc[:, a % 2, 0:256].rearrange("p (q e) -> p q e", q=NT)[:, :, 0:HD]
                        dve.tensor_copy(proj[:, :, Y_COL[1] + a * HD:Y_COL[1] + (a + 1) * HD], o).then_inc(o_free, 1)

                    take_z(0)
                    for a in range(NH):
                        s = a % 2
                        dve.wait_ge(soft_ready, b["st"] + a + 1)
                        dve.scalar_tensor_tensor(tok[:, s, 0:384], prob[:, s, :], 0.0, tok[:, s, 0:384],
                                                 ALU.max, ALU.add).then_inc(sp_ready, 1)
                        if a + 1 < NH:
                            take_z(a + 1)
                        dve.wait_ge(c_full, b["st"] + a + 1)
                        dve.tensor_tensor(prob[:, s, :], prob[:, s, :], acc[:, 2 + s, 0:384],
                                          ALU.subtract).then_inc(arg_ready, 1)
                        if a:
                            emit_stick(a - 1)
                    emit_stick(NH - 1)
                elif kind == "mla_norm":
                    dve.wait_ge(rs_done, b["req"] + 1)
                    c0 = 6 * 512
                    for i, (o, w) in enumerate(((0, QL), (QL, KVL))):
                        for t in range(NT):
                            v = proj[:, t, c0 + o:c0 + o + w]
                            ins = dve.tensor_scalar(v, v, rs[:, 2 * i + t:2 * i + t + 1], None, ALU.mult)
                    ins.then_inc(src_ready, 1)
                elif kind == "mla_T":
                    l = step[1]
                    take_lo(b, 2, yT_hi, yT_lo,
                            lambda c: (col("q_norm", 2 * l + c) if c < 2 else col("kv_norm", l), None, ALU.bypass),
                            (512, 256))
                elif kind == "merge":
                    l = step[1]
                    flat4 = pair[:].rearrange("p a t c -> p a (t c)")

                    def finish(j):
                        n = b["n"] + 3 * j
                        dve.wait_ge(e_ready, b["mg"] + j + 1)
                        dve.wait_ge(pe_used, n + 3 + PARTS)
                        half = tok[:, :, 512 * (j % 2):512 * (j % 2) + 512]
                        br = acc[:, 2 * (j % 2):2 * (j % 2) + 2, :]
                        if j < 2:
                            dve.tensor_tensor(half, flat4, br, ALU.mult).then_inc(mg_ready, 1)
                        else:
                            own(dve.tensor_tensor(flat4, flat4, br, ALU.mult))
                            dve.tensor_tensor(half, half, flat4, ALU.add).then_inc(mg_ready, 1)

                    for j in range(6):
                        n = b["n"] + 3 * j
                        if j:
                            lo(n)
                            finish(j - 1)
                            lo(n + 1)
                        lo(n + 2)
                        if j % 2 == 0:
                            for r in range(2):
                                dve.wait_ge(th_ready, b["th"] + j + r + 1)
                                dve.tensor_tensor(flat(yT_lo[:, 2 * r:2 * r + 2, :]), tr[:, (b["u"] + j + r) % 2, :],
                                                  flat(yT_hi[:, 2 * r:2 * r + 2, :]).bitcast(F32),
                                                  ALU.subtract).then_inc(tr_free, 1)
                        dve.wait_ge(pe_used, n + 2 + PARTS)
                        dve.wait_ge(bg_in[j % 2], 16 * (3 * l + j // 2 + 1))
                        bias = tf[:, j % 2, :].unsqueeze(1).to_broadcast([P, 2, 512])
                        if j:
                            dve.wait_ge(mg_ready, b["mg"] + j)
                        dve.tensor_tensor(flat4, gu[:], bias, ALU.add).then_inc(z_ready, 1)
                    ahead(b["n"] + 18)
                    finish(5)
                elif kind == "backT":
                    if step[1] == "subln":
                        take_lo(b, 4, hT_hi, hT_lo, lambda c: (col("subln", 0), 0.8, ALU.mult))
                    else:
                        take_lo(b, 4, hT_hi, hT_lo)
                elif kind == "out":
                    gate_row(b, step[1], b["u"])
                    lo(b["n"] + 2)
                    lo(b["n"] + 3)
                    ahead(b["n"] + 4)
                elif kind == "head_norm":
                    dve.wait_ge(rs_done, b["req"] + 1)
                    for t in range(NT):
                        v = proj[:, t, 0:2048].rearrange("p (h e) -> p h e", e=HD)
                        f = rs[:, 32 * t:32 * t + 32].unsqueeze(2).to_broadcast([P, 32, HD])
                        ins = dve.tensor_tensor(v, v, f, ALU.mult)
                    ins.then_inc(src_ready, 1)
                elif kind == "out_norm":
                    dve.wait_ge(sq_ready, b["sq"] + 1)
                    dve.tensor_reduce(ss[:, 0:16], flat(tok[:]).rearrange("p (h e) -> p h e", e=128), AX,
                                      ALU.add).then_inc(rs_req, 1)
                    dve.wait_ge(rs_done, b["req"] + 1)
                    for t in range(NT):
                        v = proj[:, t, 0:D].rearrange("p (h e) -> p h e", e=128)
                        f = rs[:, 8 * t:8 * t + 8].unsqueeze(2).to_broadcast([P, 8, 128])
                        ins = dve.tensor_tensor(v, v, f, ALU.mult)
                    ins.then_inc(src_ready, 1)
                elif kind == "route":
                    R = NT * EXP
                    sc, sel, key, oh1, oh2, cmp_ = (rt[:, i, 0:R] for i in (0, 1, 2, 3, 4, 5))
                    small = rt[:, 6, :]
                    pairs = rt[:, 7, :]

                    def by_t(v, w=EXP):
                        return v.rearrange("p (t e) -> p t e", t=NT)

                    def over(v, w):
                        return v.unsqueeze(2).to_broadcast([P, v.shape[1], w])

                    dve.wait_ge(tr_full, b["u"] + 2)
                    dve.tensor_scalar(sc, tr[:, (b["u"] + 1) % 2, 0:R], 1.0, None, ALU.add).then_inc(tr_free, 2)
                    dve.wait_ge(tr_free, b["u"] + 2 + 2)
                    own(dve.reciprocal(sc, sc))
                    own(dve.tensor_tensor(by_t(sel), by_t(sc), rbias[:].unsqueeze(1).to_broadcast([P, NT, EXP]), ALU.add))
                    s4 = sel.rearrange("p (g e) -> p g e", e=4)
                    best, tmp3 = small[:, 0:8], pairs[:, 0:24].rearrange("p (g e) -> p g e", e=3)
                    tmp2 = key[:, 0:16].rearrange("p (g e) -> p g e", e=2)
                    dve.tensor_tensor(tmp3, s4[:, :, 0:3], s4[:, :, 1:4], ALU.add)
                    own(dve.tensor_tensor(tmp2, s4[:, :, 0:2], s4[:, :, 2:4], ALU.add))
                    dve.tensor_reduce(best, tmp3, AX, ALU.max)
                    own(dve.tensor_reduce(small[:, 8:16], tmp2, AX, ALU.max))
                    own(dve.tensor_tensor(best, best, small[:, 8:16], ALU.max))
                    last = small[:, 8:16].unsqueeze(2)
                    own(dve.tensor_tensor(last, s4[:, :, 0:1], s4[:, :, 3:4], ALU.add))
                    own(dve.tensor_tensor(best, best, small[:, 8:16], ALU.max))

                    def first_of_max(v, ranks, w, onehot, m):
                        v3 = v.rearrange("p (t e) -> p t e", t=NT)
                        k3 = key[:, 0:NT * w].rearrange("p (t e) -> p t e", t=NT)
                        o3 = onehot.rearrange("p (t e) -> p t e", t=NT)
                        own(dve.tensor_reduce(m, v3, AX, ALU.max))
                        own(dve.tensor_tensor(k3, v3, over(m, w), ALU.is_equal))
                        own(dve.tensor_tensor(key[:, 0:NT * w], key[:, 0:NT * w], ranks, ALU.mult))
                        own(dve.tensor_reduce(m, k3, AX, ALU.max))
                        own(dve.tensor_tensor(o3, k3, over(m, w), ALU.is_equal))

                    gm = small[:, 8:16]
                    first_of_max(best, cst("grank"), GROUPS, gm, small[:, 16:18])
                    s4m = cmp_.rearrange("p (g e) -> p g e", e=4)
                    own(dve.tensor_tensor(s4m, s4, over(gm, 4), ALU.mult))
                    own(dve.tensor_scalar(gm, gm, BIG, -BIG, ALU.mult, ALU.add))
                    own(dve.tensor_tensor(s4m, s4m, over(gm, 4), ALU.add))
                    first_of_max(cmp_, cst("rank"), EXP, oh1, small[:, 16:18])
                    own(dve.scalar_tensor_tensor(cmp_, oh1, -3 * BIG, cmp_, ALU.mult, ALU.add))
                    first_of_max(cmp_, cst("rank"), EXP, oh2, small[:, 16:18])
                    own(dve.tensor_tensor(oh1, oh1, oh2, ALU.add))
                    dve.nop().then_inc(sent_ready, 1)
                    own(dve.tensor_tensor(sc, sc, oh1, ALU.mult))
                    own(dve.tensor_reduce(small[:, 16:18], by_t(sc), AX, ALU.add))
                    own(dve.reciprocal(small[:, 16:18], small[:, 16:18]))
                    own(dve.tensor_tensor(gates[:], by_t(sc), over(small[:, 16:18], EXP), ALU.mult))
                    u = b["u"] + 2
                    dve.wait_ge(tr_full, u + 1)
                    rank_f = rank[:].rearrange("p t e -> p (t e)")
                    dve.tensor_reduce(fullest[:], tr[:, u % 2, R:R + EXP], AX, ALU.max)
                    own(dve.scalar_tensor_tensor(rank_f, tr[:, u % 2, 0:R], 1.0, oh1, ALU.add, ALU.mult))
                    dve.tensor_scalar(rank_f, rank_f, -1.0, None, ALU.add).then_inc(tr_free, 1)
                    dve.tensor_copy(fullest_i[:], fullest[:]).then_inc(count_ready, 1)

        @block.tensor
        def _(pe):
            def mm3(dst, l_hi, l_lo, r_hi, r_lo, start, stop, signal=None):
                ins = pe.matmul(dst, l_hi, r_hi, start=start, stop=False, skip_group_check=True)
                if signal is not None:
                    ins.then_inc(signal, 1)
                pe.matmul(dst, l_hi, r_lo, start=False, stop=False, skip_group_check=True)
                return pe.matmul(dst, l_lo, r_hi, start=False, stop=stop, skip_group_check=True)

            def chunk_wait(n, i=0, rounds=1):
                pe.wait_ge(chunk_ready, n + 1 + STAGES * rounds * i)

            def columns(n, dst, k0, kts, first, last, width=512, src=(hT_hi, hT_lo), i=0, pitch=512):
                chunk_wait(n, i)
                s = n % PARTS
                for t in range(NT):
                    for k in range(kts):
                        c = slice(k * pitch, k * pitch + width)
                        lhs = [v[:, k0 + k, t * P:(t + 1) * P] for v in src]
                        ins = mm3(dst(t), lhs[0], lhs[1], w_hi[:, s, c], w_lo[:, s, c], first and k == 0, last and k == kts - 1)
                ins.then_inc(pe_used, 1)

            def rows(n, lhs, first, last, i=0, rounds=1):
                chunk_wait(n, i, rounds)
                s = n % PARTS
                for t in range(NT):
                    for k in range(2):
                        l_hi, l_lo = lhs(k, t)
                        for h in range(2):
                            c = slice(k * D + h * 512, k * D + (h + 1) * 512)
                            ins = mm3(acc[:, 2 * t + h, :], l_hi, l_lo, w_hi[:, s, c], w_lo[:, s, c],
                                      first and k == 0, last and k == 1)
                    if last and t == 0:
                        ins.then_inc(half_done, 1)
                ins.then_inc(pe_used, 1)

            def turn(u, srcs, i=0, per=0, scaled=None):
                if scaled is None:
                    pe.wait_ge(tr_free, u + 1 + per * i)
                else:
                    pe.wait_ge(tf_ready, scaled)
                for j, src in enumerate(srcs):
                    rows_ = src.shape[-1]
                    ins = pe.transpose(tr[0:rows_, u % 2, j * P:(j + 1) * P], src, ident)
                ins.then_inc(tr_full, 1)

            def gate_row(b, u):
                for r in range(2):
                    pe.wait_ge(tf_ready, b["tf"] + r + 1)
                    pe.wait_ge(tr_free, u + r + 1)
                    pe.matmul(tr[:, (u + r) % 2, :], ones, tf[:, (b["tf"] + r) % 2, :], start=True,
                              stop=True).then_inc(tr_full, 1)

            def ffn(b, nb, k=None):
                peeled, turns = block_order(nb)
                n0, g0 = b["n"], b["hid"]
                u_of, u_unit, per_turn = ffn_order(b["u"], k is not None)

                def up(n, half, g, i=0):
                    if half == 0:
                        pe.wait_ge(hid_ready, g0 + g + 2 * i)
                    columns(n, lambda t: gu[:, t, :], 4 * half, 4, half == 0, half == 1, i=i)

                def turn_hidden(g, i=0):
                    hid = pair[:, 1]
                    pe.wait_ge(hid_ready, g0 + g + 1 + 2 * i)
                    turn(u_of(g), [hid[:, t, c * P:(c + 1) * P] for c in range(2) for t in range(NT)], i, per_turn)

                def down(n, g, first=False, last=False, i=0):
                    pe.wait_ge(tr_free, u_of(g) + 1 + 2 + per_turn * i)
                    rows(n, lambda k, t: tuple(v[:, (2 * k + t) * P:(2 * k + t + 1) * P] for v in (hid_hi, hid_lo)),
                         first, last, i)

                def sum_unit(g, i=0):
                    unit, u = unit_base[k] + g - 2, u_unit(g)
                    pe.wait_ge(slice_sum, SLICES * (unit + 1) + 2 * SLICES * i)
                    pe.wait_ge(tr_free, u + 1 + per_turn * i)
                    for j in range(UC):
                        ins = pe.matmul(tr[:, u % 2, j:j + 1], ada_acc[:, unit % 2, j * P:(j + 1) * P], ones[:, 0:1],
                                        start=True, stop=True)
                    ins.then_inc(tr_full, 1)

                def block_(g, i=0):
                    up(n0 + 3 * g - 1, 0, g, i)
                    turn_hidden(g - 1, i)
                    if k is not None and g >= 3:
                        sum_unit(g - 1, i)
                    up(n0 + 3 * g, 1, g, i)
                    down(n0 + 3 * g + 1, g - 1, isinstance(i, int) and g == 1, False, i)

                for half in range(2):
                    pe.wait_ge(tr_free, b["u"] + 2 * half)
                    up(n0 + half, half, 0)
                gate_row(b, b["u"])
                for g in range(1, 1 + peeled):
                    block_(g)
                with pe.Fori(0, turns) as i:
                    block_(1 + peeled, i)
                    block_(2 + peeled, i)
                turn_hidden(nb - 1)
                if k is not None:
                    sum_unit(nb - 1)
                down(n0 + 3 * nb - 1, nb - 1, False, True)

            def moe(b, l):
                n0, g0 = b["n"], b["hid"]
                u0 = b["u"] + 2

                def bank(what, i=0):
                    u = u0 + MOE_TR[what]
                    pe.wait_ge(tr_free, u + 1 + 2 * PAIR_TR * i)
                    return tr[:, u % 2, :]

                def taken(what, i=0):
                    pe.wait_ge(tr_free, u0 + MOE_TR[what] + 1 + 2 + 2 * PAIR_TR * i)

                def gather(p, r, i=0):
                    if r == 0:
                        pe.wait_ge(pick_ready, l * PAIRS + p + 1 + 2 * i)
                    dst = bank(("g", p, r), i)
                    for part, h in enumerate((h_hi, h_lo)):
                        for t in range(NT):
                            ins = pe.matmul(dst[:, part * S:(part + 1) * S], h[:, t, r * P:(r + 1) * P],
                                            pick[:, t, :], start=(t == 0), stop=(t == NT - 1), skip_group_check=True)
                    ins.then_inc(tr_full, 1)

                def gather_end(p, i=0):
                    dst = bank(("pick", p), i)
                    for j in range(4):
                        e, t = j // 2, j % 2
                        ins = pe.transpose(dst[:, j * P:(j + 1) * P], pick[:, t, e * P:(e + 1) * P].bitcast(F32), ident)
                    ins.then_inc(tr_full, 1)
                    dst = bank(("weight", p), i)
                    for e in range(2):
                        for t in range(NT):
                            ins = pe.matmul(dst[:, e:e + 1], pickg[:, t, e * P:(e + 1) * P], ones[:, 0:1],
                                            start=(t == 0), stop=(t == NT - 1), skip_group_check=True)
                    ins.then_inc(tr_full, 1)

                def up(e, j, half, i=0):
                    p, n = e // 2, moe_up_at(n0, e, j) + half
                    if half == 0:
                        if e % 2 == 0 and j == 0:
                            taken(("g", p, KT - 1), i)
                        if not isinstance(i, int) or e:
                            pe.wait_ge(hid_ready, g0 + 2 * e + j - 1 + 8 * i)
                    chunk_wait(n, i, 4)
                    slots = slice((e % 2) * P, (e % 2 + 1) * P)
                    src_hi, src_lo = gathered[p % 2]
                    for k in range(4):
                        c = slice(k * 512, (k + 1) * 512)
                        ins = mm3(gu[:, j, :], src_hi[:, 4 * half + k, slots], src_lo[:, 4 * half + k, slots],
                                  w_hi[:, n % PARTS, c], w_lo[:, n % PARTS, c], half == 0 and k == 0, half == 1 and k == 3)
                    ins.then_inc(pe_used, 1)

                def turn_hidden(e, i=0):
                    pe.wait_ge(hid_ready, g0 + 2 * e + 2 + 8 * i)
                    dst = bank(("hid", e), i)
                    for k in range(4):
                        ins = pe.transpose(dst[:, k * P:(k + 1) * P], pair[:, 1, k // 2, (k % 2) * P:(k % 2 + 1) * P], ident)
                    ins.then_inc(tr_full, 1)

                def down(e, h, i=0):
                    if h == 0:
                        taken(("hid", e), i)
                    n = moe_down_at(n0, e, h)
                    dst = bank(("y", e, h), i)
                    chunk_wait(n, i, 4)
                    for k in range(4):
                        c = slice(k * 512, (k + 1) * 512)
                        ins = mm3(dst, hid_hi[:, k * P:(k + 1) * P], hid_lo[:, k * P:(k + 1) * P],
                                  w_hi[:, n % PARTS, c], w_lo[:, n % PARTS, c], k == 0, k == 3,
                                  signal=pe_used if h and k == 0 else None)
                    ins.then_inc(tr_full, 1)

                def scatter(e, h, i=0):
                    taken(("y", e, h), i)
                    if e % 2 == 0 and h == 0:
                        taken(("pick", e // 2), i)
                    first, last = isinstance(i, int) and e == 0, isinstance(i, int) and e == EXP - 1
                    for t in range(NT):
                        lhs = pickT[:, e // 2 % 2, (2 * (e % 2) + t) * P:(2 * (e % 2) + t + 1) * P]
                        ins = pe.matmul(acc[:, 2 * t + h, :], lhs, y_parts[h][0], start=first, stop=False,
                                        skip_group_check=True)
                        if h == 0 and t == 0:
                            ins.then_inc(pe_used, 1)
                        ins = pe.matmul(acc[:, 2 * t + h, :], lhs, y_parts[h][1], start=False, stop=last,
                                        skip_group_check=True)
                        if last and h == 1 and t == 0:
                            ins.then_inc(half_done, 1)
                    if last and h == 1:
                        ins.then_inc(whole_done, 1)

                def expert(e, i=0):
                    rounds = [(e // 2 + 1, 4 * (e % 2) + r) for r in range(4)] if e < EXP - 2 else []
                    up(e, 0, 0, i)
                    if e:
                        turn_hidden(e - 1, i)
                    up(e, 0, 1, i)
                    if e:
                        down(e - 1, 0, i)
                        down(e - 1, 1, i)
                        scatter(e - 1, 0, i)
                    for r in rounds[:1]:
                        gather(*r, i)
                    if e:
                        scatter(e - 1, 1, i)
                    for r in rounds[1:2]:
                        gather(*r, i)
                    up(e, 1, 0, i)
                    for r in rounds[2:3]:
                        gather(*r, i)
                    up(e, 1, 1, i)
                    for r in rounds[3:]:
                        gather(*r, i)
                    if rounds and e % 2:
                        gather_end(e // 2 + 1, i)

                gate_row(b, b["u"])
                for r in range(KT):
                    gather(0, r)
                gather_end(0)
                expert(0)
                expert(1)
                with pe.Fori(0, (PAIRS - 2) // 2) as i:
                    for e in range(2, 6):
                        expert(e, i)
                expert(EXP - 2)
                expert(EXP - 1)
                turn_hidden(EXP - 1)
                down(EXP - 1, 0)
                down(EXP - 1, 1)
                scatter(EXP - 1, 0)
                scatter(EXP - 1, 1)

            def moe_dense(b):
                n0, g0, u0 = b["n"], b["hid"], b["u"] + 2

                def up(e, j, i=0):
                    g = 2 * e + j
                    if not isinstance(i, int) or g:
                        pe.wait_ge(hid_ready, g0 + g + 2 * i)
                    n = moe_up_at(n0, e, j)
                    columns(n, lambda t: gu[:, t, :], 0, 4, True, False, i=i)
                    columns(n + 1, lambda t: gu[:, t, :], 4, 4, False, True, i=i)

                def turn_hidden(g, i=0):
                    pe.wait_ge(hid_ready, g0 + g + 1 + 2 * i)
                    turn(u0 + g, [pair[:, 1, t, c * P:(c + 1) * P] for c in range(2) for t in range(NT)], i, 2)

                def down(e, h, i=0):
                    first, last = isinstance(i, int) and e == 0, isinstance(i, int) and e == EXP - 1
                    if h == 0:
                        pe.wait_ge(tr_free, u0 + 2 * e + 1 + 1 + 2 + 2 * i)
                    n = moe_down_at(n0, e, h)
                    chunk_wait(n, i)
                    for t in range(NT):
                        for k in range(4):
                            c = slice(k * 512, (k + 1) * 512)
                            ins = mm3(acc[:, 2 * t + h, :], yT_hi[:, k, t * P:(t + 1) * P], yT_lo[:, k, t * P:(t + 1) * P],
                                      w_hi[:, n % PARTS, c], w_lo[:, n % PARTS, c], first and k == 0, last and k == 3)
                        if last and h == 1 and t == 0:
                            ins.then_inc(half_done, 1)
                    ins.then_inc(pe_used, 1)

                def expert(e, i=0):
                    up(e, 0, i)
                    turn_hidden(2 * e - 1, i)
                    down(e - 1, 0, i)
                    down(e - 1, 1, i)
                    turn_hidden(2 * e, i)
                    up(e, 1, i)

                gate_row(b, b["u"])
                up(0, 0)
                turn_hidden(0)
                up(0, 1)
                expert(1)
                with pe.Fori(0, EXP - 2) as i:
                    expert(2, i)
                turn_hidden(MOE_BLOCKS - 1)
                down(EXP - 1, 0)
                down(EXP - 1, 1)
                pe.wait_ge(pe_used, n0 + 3 * MOE_BLOCKS + PARTS)
                pe.nop().then_inc(whole_done, 1)

            def small_mm(dst, lhs, rhs, start=True, stop=True):
                return pe.matmul(dst, lhs, rhs, start=start, stop=stop, skip_group_check=True)

            def value_mm(b, h, pT, v, width):
                if h >= 2:
                    pe.wait_ge(o_free, b["ov"] + h - 1)
                o = acc[:, h % 2, :]
                small_mm(o[:, 0:width], pT[:, 0:128], v(0))
                small_mm(o[:, P:P + width], pT[:, 128:256], v(0), True, False)
                small_mm(o[:, P:P + width], pT[:, 256:384], v(1), False, True).then_inc(o_full, 1)

            pe.nop().then_inc(pe_used, PARTS)
            pe.nop().then_inc(ada_sum, 2)
            pe.wait_ge(ld, 16 * N_LD)
            pe.matmul(tr[0:8, 0, :], t5[:], t5hot, start=True, stop=True).then_inc(t5_mm, 1)
            for unit in range(FIRST_UNITS):
                pe.wait_ge(slice_sum, SLICES * (unit + 1))
                for j in range(UC):
                    at = unit * UC + j
                    ins = pe.matmul(acc[:, 0, at:at + 1], ada_acc[:, unit % 2, j * P:(j + 1) * P], ones[:, 0:1],
                                    start=True, stop=True)
                ins.then_inc(ada_sum, 1)
            pe.wait_ge(t5_sb, 1)

            for step, b in plan:
                kind = step[0]
                if kind == "norm":
                    pe.wait_ge(src_ready, b["src"] + 1)
                    for r in range(4):
                        turn(b["u"] + r, [tok[:, t, (2 * r + k) * P:(2 * r + k + 1) * P] for k in range(2) for t in range(NT)],
                             scaled=b["tf"] + r - 1 if r >= 2 else None)
                elif kind == "ffn" and not step[3]:
                    ffn(b, step[2], step[1])
                elif kind == "ffn":
                    l = (step[1] - 3 * DEPTH) // 2
                    pe.wait_ge(count_ready, l + 1)
                    most = pe.value_load(fullest_i[0:1, 0:1], min_val=0, max_val=S)
                    with pe.If(most <= P):
                        moe(b, l)
                    with pe.Else():
                        moe_dense(b)
                        pe.wait_ge(tr_full, b["u"] + 2 + MOE_BLOCKS)
                        pe.nop().then_inc(tr_full, MOE_TURNS - MOE_BLOCKS - 2)
                elif kind == "proj":
                    for j in range(step[1]):
                        if j >= 2:
                            pe.wait_ge(ev_ready, b["ev"] + j - 1)
                        w = 512 if j < 6 else PROJ_W - 6 * 512
                        for half in range(2):
                            if j == 0:
                                pe.wait_ge(tr_free, b["u"] + 2 * half)
                            columns(b["n"] + 2 * j + half, lambda t: acc[:, 2 * (j % 2) + t, 0:w], 4 * half, 4,
                                    half == 0, half == 1, w)
                elif kind == "qkT":
                    pe.wait_ge(src_ready, b["src"])
                    pe.wait_ge(ev_ready, b["ev"])
                    _, how, q0, k0, _ = step
                    w = QK_C if how == "mla" else P
                    nq = 4 if how == "pairs" else 8
                    cols = [q0 + w * j for j in range(nq)] + [k0 + w * j for j in range(nq)]
                    for r in range(nq):
                        turn(b["u"] + r, [proj[:, t, c:c + w] for c in cols[2 * r:2 * r + 2] for t in range(NT)])
                elif kind in ("soft", "diff", "stick"):
                    which = step[1] if kind == "soft" else kind
                    heads = {"band": 16, "diff": 16}.get(which, NH)
                    nq = 4 if which in ("moba", "stick") else 8

                    def head(a):
                        if which == "mla":
                            return qk[0:QK_C, a, :], qk[0:QK_C, nq + a, :]
                        p = slice(HD * (a % 2), HD * (a % 2) + HD)
                        return qk[p, a // 2, :], qk[p, nq + a // 2, :]

                    def scores(a):
                        q, k = head(a)
                        s = gu[:, a % 2, :]
                        biased = which in ("band", "diff")
                        if a == 0:
                            pe.wait_ge(tr_free, b["u"] + 2)
                        if a >= 2:
                            pe.wait_ge(s_free, b["sc"] + a - 1)
                        if which == "band" or (which == "diff" and a % 2 == 0):
                            h = a if which == "band" else a // 2
                            before = (4 if which == "band" else 0) + h // 2 + 1
                            pe.wait_ge(bias_ld[h % 2], 32 * before)
                        for qt, (o, w) in enumerate(((0, 128), (128, 256))):
                            ins = small_mm(s[:, o:o + w], q[:, qt * P:(qt + 1) * P], k[:, 0:w], True, not biased)
                            if biased:
                                h = a if which == "band" else a // 2
                                ins = small_mm(s[:, o:o + w], flip, bias_in[:, h % 2, o:o + w], False, True)
                        ins.then_inc(s_full, 1)

                    def scores_T(a):
                        q, k = head(a)
                        s = gu[:, a % 2, :]
                        if a == 0:
                            pe.wait_ge(tr_free, b["u"] + 2)
                        if a >= 2:
                            pe.wait_ge(s_free, b["sc"] + a - 1)
                        small_mm(s[:, 0:256], k[:, 0:P], q[:, 0:S])
                        small_mm(s[:, 256:384], k[:, P:S], q[:, P:S]).then_inc(s_full, 1)

                    def values(c0, width):
                        return lambda h: (lambda kt: proj[:, kt, c0 + h * width:c0 + (h + 1) * width])

                    if which == "stick":
                        v = values(2560, HD)

                        def suffix(a):
                            sp = tok[:, a % 2, 0:384]
                            c = acc[:, 2 + a % 2, :]
                            pe.wait_ge(sp_ready, b["st"] + a + 1)
                            if a >= 2:
                                pe.wait_ge(arg_ready, b["st"] + a - 1)
                            small_mm(c[:, 256:384], tri, sp[:, 256:384])
                            small_mm(c[:, 0:256], tri, sp[:, 0:256], True, False)
                            small_mm(c[:, 128:256], ones, sp[:, 256:384], False, True).then_inc(c_full, 1)

                        def stick_out(a):
                            pe.wait_ge(p_ready, b["pr"] + a + 1)
                            value_mm(b, a, probT[:, a % 2, :], v(a), HD)

                        scores_T(0)
                        for a in range(NH):
                            if a + 1 < NH:
                                scores_T(a + 1)
                            suffix(a)
                            if a:
                                stick_out(a - 1)
                        stick_out(NH - 1)
                    else:
                        v = {"moba": values(1024, HD), "mla": lambda h: (lambda kt: proj[:, kt, mla_value_col(h):mla_value_col(h) + HD]), "band": values(2048, HD),
                             "diff": values(2048, 128)}[which]
                        width = 128 if which == "diff" else HD

                        def turn_head(h):
                            if which == "diff":
                                pe.wait_ge(a_ready, h + 1)
                                p = mixp
                                src = [p[:, j * P:(j + 1) * P] for j in range(3)]
                            else:
                                pe.wait_ge(p_ready, b["pr"] + h + 1)
                                src = [prob[:, h % 2, j * P:(j + 1) * P] for j in range(3)]
                            turn(b["u"] + h, src)

                        def out_head(h):
                            pe.wait_ge(tr_free, b["u"] + h + 1 + 2)
                            value_mm(b, h, probT[:, h % 2, :], v(h), width)

                        if which == "diff":
                            for h in range(10):
                                if h < 8:
                                    scores(2 * h)
                                    scores(2 * h + 1)
                                if 1 <= h <= 8:
                                    turn_head(h - 1)
                                if h >= 2:
                                    out_head(h - 2)
                        else:
                            for h in range(heads + 2):
                                if h < heads:
                                    scores(h)
                                if 1 <= h <= heads:
                                    turn_head(h - 1)
                                if h >= 2:
                                    out_head(h - 2)
                elif kind == "mla_T":
                    pe.wait_ge(src_ready, b["src"])
                    c0 = 6 * 512
                    turn(b["u"], [proj[:, t, c0 + k * P:c0 + (k + 1) * P] for k in range(2) for t in range(NT)])
                    turn(b["u"] + 1, [proj[:, t, c0 + QL:c0 + QL + P] for t in range(NT)])
                elif kind == "mla_up":
                    n = b["n"]
                    pe.wait_ge(tr_free, b["u"] + 2)
                    pe.wait_ge(o_free, b["ov"])
                    wide = acc[:].rearrange("p (t a) c -> p t a c", t=NT)
                    chunk_wait(n)
                    s = n % PARTS
                    for t in range(NT):
                        for h, w in ((0, 512), (1, 256)):
                            for k in range(2):
                                c = slice(k * 768 + h * 512, k * 768 + h * 512 + w)
                                ins = mm3(wide[:, t, h, 0:w], yT_hi[:, k, t * P:(t + 1) * P], yT_lo[:, k, t * P:(t + 1) * P],
                                          w_hi[:, s, c], w_lo[:, s, c], k == 0, k == 1)
                    ins.then_inc(pe_used, 1)
                    chunk_wait(n + 1)
                    s = (n + 1) % PARTS
                    pe.wait_ge(ev_ready, b["ev"] + 1)
                    for t in range(NT):
                        for h in range(2):
                            c = slice(h * 512, h * 512 + 512)
                            ins = mm3(wide[:, t, h, :], yT_hi[:, 2, t * P:(t + 1) * P], yT_lo[:, 2, t * P:(t + 1) * P],
                                      w_hi[:, s, c], w_lo[:, s, c], True, True)
                    ins.then_inc(pe_used, 1)
                elif kind == "merge":
                    pe.wait_ge(o_free, b["ov"])
                    for j in range(6):
                        n = b["n"] + 3 * j
                        if j % 2 == 0:
                            for r in range(2):
                                c0 = Y_COL[j // 2] + 2 * r * P
                                turn(b["u"] + j + r, [proj[:, t, c0 + k * P:c0 + (k + 1) * P] for k in range(2) for t in range(NT)])
                        if j:
                            pe.wait_ge(z_ready, b["mg"] + j)
                        columns(n, lambda t: gu[:, t, :], 0, 4, True, False)
                        columns(n + 1, lambda t: gu[:, t, :], 4, 4, False, True)
                        if j >= 2:
                            pe.wait_ge(mg_ready, b["mg"] + j - 1)
                        pe.wait_ge(tr_free, b["u"] + 2 * (j // 2 + 1) + 2)
                        columns(n + 2, lambda t: acc[:, 2 * (j % 2) + t, :], 0, 4, True, True, src=(yT_hi, yT_lo))
                elif kind == "backT":
                    src = tok if step[1] == "merged" else proj
                    pe.wait_ge(mg_ready, b["mg"]) if step[1] == "merged" else pe.wait_ge(o_free, b["ov"])
                    if step[1] == "subln":
                        pe.wait_ge(src_ready, b["src"])
                    for r in range(4):
                        turn(b["u"] + r, [src[:, t, (2 * r + k) * P:(2 * r + k + 1) * P] for k in range(2) for t in range(NT)],
                             scaled=b["tf"] + r - 1 if r >= 2 and step[1] == "subln" else None)
                elif kind == "out":
                    for c in range(4):
                        pe.wait_ge(tr_free, b["u"] + c - 1)
                        rows(b["n"] + c, lambda k, t: tuple(v[:, 2 * c + k, t * P:(t + 1) * P] for v in (hT_hi, hT_lo)),
                             c == 0, c == 3)
                        if c == 1:
                            gate_row(b, b["u"])
                elif kind == "route":
                    pe.wait_ge(rw_ready, 1)
                    pe.wait_ge(tr_free, b["u"] + 2)
                    for k in range(KT):
                        e = slice(k * EXP, (k + 1) * EXP)
                        ins = mm3(tr[0:EXP, b["u"] % 2, 0:S], rw_hi[:, e], rw_lo[:, e], hT_hi[:, k, :], hT_lo[:, k, :],
                                  k == 0, k == KT - 1)
                    ins.then_inc(tr_full, 1)
                    pe.wait_ge(th_ready, b["th"] + 1)
                    for t in range(NT):
                        ins = pe.transpose(tr[:, (b["u"] + 1) % 2, t * EXP:(t + 1) * EXP], tf[0:EXP, 0, t * P:(t + 1) * P],
                                           ident[0:EXP, 0:EXP])
                    ins.then_inc(tr_full, 1)
                    for j in range(8):
                        part, t, half = j // 4, j // 2 % 2, j % 2
                        if j >= 6:
                            pe.wait_ge(h_ready, 8 * step[1] + j - 5)
                        for c in range(4):
                            src = (hT_hi, hT_lo)[part][:, 4 * half + c, t * P:(t + 1) * P].bitcast(F32)
                            ins = pe.transpose(h_banks[j % 6][:, c * P:(c + 1) * P], src, ident)
                        ins.then_inc(h_full, 1)
                    pe.wait_ge(h_ready, 8 * step[1] + 8)
                    l = step[1]
                    pe.wait_ge(sent_ready, l + 1)
                    pe.wait_ge(tr_free, b["u"] + 3)
                    bank, sent, before = tr[:, (b["u"] + 2) % 2, :], rt[:, 3, :], cst("before")
                    s0, s1 = sent[:, 0:EXP], sent[:, EXP:2 * EXP]
                    for dst, terms in ((0, ((before, s0),)), (EXP, ((before, s1), (ones, s0))),
                                       (2 * EXP, ((ones, s0), (ones, s1)))):
                        for j, (lhs, rhs) in enumerate(terms):
                            ins = small_mm(bank[:, dst:dst + EXP], lhs, rhs, j == 0, j == len(terms) - 1)
                    ins.then_inc(tr_full, 1)


def constants():
    c = np.zeros((P, N_CONST), np.float32)

    def put(name, v):
        c[:, CONST[name][0]:CONST[name][1]] = np.asarray(v, np.float32).reshape(P, -1)

    r = np.arange(P)
    put("ident", np.eye(P))
    put("flip", np.eye(P)[::-1])
    put("ones", np.ones((P, P)))
    put("tri", (r[:, None] >= r[None, :]))
    put("before", (r[:, None] < r[None, :]))
    put("slots", np.tile(r, (P, 1)))
    keep = r[None, :] <= r[:, None]
    put("causal", np.where(np.concatenate([keep, np.ones((P, P), bool), keep], 1), 0.0, -BIG))
    keep = r[:, None] < r[None, :]
    put("strict", np.where(np.concatenate([keep, np.ones((P, P), bool), keep], 1), 0.0, -BIG))
    keep = (r[None, :] // BAND_CHUNK) <= (r[:, None] // BAND_CHUNK)
    put("chunked", np.where(np.concatenate([keep, np.ones((P, P), bool), keep], 1), 0.0, -BIG))
    for name, rot in (("p", ROT), ("m", ROPE)):
        inv = np.power(np.float32(THETA), -np.arange(0, rot, 2, dtype=np.float32) / np.float32(rot)).astype(np.float32)
        ang = np.arange(S, dtype=np.float32)[:, None] * inv[None, :]
        for f, fn in (("cos", np.cos), ("sin", np.sin)):
            put(f"{f}_{name}", fn(ang).astype(np.float32).reshape(NT, P, rot // 2).transpose(1, 0, 2))
    put("rank", np.tile(np.arange(EXP, 0, -1), (P, NT)))
    put("grank", np.tile(np.arange(GROUPS, 0, -1), (P, NT)))
    rel = np.arange(512) - 256
    n = np.abs(rel)
    large = 8 + (np.log(np.maximum(n, 1).astype(np.float32) / np.float32(8)) / math.log(1024 / 8) * 8).astype(np.int32)
    bucket = np.where(rel > 0, 16, 0) + np.where(n < 8, n, np.minimum(large, 15))
    return c, (np.arange(32)[:, None] == bucket[None, :]).astype(np.float32)


def weight_stream(a):
    n_chunks = make_plan()[-1][1]["n"]
    w = np.zeros((n_chunks, P, CW), np.float32)
    at = 0

    def tiles(m, kt, width):
        return m.reshape(kt, P, width).transpose(1, 0, 2)

    def add(block, pitch=None):
        nonlocal at
        kt, width = block.shape[1], block.shape[2]
        pitch = pitch or width
        w[at].reshape(P, CW)[:, :kt * pitch].reshape(P, kt, pitch)[:, :, :width] = block
        at += 1

    def ffn(blocks):
        held = None
        for g, u, d in blocks:
            for half in range(2):
                r = slice(512 * half, 512 * half + 512)
                add(np.concatenate([tiles(g[r], 4, BLK), tiles(u[r], 4, BLK)], 2))
            if held is not None:
                add(held)
            held = tiles(d, 2, D)
        add(held)

    def dense_ffn(l, s):
        ffn((a["ffn_w_gate"][l, s][:, c:c + BLK], a["ffn_w_up"][l, s][:, c:c + BLK], a["ffn_w_down"][l, s][c:c + BLK])
            for c in range(0, FF, BLK))

    def col_blocks(m, width=512):
        for half in range(2):
            add(tiles(m[512 * half:512 * half + 512], 4, width), 512)

    for l in range(DEPTH):
        dense_ffn(l, 0)
        w_in = a["mix_w_in"][l]
        for j in range(6):
            col_blocks(w_in[:, 512 * j:512 * j + 512])
        col_blocks(w_in[:, 3072:PROJ_W], PROJ_W - 3072)
        add(tiles(a["mla_w_uq"][l], 2, 768))
        add(tiles(a["mla_w_ukv"][l], 1, 1024))
        for n in range(3):
            for half in range(2):
                c = PROJ_W + n * D + half * 512
                col_blocks(w_in[:, c:c + 512])
                add(tiles(a["mix_w_branch"][l, n][:, half * 512:half * 512 + 512], 4, 512))
        for c in range(4):
            add(tiles(a["mix_w_out"][l][256 * c:256 * c + 256], 2, D))
        dense_ffn(l, 1)
    for l, which in enumerate("ab"):
        for j in range(6):
            col_blocks(a[f"{which}_w_qkv_2"][0][:, 512 * j:512 * j + 512])
        for c in range(4):
            add(tiles(a[f"{which}_w_o_2"][0][256 * c:256 * c + 256], 2, D))
        for e in range(EXP + 1):
            for j in range(2):
                if e < EXP:
                    for half in range(2):
                        r, c = slice(512 * half, 512 * half + 512), slice(BLK * j, BLK * j + BLK)
                        add(np.concatenate([tiles(a["moe_w_gate_2"][l, e][r, c], 4, BLK),
                                            tiles(a["moe_w_up_2"][l, e][r, c], 4, BLK)], 2))
                if e and j == 0:
                    for half in range(2):
                        add(tiles(a["moe_w_down_2"][l, e - 1][:, 512 * half:512 * half + 512], 4, 512))
    assert at == n_chunks, (at, n_chunks)
    return w


def modulation_stream(a):
    w = np.concatenate([a[name][l] for name in ("ada_w", "ada_w_2") for l in range(DEPTH)], 1)
    w = w.reshape(SLICES, 2, P, UNITS, UW).transpose(3, 0, 2, 1, 4)
    return w.reshape(UNITS * SLICES, P, 2 * UW)


def column_vectors(a):
    v = np.zeros((P, N_VEC), np.float32)

    def put(name, *parts):
        cols = np.concatenate([np.asarray(p).reshape(-1, P).T for p in parts], 1)
        v[:, VEC[name][0]:VEC[name][1]] = cols

    put("c", a["c"])
    put("c_2", a["c_2"])
    put("ada_b", a["ada_b"], a["ada_b_2"])
    second = [p for l in range(DEPTH) for p in (a["norm_mix_g_2"][l], a["norm_ffn_g_2"][l])]
    put("pre", a["norm_pre"], *second)
    put("post", a["norm_post"])
    put("q_norm", a["mla_q_norm"])
    put("kv_norm", a["mla_kv_norm"])
    for name, src in (("a_q", "a_q_gain_2"), ("a_k", "a_k_gain_2"), ("b_q", "b_q_gain_2"), ("b_k", "b_k_gain_2")):
        put(name, np.tile(a[src][0], 2))
    put("subln", a["a_subln_g_2"])
    return v


def kernel(**inputs):
    import concourse.bacc as _bacc
    from concourse.bass_utils import run_bass_kernel_spmd as _run

    a = {k: np.asarray(v) for k, v in inputs.items()}
    const, t5hot = constants()
    rw = a["router_w_2"].reshape(KT, P, EXP).transpose(1, 0, 2).reshape(P, KT * EXP)
    arrays = {
        "wstream": weight_stream(a), "ada_stream": modulation_stream(a), "x_in": a["x"][0], "const_in": const, "vec_in": column_vectors(a),
        "bgate_in": a["mix_b_gate"].reshape(DEPTH, 3 * D), "lam_in": a["a_lambda_2"].reshape(4 * HD),
        "rbias_in": a["router_bias_2"], "t5_in": a["t5_bias_2"], "t5hot_in": t5hot, "rel_in": a["b_rel_bias_2"][0],
        "rw_in": rw,
    }
    arrays = {k: np.ascontiguousarray(v) for k, v in arrays.items()}
    nc = _bacc.Bacc("TRN2", target_bir_lowering=False, num_devices=1)
    aps = [nc.dram_tensor(k, v.shape, mybir.dt.from_np(v.dtype), kind="ExternalInput").ap() for k, v in arrays.items()]
    out = nc.dram_tensor("x_out", (S, D), F32, kind="ExternalOutput").ap()
    build(nc, *aps, out)
    r = _run(nc, [arrays], core_ids=[0])
    return r.results[0]["x_out"].reshape(1, S, D)
```
